# Optimizing a Trainium2 kernel written in Bass

```python
import math
import jax, jax.numpy as jnp
from jax import lax
import numpy as np

D_MODEL = 1024
BATCH = 1
SEQ = 512
DEPTH = 2

MEM_LEN = 256
D_FF = 2816
CONV_CH = 256
CONV_W = 31
SC_CH = 256
SC_W = 3
N_HEADS = 8
HEAD_DIM = 64
ATT_W = N_HEADS * HEAD_DIM
IDX_HEADS = 4
IDX_DIM = 64
TOPK_MAX = 256
Q_BLOCK = 128
ROPE_THETA = 10000.0
XA_HEADS = 4
XA_DIM = D_MODEL // XA_HEADS
MIX_W = CONV_CH + SC_CH + ATT_W
SPLIT_SIZES = (CONV_CH, CONV_CH,
               SC_CH, SC_CH, SC_CH,
               ATT_W, ATT_W, ATT_W,
               IDX_HEADS * IDX_DIM, IDX_DIM, IDX_HEADS)
N_IN = sum(SPLIT_SIZES)
SPLIT_POINTS = tuple(int(v) for v in np.cumsum(SPLIT_SIZES)[:-1])
IDX_SCALE = (IDX_HEADS ** -0.5) * (IDX_DIM ** -0.5)


def rms_norm(x, g, eps=1e-6):
    xf = x.astype(jnp.float32)
    y = xf * lax.rsqrt(jnp.mean(xf * xf, axis=-1, keepdims=True) + eps)
    return (y * g.astype(jnp.float32)).astype(x.dtype)

def layer_norm(x, g, b, eps=1e-5):
    xf = x.astype(jnp.float32)
    mu = jnp.mean(xf, axis=-1, keepdims=True)
    var = jnp.mean(jnp.square(xf - mu), axis=-1, keepdims=True)
    y = (xf - mu) * lax.rsqrt(var + eps)
    return (y * g.astype(jnp.float32) + b.astype(jnp.float32)).astype(x.dtype)

def swiglu(h, w_gate, w_up, w_down):
    return (jax.nn.silu(h @ w_gate) * (h @ w_up)) @ w_down

def causal_dwconv(x, w):
    width, ch = w.shape
    return lax.conv_general_dilated(
        x, w[:, None, :].astype(x.dtype), window_strides=(1,), padding=[(width - 1, 0)],
        dimension_numbers=('NWC', 'WIO', 'NWC'), feature_group_count=ch)

def rope_tables(positions, dim):
    inv_freq = ROPE_THETA ** (-jnp.arange(0, dim, 2, dtype=jnp.float32) / dim)
    ang = positions.astype(jnp.float32)[..., None] * inv_freq
    return jnp.cos(ang), jnp.sin(ang)

def apply_rope(t, cos, sin):
    tf = t.astype(jnp.float32)
    half = tf.shape[-1] // 2
    t1, t2 = tf[..., :half], tf[..., half:]
    c, s = cos[:, :, None, :], sin[:, :, None, :]
    return jnp.concatenate([t1 * c - t2 * s, t2 * c + t1 * s], axis=-1).astype(t.dtype)

def conformer_conv(a_val, a_gate, dw, dw_b, ln_g, ln_b):
    h = a_val * jax.nn.sigmoid(a_gate)
    h = causal_dwconv(h, dw) + dw_b
    return jax.nn.silu(layer_norm(h, ln_g, ln_b))

def short_gated_conv(b_gate, c_gate, h, w):
    return b_gate * causal_dwconv(c_gate * h, w)

def dsa_attention(q, k, v, q_idx, k_idx, w_idx):
    bsz, seq, nh, dh = q.shape
    topk = min(TOPK_MAX, seq // 4)
    nb = seq // Q_BLOCK
    key_pos = jnp.arange(seq)
    b_ar = jnp.arange(bsz)[:, None, None]

    def to_blocks(t):
        return jnp.moveaxis(t.reshape(bsz, nb, Q_BLOCK, *t.shape[2:]), 1, 0)

    q_pos = jnp.arange(seq).reshape(nb, Q_BLOCK)

    def one_block(args):
        qb, qib, wb, tb = args
        logits = jnp.einsum('bqhd,bsd->bqhs', qib, k_idx).astype(jnp.float32)
        score = jnp.einsum('bqh,bqhs->bqs', wb.astype(jnp.float32), jax.nn.relu(logits)) * IDX_SCALE
        causal = key_pos[None, :] <= tb[:, None]
        score = jnp.where(causal[None], score, -jnp.inf)
        top_val, top_idx = lax.top_k(score, topk)
        k_sel = k[b_ar, top_idx]
        v_sel = v[b_ar, top_idx]
        s = jnp.einsum('bqhd,bqkhd->bqhk', qb, k_sel).astype(jnp.float32) * (dh ** -0.5)
        s = jnp.where(jnp.isfinite(top_val)[:, :, None, :], s, -jnp.inf)
        p = jax.nn.softmax(s, axis=-1).astype(v.dtype)
        return jnp.einsum('bqhk,bqkhd->bqhd', p, v_sel)

    out = lax.map(one_block, (to_blocks(q), to_blocks(q_idx), to_blocks(w_idx), q_pos))
    return jnp.moveaxis(out, 0, 1).reshape(bsz, seq, nh * dh)

def memory_cross_attention(h, mem_n, wq, wkv, wo):
    bsz, seq, _ = h.shape
    m = mem_n.shape[1]
    q = (h @ wq).reshape(bsz, seq, XA_HEADS, XA_DIM)
    k, v = jnp.split(mem_n @ wkv, 2, axis=-1)
    k = k.reshape(bsz, m, XA_HEADS, XA_DIM)
    v = v.reshape(bsz, m, XA_HEADS, XA_DIM)
    s = jnp.einsum('bshd,bmhd->bhsm', q, k).astype(jnp.float32) * (XA_DIM ** -0.5)
    p = jax.nn.softmax(s, axis=-1).astype(v.dtype)
    o = jnp.einsum('bhsm,bmhd->bshd', p, v).reshape(bsz, seq, D_MODEL)
    return o @ wo

def first_inputs(seed: int = 0) -> dict:
    key = jax.random.key(seed)
    ks = iter(jax.random.split(key, 32))
    L, D, F = DEPTH, D_MODEL, D_FF

    def w(shape, fan_in):
        return jax.random.normal(next(ks), shape, jnp.float32) * (fan_in ** -0.5)

    def gain(shape):
        return 1.0 + 0.01 * jax.random.normal(next(ks), shape, jnp.float32)

    def bias(shape):
        return 0.01 * jax.random.normal(next(ks), shape, jnp.float32)

    x = jax.random.normal(next(ks), (BATCH, SEQ, D), jnp.float32)
    mem = jax.random.normal(next(ks), (BATCH, MEM_LEN, D), jnp.float32)
    start = jax.random.randint(next(ks), (BATCH, 1), 0, 1024, dtype=jnp.int32)
    positions = (start + jnp.arange(SEQ, dtype=jnp.int32)[None, :]).astype(jnp.int32)
    return {
        "x": x, "mem": mem, "positions": positions,
        "ffn1_norm": gain((L, D)), "ffn1_w_gate": w((L, D, F), D), "ffn1_w_up": w((L, D, F), D),
        "ffn1_w_down": w((L, F, D), F),
        "mix_norm": gain((L, D)), "w_in": w((L, D, N_IN), D),
        "conf_dw": w((L, CONV_W, CONV_CH), CONV_W), "conf_dw_b": bias((L, CONV_CH)),
        "conf_ln_g": gain((L, CONV_CH)), "conf_ln_b": bias((L, CONV_CH)),
        "sc_dw": w((L, SC_W, SC_CH), SC_W),
        "w_out": w((L, MIX_W, D), MIX_W),
        "xa_norm": gain((L, D)), "mem_norm": gain((L, D)),
        "xa_wq": w((L, D, D), D), "xa_wkv": w((L, D, 2 * D), D), "xa_wo": w((L, D, D), D),
        "ffn2_norm": gain((L, D)), "ffn2_w_gate": w((L, D, F), D), "ffn2_w_up": w((L, D, F), D),
        "ffn2_w_down": w((L, F, D), F),
        "final_norm": gain((D,)),
    }

def first_block(x, mem, positions, ffn1_norm, ffn1_w_gate, ffn1_w_up, ffn1_w_down, mix_norm, w_in,
              conf_dw, conf_dw_b, conf_ln_g, conf_ln_b, sc_dw, w_out, xa_norm, mem_norm,
              xa_wq, xa_wkv, xa_wo, ffn2_norm, ffn2_w_gate, ffn2_w_up, ffn2_w_down, final_norm):
    bsz, seq, _ = x.shape
    cos, sin = rope_tables(positions, HEAD_DIM)
    for l in range(DEPTH):
        x = x + 0.5 * swiglu(rms_norm(x, ffn1_norm[l]), ffn1_w_gate[l], ffn1_w_up[l], ffn1_w_down[l])
        h = rms_norm(x, mix_norm[l])
        (a_val, a_gate, b_gate, c_gate, b_h, q, k, v,
         q_idx, k_idx, w_idx) = jnp.split(h @ w_in[l], SPLIT_POINTS, axis=-1)
        y_a = conformer_conv(a_val, a_gate, conf_dw[l], conf_dw_b[l], conf_ln_g[l], conf_ln_b[l])
        y_b = short_gated_conv(b_gate, c_gate, b_h, sc_dw[l])
        q = apply_rope(q.reshape(bsz, seq, N_HEADS, HEAD_DIM), cos, sin)
        k = apply_rope(k.reshape(bsz, seq, N_HEADS, HEAD_DIM), cos, sin)
        v = v.reshape(bsz, seq, N_HEADS, HEAD_DIM)
        q_idx = apply_rope(q_idx.reshape(bsz, seq, IDX_HEADS, IDX_DIM), cos, sin)
        k_idx = apply_rope(k_idx[:, :, None, :], cos, sin)[:, :, 0, :]
        y_c = dsa_attention(q, k, v, q_idx, k_idx, w_idx)
        x = x + jnp.concatenate([y_a, y_b, y_c], axis=-1) @ w_out[l]
        x = x + memory_cross_attention(rms_norm(x, xa_norm[l]), rms_norm(mem, mem_norm[l]),
                                       xa_wq[l], xa_wkv[l], xa_wo[l])
        x = x + 0.5 * swiglu(rms_norm(x, ffn2_norm[l]), ffn2_w_gate[l], ffn2_w_up[l], ffn2_w_down[l])
    return rms_norm(x, final_norm)


RET_HEADS = 4
RET_QK_DIM = 64
RET_V_DIM = 128
RET_CHUNK = 128
DIFF_HEADS = 4
DIFF_HEAD_DIM = 64
DIFF_V_DIM = 2 * DIFF_HEAD_DIM
FFN_HIDDEN = ((int(math.ceil(8 * D_MODEL / 3)) + 255) // 256) * 256
NORM_EPS = 1e-6

RET_Q_W = RET_HEADS * RET_QK_DIM
RET_V_W = RET_HEADS * RET_V_DIM
DIFF_QK_W = DIFF_HEADS * 2 * DIFF_HEAD_DIM
DIFF_V_W = DIFF_HEADS * DIFF_V_DIM
IN_SPLITS = [RET_Q_W, RET_Q_W, RET_V_W, RET_V_W, DIFF_QK_W, DIFF_QK_W, DIFF_V_W]
IN_WIDTH = sum(IN_SPLITS)
MIX_WIDTH = RET_V_W + DIFF_V_W


def rmsnorm(x, g):
    xf = x.astype(jnp.float32)
    y = xf * lax.rsqrt(jnp.mean(xf * xf, axis=-1, keepdims=True) + NORM_EPS)
    return (y * g.astype(jnp.float32)).astype(x.dtype)

def retention_gammas():
    return 1.0 - jnp.exp2(-5.0 - jnp.arange(RET_HEADS, dtype=jnp.float32))

def retention_chunkwise(q, k, v):
    B, S, H, dk = q.shape
    dv = v.shape[-1]
    C = RET_CHUNK
    N = S // C
    dt = q.dtype
    log_g = jnp.log(retention_gammas())
    k = k * jnp.asarray(dk ** -0.5, dt)
    q = q.reshape(B, N, C, H, dk)
    k = k.reshape(B, N, C, H, dk)
    v = v.reshape(B, N, C, H, dv)
    idx = jnp.arange(C, dtype=jnp.float32)
    rel = idx[:, None] - idx[None, :]
    decay = jnp.where(rel[None] >= 0,
                      jnp.exp(jnp.maximum(rel, 0.0)[None] * log_g[:, None, None]),
                      0.0).astype(dt)
    s = jnp.einsum('bnchd,bnshd->bnhcs', q, k) * decay
    inner = jnp.einsum('bnhcs,bnshe->bnche', s, v)
    k_decay = jnp.exp((C - 1 - idx)[:, None] * log_g[None, :]).astype(dt)
    kv = jnp.einsum('bnshd,bnshe->nbhde', k * k_decay[:, :, None], v)
    g_chunk = jnp.exp(C * log_g).astype(dt)[None, :, None, None]

    def step(state, kv_n):
        return g_chunk * state + kv_n, state

    _, states = lax.scan(step, jnp.zeros((B, H, dk, dv), dt), kv)
    q_decay = jnp.exp((idx + 1.0)[:, None] * log_g[None, :]).astype(dt)
    cross = jnp.einsum('bnchd,nbhde->bnche', q * q_decay[:, :, None], states)
    return (inner + cross).reshape(B, S, H, dv)

def alibi_slopes(n):
    return jnp.exp2(-8.0 * jnp.arange(1, n + 1, dtype=jnp.float32) / n)

def diff_attention(q, k, v, lam):
    S = q.shape[1]
    d = q.shape[-1]
    scale = d ** -0.5
    slopes = alibi_slopes(q.shape[2])
    outs = []
    for i in range(S // Q_BLOCK):
        q0 = i * Q_BLOCK
        kend = q0 + Q_BLOCK
        qb = q[:, q0:kend]
        kb = k[:, :kend]
        vb = v[:, :kend]
        s = jnp.einsum('bqhjd,bkhjd->bhjqk', qb, kb).astype(jnp.float32) * scale
        dist = (q0 + jnp.arange(Q_BLOCK, dtype=jnp.float32))[:, None] - jnp.arange(kend, dtype=jnp.float32)[None, :]
        s = s - slopes[None, :, None, None, None] * dist
        s = jnp.where(dist >= 0, s, -jnp.inf)
        p = jax.nn.softmax(s, axis=-1)
        a = p[:, :, 0] - lam * p[:, :, 1]
        outs.append(jnp.einsum('bhqk,bkhe->bqhe', a.astype(vb.dtype), vb))
    return jnp.concatenate(outs, axis=1)

def second_inputs(seed: int = 0) -> dict:
    key = jax.random.key(seed)
    ks = jax.random.split(key, 16)
    f = jnp.float32

    def nrm(k, shape, scale):
        return jax.random.normal(k, shape, f) * scale

    def gain(k, shape):
        return 1.0 + 0.02 * jax.random.normal(k, shape, f)

    return {
        "x": jax.random.normal(ks[0], (BATCH, SEQ, D_MODEL), f),
        "attn_norm": gain(ks[1], (DEPTH, D_MODEL)),
        "w_in": nrm(ks[2], (DEPTH, D_MODEL, IN_WIDTH), D_MODEL ** -0.5),
        "ret_norm": gain(ks[3], (DEPTH, RET_V_DIM)),
        "lambda_q1": nrm(ks[4], (DEPTH, DIFF_HEAD_DIM), 0.1),
        "lambda_k1": nrm(ks[5], (DEPTH, DIFF_HEAD_DIM), 0.1),
        "lambda_q2": nrm(ks[6], (DEPTH, DIFF_HEAD_DIM), 0.1),
        "lambda_k2": nrm(ks[7], (DEPTH, DIFF_HEAD_DIM), 0.1),
        "diff_norm": gain(ks[8], (DEPTH, DIFF_V_DIM)),
        "w_out": nrm(ks[9], (DEPTH, MIX_WIDTH, D_MODEL), MIX_WIDTH ** -0.5),
        "ffn_norm": gain(ks[10], (DEPTH, D_MODEL)),
        "w_gate": nrm(ks[11], (DEPTH, D_MODEL, FFN_HIDDEN), D_MODEL ** -0.5),
        "w_up": nrm(ks[12], (DEPTH, D_MODEL, FFN_HIDDEN), D_MODEL ** -0.5),
        "w_down": nrm(ks[13], (DEPTH, FFN_HIDDEN, D_MODEL), FFN_HIDDEN ** -0.5),
        "final_norm": gain(ks[14], (D_MODEL,)),
    }

def second_block(x, attn_norm, w_in, ret_norm, lambda_q1, lambda_k1, lambda_q2, lambda_k2,
              diff_norm, w_out, ffn_norm, w_gate, w_up, w_down, final_norm):
    B, S, _ = x.shape
    offsets = np.cumsum(IN_SPLITS)[:-1].tolist()
    h = x
    for l in range(DEPTH):
        u = rmsnorm(h, attn_norm[l])
        proj = u @ w_in[l]
        rq, rk, rv, rg, dq, dk, dv = jnp.split(proj, offsets, axis=-1)

        ret = retention_chunkwise(rq.reshape(B, S, RET_HEADS, RET_QK_DIM),
                                  rk.reshape(B, S, RET_HEADS, RET_QK_DIM),
                                  rv.reshape(B, S, RET_HEADS, RET_V_DIM))
        ret = rmsnorm(ret, ret_norm[l]).reshape(B, S, RET_V_W)
        ret = jax.nn.silu(rg) * ret

        lam_init = 0.8 - 0.6 * math.exp(-0.3 * l)
        lam = (jnp.exp(jnp.sum(lambda_q1[l].astype(jnp.float32) * lambda_k1[l].astype(jnp.float32)))
               - jnp.exp(jnp.sum(lambda_q2[l].astype(jnp.float32) * lambda_k2[l].astype(jnp.float32)))
               + lam_init)
        dif = diff_attention(dq.reshape(B, S, DIFF_HEADS, 2, DIFF_HEAD_DIM),
                             dk.reshape(B, S, DIFF_HEADS, 2, DIFF_HEAD_DIM),
                             dv.reshape(B, S, DIFF_HEADS, DIFF_V_DIM), lam)
        dif = (rmsnorm(dif, diff_norm[l]) * (1.0 - lam_init)).reshape(B, S, DIFF_V_W)

        mix = jnp.concatenate([ret, dif], axis=-1)
        h = h + mix @ w_out[l]

        u = rmsnorm(h, ffn_norm[l])
        h = h + (jax.nn.silu(u @ w_gate[l]) * (u @ w_up[l])) @ w_down[l]
    return rmsnorm(h, final_norm)


def setup_inputs(seed=0):
    out = dict(first_inputs(seed))
    for name, value in second_inputs(seed + 1).items():
        if name != "x":
            out[name + "_2"] = value
    return out


def reference(
    x, mem, positions, ffn1_norm, ffn1_w_gate, ffn1_w_up, ffn1_w_down, mix_norm, w_in, conf_dw,
    conf_dw_b, conf_ln_g, conf_ln_b, sc_dw, w_out, xa_norm, mem_norm, xa_wq, xa_wkv, xa_wo,
    ffn2_norm, ffn2_w_gate, ffn2_w_up, ffn2_w_down, final_norm, attn_norm_2, w_in_2, ret_norm_2,
    lambda_q1_2, lambda_k1_2, lambda_q2_2, lambda_k2_2, diff_norm_2, w_out_2, ffn_norm_2,
    w_gate_2, w_up_2, w_down_2, final_norm_2,
):
    x = first_block(
        x, mem, positions, ffn1_norm, ffn1_w_gate, ffn1_w_up, ffn1_w_down, mix_norm, w_in,
        conf_dw, conf_dw_b, conf_ln_g, conf_ln_b, sc_dw, w_out, xa_norm, mem_norm, xa_wq,
        xa_wkv, xa_wo, ffn2_norm, ffn2_w_gate, ffn2_w_up, ffn2_w_down, final_norm,
    )
    return second_block(
        x, attn_norm_2, w_in_2, ret_norm_2, lambda_q1_2, lambda_k1_2, lambda_q2_2, lambda_k2_2,
        diff_norm_2, w_out_2, ffn_norm_2, w_gate_2, w_up_2, w_down_2, final_norm_2,
    )


_drawn_inputs = setup_inputs


def setup_inputs(seed=0):
    import zlib

    import numpy as np

    out = dict(_drawn_inputs(seed))
    spreads = {}
    factors = {'ffn1_norm': 3.291,
     'conf_ln_g': 4.903,
     'conf_ln_b': 4.841,
     'xa_norm': 8.0,
     'mem_norm': 8.0,
     'ffn2_norm': 5.337,
     'final_norm': 3.314,
     'ret_norm_2': 17.005,
     'diff_norm_2': 12.894,
     'ffn_norm_2': 2.979,
     'final_norm_2': 8.119}
    for name, (base, spread) in spreads.items():
        noise = np.random.default_rng([zlib.crc32(name.encode()), seed]).standard_normal(out[name].shape)
        drawn = base * np.exp(spread * noise) if base else spread * noise
        out[name] = __import__('jax').numpy.asarray(drawn.astype(out[name].dtype))
    for name, factor in factors.items():
        out[name] = (out[name] * factor).astype(out[name].dtype)
    return out
```

```python
import math
from contextlib import ExitStack, contextmanager

import numpy as np

import concourse.bass as bass
from concourse import mybir

F32 = mybir.dt.float32
F32R = mybir.dt.float32r
I32 = mybir.dt.int32
ACT = mybir.ActivationFunctionType
ALU = mybir.AluOpType
AX_X = mybir.AxisListType.X

P = 128
S = 512
D = 1024
F = 2816
KT = D // P
NQ = S // P
MEM = 256
RING = 4
CH = KT * P
BIG = 1e30
TAKEN = -3e38
EPS = 1e-6
LN_EPS = 1e-5
TAPS, SC_TAPS = 31, 3
TOPK = 128
ROUNDS = TOPK // 8
PAD, SC_PAD = TAPS - 1, SC_TAPS - 1
LOG_GAMMA = [math.log(1.0 - 2.0 ** (-5 - h)) for h in range(4)]
SLOPE = [2.0 ** (-8.0 * (h + 1) / 4) for h in range(4)]
LAM_INIT = [0.8 - 0.6 * math.exp(-0.3 * m) for m in range(2)]
TWO_PI = (6.28125, 0.0019350051879882812, 2 * math.pi - 6.28125 - 0.0019350051879882812)
ROUND = 1.5 * 2 ** 23

C_ID, C_ROT, C_DIST, C_NEG, C_DEC, C_BIG, C_INV, C_ONE = 0, 128, 256, 768, 1280, 1792, 1920, 1921
C_N = C_ONE + P

G_FFN1, G_FINAL, G_MIX, G_XA, G_MEM, G_FFN2, G_ATTN2, G_FINAL2, G_FFNN2 = 0, 16, 24, 40, 56, 72, 88, 104, 112
G_DW, G_DWB = 128, 252
G_LNG, G_LNB, G_SC, G_RET, G_DIF = 256, 260, 264, 276, 278
G_N = 3 * P

IN1 = ([(3072, 64), (3136, 4)] + [(2816 + 64 * h, 64) for h in range(4)]
       + [(128 * c, 128) for c in range(10)]
       + [(1280 + 128 * c, 128) for c in range(12)])
C_AV, C_AG, C_BG, C_CG, C_BH, C_Q, C_K, C_V = 6, 8, 10, 12, 14, 16, 20, 24
R_Q, R_K, R_V, R_G, D_Q, D_K, D_V = 0, 2, 4, 8, 12, 16, 20

F_GROUPS = [(0, 8), (8, 8), (16, 6)]
F_TILES = F // P
N_FFN = 2 * F_TILES + KT * len(F_GROUPS)
O_MIX = N_FFN
O_OUT = O_MIX + len(IN1)
O_WQ = O_OUT + 8
O_KV = O_WQ + 8
O_WO = O_KV + 16
O_FFN2 = O_WO + 8
N_L1 = O_FFN2 + N_FFN
O2_OUT = 24
O2_FFN = O2_OUT + 8
N_L2 = O2_FFN + N_FFN
N_ALL = 2 * N_L1 + 2 * N_L2
for _n in (N_FFN, O_MIX, O_OUT, O_WQ, O_KV, O_WO, O_FFN2, N_L1, O2_OUT, O2_FFN, N_L2):
    assert _n % RING == 0

ROPES, SCORES1, PV1 = 13, 48, 12
WTILES = [0, 128, 384, 768]


def constants():
    c = np.zeros((P, C_N), np.float32)
    p = np.arange(P)[:, None]
    m = np.arange(S)[None, :]
    c[:, C_ID:C_ID + P] = np.eye(P)
    for j in range(P):
        c[j + 32 if j % 64 < 32 else j - 32, C_ROT + j] = -1.0 if j % 64 < 32 else 1.0
    dist = 384 + p - m
    c[:, C_DIST:C_DIST + S] = dist
    c[:, C_NEG:C_NEG + S] = np.where(dist >= 0, 0.0, -BIG)
    c[:, C_DEC:C_DEC + S] = np.where(m - p >= 0, m - p, 1e9)
    c[:, C_BIG:C_BIG + P] = np.where(np.arange(P)[None, :] <= p, 0.0, BIG)
    inv = (10000.0 ** (-np.arange(0, 64, 2) / 64)).astype(np.float32)
    c[:, C_INV] = inv[np.arange(P) % 32]
    c[:, C_ONE:C_ONE + P] = 1.0
    return c


class Chain:

    def __init__(self, sem):
        self.sem, self.base, self.k = sem, 0, 0

    def done(self, eng, ins):
        ins.then_inc(self.sem, 1)
        self.k += 1
        eng.wait_ge(self.sem, self.base + self.k)

    @contextmanager
    def loop(self, eng, start, end, per):
        base, k = self.base, self.k
        with eng.Fori(start, end) as i:
            self.base = base + (i - start) * per
            yield i
            assert self.k == k + per, f"per should be {self.k - k}"
        self.base, self.k = base, k + per * (end - start)


def two_blocks(nc, A, out):
    ctx = ExitStack()
    with ctx:
        def sb(name, shape, dt=F32):
            return ctx.enter_context(nc.sbuf_tensor(name, shape, dt))

        def sem(name):
            return ctx.enter_context(nc.semaphore(name))

        x = sb("x", [P, KT * S])
        u_hi, u_lo = sb("u_hi", [P, KT * S], F32R), sb("u_lo", [P, KT * S], F32R)
        h_hi, h_lo = sb("h_hi", [P, KT * S], F32R), sb("h_lo", [P, KT * S], F32R)
        raw = sb("raw", [P, RING, CH])
        w_hi, w_lo = sb("w_hi", [P, RING, CH], F32R), sb("w_lo", [P, RING, CH], F32R)
        const = sb("const", [P, C_N])
        par = sb("par", [P, G_N])
        cos_t, sin_t = sb("cos_t", [P, S]), sb("sin_t", [P, S])
        rstd = sb("rstd", [P, S])
        small = sb("small", [P, 128])
        mem = sb("mem", [P, 16140])
        bank = [ctx.enter_context(nc.psum_tensor(f"bank{i}", [P, S], F32)) for i in range(8)]

        def view(at, n):
            return mem[:, at:at + n]

        def tile(t, k, n=1):
            if isinstance(k, int):
                return t[:, k * S:(k + n) * S]
            return t[:, bass.ds(k * S, n * S)]

        def col(k):
            return par[:, k:k + 1] if isinstance(k, int) else par[:, bass.ds(k, 1)]

        def f32(ap):
            return ap.bitcast(F32)

        ident, rot = const[:, C_ID:C_ID + P], const[:, C_ROT:C_ROT + P]
        ones = const[:, C_ONE:C_ONE + P]
        one = const[:, C_ONE:C_ONE + 1]

        y_buf = [view(13572, S), view(14084, S)]
        square, diag = y_buf
        rope_t = view(14596, S)
        sumsq = rope_t
        conv = [view(15108, S), view(15620, S)]
        gate_t, tanh_t, up_t = view(0, S), view(S, S), view(2 * S, S)
        q_t, k_t, v_t = view(0, 2048), view(2048, 2048), view(4096, 2048)
        work = [view(6144 + WTILES[t], P * (t + 1)) for t in range(NQ)]
        pt = [view(7424 + 2048 * i, 2048) for i in range(2)]
        q_idx = [view(7424 + S * h, S) for h in range(4)]
        a_pad = [view(9472 + (PAD + S) * i, PAD + S) for i in range(2)]
        k_idx = view(10556, S)
        yb_t = k_idx
        w_idx_t = conv[0]
        tap_t = q_idx[0]
        sp = [view(11520 + S * i, S) for i in range(2)]
        prob = [view(12544 + S * i, S) for i in range(2)]
        relu_t = sp
        c_pad = [view(11520 + (SC_PAD + S) * i, SC_PAD + S) for i in range(2)]
        b_gate = [view(12548 + S * i, S) for i in range(2)]
        qx = view(0, 4096)
        km, vm = view(4096, 2048), view(6144, 2048)
        mem_in = view(8192, 2048)
        ptx = [view(10240 + 1024 * i, 1024) for i in range(2)]
        px = [view(12288 + MEM * i, MEM) for i in range(2)]
        vx_t = [view(12800 + MEM * i, MEM) for i in range(2)]
        rq_t, rk_t, rv_t = view(0, 1024), view(1024, 1024), view(2048, 2048)
        dq_t, dk_t, dv_t = view(0, 2048), view(2048, 2048), view(9216, 2048)
        z_t = view(4096, 2048)
        table = [view(6144 + S * i, S) for i in range(2)]
        sd = view(7168, 2048)
        d_pt = sd
        gate_s = view(9216, 2048)
        dsp = [[view(11264 + S * (2 * b + i), S) for i in range(2)] for b in range(2)]
        dp = [y_buf, [rope_t, table[1]]]
        zsq = conv
        x_in = view(0, 4096)
        par_in = view(8192, G_N)
        pos_i = view(9216, S).bitcast(I32)
        lam_in = view(10240, 2 * 4 * 64)
        y_out = view(0, 4096)

        neg_max = [small[:, i:i + 1] for i in range(8)]
        row_sum = [small[:, 8 + i:9 + i] for i in range(8)]
        row_inv = [small[:, 16 + i:17 + i] for i in range(8)]
        var, inv = small[:, 24:28], small[:, 28:32]
        ln_var, ln_inv = small[:, 32:36], small[:, 36:40]
        w_idx = small[:, 40:56]
        max8 = small[:, 56:64]
        h_var, h_inv = small[:, 64:80], small[:, 80:96]
        minus_half = small[:, 96:112]
        neg_lam = small[:, 112:114]
        lam_s = small[:, 114:118]
        half_pi = small[:, 118:119]
        mem_var, mem_inv = small[:, 120:122], small[:, 122:124]

        S_BANK, T_BANK = (4, 5), (6, 7)

        raw_in = [sem(f"raw_in{i}") for i in range(RING)]
        setup_in, x_landed, mem_landed, stored = sem("setup_in"), sem("x_landed"), sem("mem_landed"), sem("stored")
        rounded = sem("rounded")
        split = sem("split")
        tiles = sem("tiles")
        taken = sem("taken")
        u_rounded, u_ready = sem("u_rounded"), sem("u_ready")
        sq_sum = sem("sq_sum")
        stat_mm, stat_var, stat_inv, stat_diag, stat_bc, rstd_set = (
            sem(n) for n in ("stat_mm", "stat_var", "stat_inv", "stat_diag", "stat_bc", "rstd_set"))
        x_set, x_tr = sem("x_set"), sem("x_tr")
        par_tr, par_set, tab_set, pool_set = sem("par_tr"), sem("par_set"), sem("tab_set"), sem("pool_set")
        tab_sin = sem("tab_sin")
        f_tanh, f_prod, f_rounded, f_ready = sem("f_tanh"), sem("f_prod"), sem("f_rounded"), sem("f_ready")
        rot_mm, cos_mul, roped = sem("rot_mm"), sem("cos_mul"), sem("roped")
        wi_tr, wi_set = sem("wi_tr"), sem("wi_set")
        idx_mm, idx_relu, idx_add = sem("idx_mm"), sem("idx_relu"), sem("idx_add")
        pads, a_tanh, a_glu = sem("pads"), sem("a_tanh"), sem("a_glu")
        conv0, conv1 = sem("conv0"), sem("conv1")
        y_made, y_rounded, y_ready = sem("y_made"), sem("y_rounded"), sem("y_ready")
        v_tr, v_set = sem("v_tr"), sem("v_set")
        ln_mean, ln_cent, ln_sq, ln_mm, ln_v, ln_i, ln_d, ln_bc, ln_y, ln_z, ln_t = (
            sem(n) for n in ("ln_mean", "ln_cent", "ln_sq", "ln_mm", "ln_v", "ln_i", "ln_d", "ln_bc", "ln_y", "ln_z", "ln_t"))
        masked = sem("masked")
        s_mm, s_min, p_exp, p_norm, t_mm, t_set, pv_mm = (
            sem(n) for n in ("s_mm", "s_min", "p_exp", "p_norm", "t_mm", "t_set", "pv_mm"))
        o_rounded, o_ready = sem("o_rounded"), sem("o_ready")
        mem_sq, mem_v, mem_i, mem_n, mem_tr, gm_rounded, gm_ready = (
            sem(n) for n in ("mem_sq", "mem_v", "mem_i", "mem_n", "mem_tr", "gm_rounded", "gm_ready"))
        r_mm, r_dec, dec_set, rpv_mm, z_sq, z_mm = (sem(n) for n in ("r_mm", "r_dec", "dec_set", "rpv_mm", "z_sq", "z_mm"))
        h_v, h_i, h_d, h_bc, z_norm, g_tanh, al_set = (
            sem(n) for n in ("h_v", "h_i", "h_d", "h_bc", "z_norm", "g_tanh", "al_set"))
        chain_v, chain_a, chain_p = sem("chain_v"), sem("chain_a"), sem("chain_p")

        W = {n: A[n].rearrange("l (k p) n -> l p k n", p=P) for n in (
            "ffn1_w_gate", "ffn1_w_up", "ffn1_w_down", "w_in", "w_out", "xa_wq", "xa_wkv", "xa_wo",
            "ffn2_w_gate", "ffn2_w_up", "ffn2_w_down", "w_in_2", "w_out_2", "w_gate_2", "w_up_2", "w_down_2")}

        block = ctx.enter_context(nc.Block())

        @block.sync
        def _(sp_e):
            def load(b4, j, w, l, k0, kn, c, width=P):
                sp_e.wait_ge(split, 4 * b4 + j + 1)
                dst = raw[:, j % RING, 0:kn * P].rearrange("p (k n) -> p k n", n=P)[:, :, 0:width]
                cols = slice(c, c + width) if isinstance(c, int) else bass.ds(c, width)
                sp_e.dma_start(dst, w[l, :, k0:k0 + kn, cols]).then_inc(raw_in[j % RING], 16)

            def load_ffn(b4, l, gate, up, down):
                for f0, fn in F_GROUPS:
                    with sp_e.Fori(0, fn // 2) as i:
                        for j in range(4):
                            load(b4 + i, j, W[up if j % 2 else gate], l, 0, KT, (i * 2 + (f0 + j // 2)) * P)
                    b4 = b4 + fn // 2
                    with sp_e.Fori(0, 2) as i:
                        for j in range(4):
                            load(b4 + i, j, W[down], l, f0, fn, (i * 4 + j) * P)
                    b4 = b4 + 2

            def load_plain(b4, l, name, chunks):
                with sp_e.Fori(0, chunks // 4) as i:
                    for j in range(4):
                        load(b4 + i, j, W[name], l, 0, KT, (i * 4 + j) * P)

            sp_e.wait_ge(pool_set, 1)
            sp_e.dma_start(const[:, :], A["consts"]).then_inc(setup_in, 16)
            sp_e.dma_start(x_in.rearrange("p (t d) -> p t d", t=NQ),
                           A["x"][0].rearrange("(t p) d -> p t d", p=P)).then_inc(x_landed, 16)
            rows = [("ffn1_norm", 0, 0), ("final_norm", 0, 16), ("mix_norm", 0, 24), ("xa_norm", 0, 40),
                    ("mem_norm", 0, 56), ("ffn2_norm", 0, 72), ("attn_norm_2", 0, 88), ("final_norm_2", 0, 104),
                    ("ffn_norm_2", 0, 112), ("conf_dw", 1, 0), ("conf_dw_b", 1, 124), ("conf_ln_g", 2, 0),
                    ("conf_ln_b", 2, 4), ("sc_dw", 2, 8), ("ret_norm_2", 2, 20), ("diff_norm_2", 2, 22)]
            for name, t, r in rows:
                a = A[name]
                if len(a.shape) == 3:
                    a = a.rearrange("l j (i c) -> (l j i) c", c=P)
                elif len(a.shape) == 2:
                    a = a.rearrange("l (i c) -> (l i) c", c=P)
                else:
                    a = a.rearrange("(i c) -> i c", c=P)
                sp_e.dma_start(par_in[r:r + a.shape[0], t * P:(t + 1) * P], a).then_inc(setup_in, 16)
            sp_e.dma_start(pos_i, A["positions"].to_broadcast([P, S])).then_inc(setup_in, 16)
            for i, name in enumerate(("lambda_q1_2", "lambda_k1_2", "lambda_q2_2", "lambda_k2_2")):
                sp_e.dma_start(lam_in[:, i * P:(i + 1) * P],
                               A[name].rearrange("(o l) d -> o (l d)", o=1).to_broadcast([P, P])).then_inc(setup_in, 16)

            for l in range(2):
                b4 = l * (N_L1 // 4)
                load_ffn(b4, l, "ffn1_w_gate", "ffn1_w_up", "ffn1_w_down")
                for c, (first, width) in enumerate(IN1):
                    load(b4 + O_MIX // 4 + c // 4, c % 4, W["w_in"], l, 0, KT, first, width)
                load_plain(b4 + O_OUT // 4, l, "w_out", 8)
                sp_e.wait_ge(o_ready, PV1 * l + 4)
                sp_e.dma_start(mem_in.rearrange("p (t d) -> p t d", t=2),
                               A["mem"][0].rearrange("(t p) d -> p t d", p=P)).then_inc(mem_landed, 16)
                load_plain(b4 + O_WQ // 4, l, "xa_wq", 8)
                load_plain(b4 + O_KV // 4, l, "xa_wkv", 16)
                load_plain(b4 + O_WO // 4, l, "xa_wo", 8)
                load_ffn(b4 + O_FFN2 // 4, l, "ffn2_w_gate", "ffn2_w_up", "ffn2_w_down")
            for l in range(2):
                b4 = 2 * (N_L1 // 4) + l * (N_L2 // 4)
                load_plain(b4, l, "w_in_2", 24)
                load_plain(b4 + O2_OUT // 4, l, "w_out_2", 8)
                load_ffn(b4 + O2_FFN // 4, l, "w_gate_2", "w_up_2", "w_down_2")
            sp_e.wait_ge(x_set, 8 + 8 + 8 + 8)
            sp_e.dma_start(out[0].rearrange("(t p) d -> p t d", p=P),
                           y_out.rearrange("p (t d) -> p t d", t=NQ)).then_inc(stored, 16)
            sp_e.wait_ge(stored, 16)

        @block.tensor
        def _(pe):
            mm = nc.tensor.matmul

            def chunk(b4, j, rhs_hi, rhs_lo, kn=KT, last=None, n=S):
                at = 4 * b4 + j
                pe.wait_ge(split, at + RING + 1)
                pe.wait_ge(taken, at + 1)
                s = j % RING
                for k in range(kn):
                    if last is not None and k == kn - 1:
                        pe.wait_ge(last[0], last[1])
                    w = slice(k * P, (k + 1) * P)
                    r = slice(k * n, (k + 1) * n)
                    o = bank[s][:, 0:n]
                    mm(o, w_hi[:, s, w], rhs_hi[:, r], start=k == 0, stop=False)
                    mm(o, w_hi[:, s, w], rhs_lo[:, r], start=False, stop=False)
                    ins = mm(o, w_lo[:, s, w], rhs_hi[:, r], start=False, stop=k == kn - 1)
                ins.then_inc(tiles, 1)

            def stat(q):
                pe.wait_ge(sq_sum, 8 * q + 8)
                for t in range(NQ):
                    ins = mm(bank[7][:, t:t + 1], sumsq[:, t * P:(t + 1) * P], one, start=True, stop=True)
                ins.then_inc(stat_mm, 1)

            def spread(q):
                pe.wait_ge(stat_diag, q + 1)
                mm(bank[7][:, :], ones, diag, start=True, stop=True).then_inc(stat_bc, 1)

            def first_two(b4, q, j, **kw):
                last = (u_ready, 8 * q + 8)
                if j == 0:
                    pe.wait_ge(u_ready, 8 * q + 7)
                chunk(b4, j, u_hi, u_lo, last=last if j == 0 else None)
                if j == 0:
                    stat(q)
                if j == 1:
                    spread(q)

            def ffn(b4, q, f):
                for g, (f0, fn) in enumerate(F_GROUPS):
                    if g == 0:
                        for j in range(4):
                            first_two(b4, q, j)
                    with pe.Fori(1 if g == 0 else 0, fn // 2) as i:
                        for j in range(4):
                            chunk(b4 + i, j, u_hi, u_lo)
                    b4 = b4 + fn // 2
                    pe.wait_ge(f_ready, F_TILES * f + f0 + fn - 1)
                    with pe.Fori(0, 2) as i:
                        for j in range(4):
                            chunk(b4 + i, j, h_hi, h_lo, kn=fn,
                                  last=(f_ready, F_TILES * f + (f0 + fn)) if j == 0 else None)
                    b4 = b4 + 2

            def plain(b4, chunks, hi, lo, n=S):
                with pe.Fori(0, chunks // 4) as i:
                    for j in range(4):
                        chunk(b4 + i, j, hi, lo, n=n)

            def rotate(r0, r, b4, c, src, rows=P):
                pe.wait_ge(taken, 4 * b4 + c + RING + 1)
                if r:
                    pe.wait_ge(roped, r0 + r)
                mm(bank[6][0:rows, :], rot[0:rows, 0:rows], src[0:rows, :], start=True, stop=True).then_inc(rot_mm, 1)

            def transposes(e, src, blocks, to, width=P):
                for j in range(blocks):
                    ins = nc.tensor.transpose(bank[to][:, j * P:(j + 1) * P], src[:, j * P:(j + 1) * P], ident)
                ins.then_inc(e, 1)

            def v_transpose(v0, i, b4, c, blocks=NQ, src=None):
                pe.wait_ge(taken, 4 * b4 + c + RING + 1)
                if i >= 2:
                    pe.wait_ge(v_set, v0 + i - 1)
                transposes(v_tr, src if src is not None else y_buf[c % 2], blocks, T_BANK[c % 2])

            pe.wait_ge(x_landed, 16)
            pe.wait_ge(setup_in, 16 * 22)
            for t in range(3):
                ins = nc.tensor.transpose(bank[3][:, t * P:(t + 1) * P], par_in[:, t * P:(t + 1) * P], ident)
            ins.then_inc(par_tr, 1)
            for k in range(KT):
                if k >= 4:
                    pe.wait_ge(x_set, k - 3)
                for t in range(NQ):
                    ins = nc.tensor.transpose(bank[4 + k % 4][:, t * P:(t + 1) * P],
                                              x_in[:, t * D + k * P:t * D + (k + 1) * P], ident)
                ins.then_inc(x_tr, 1)
            pe.wait_ge(x_set, KT)

            for l in range(2):
                L = l * (N_L1 // 4)
                ffn(L, 4 * l, 2 * l)

                b4, q, r0 = L + O_MIX // 4, 4 * l + 1, ROPES * l
                N0 = 4 * b4
                for c in range(len(IN1)):
                    if c < 2:
                        first_two(b4, q, c)
                    else:
                        chunk(b4 + c // 4, c % 4, u_hi, u_lo)
                    p = c - 1
                    if p == 0:
                        rotate(r0, 0, b4, 0, y_buf[0], 64)
                    if p == 1:
                        pe.wait_ge(taken, N0 + 2 + RING)
                        for t in range(NQ):
                            ins = nc.tensor.transpose(bank[7][:, 4 * t:4 * t + 4], w_idx_t[0:4, t * P:(t + 1) * P],
                                                      const[0:4, C_ID:C_ID + 4])
                        ins.then_inc(wi_tr, 1)
                    if 2 <= p < 6:
                        rotate(r0, p - 1, b4, p, y_buf[p % 2], 64)
                    if C_Q <= p < C_V:
                        rotate(r0, 5 + p - C_Q, b4, p, y_buf[p % 2])
                    if p == 7:
                        pe.wait_ge(roped, r0 + 5)
                        for i in range(12):
                            t, h = 1 + i // 4, i % 4
                            if i >= 2:
                                pe.wait_ge(idx_relu, 12 * l + i - 1)
                            mm(bank[S_BANK[i % 2]][:, 0:P * (t + 1)], q_idx[h][0:64, t * P:(t + 1) * P],
                               k_idx[0:64, 0:P * (t + 1)], start=True, stop=True).then_inc(idx_mm, 1)
                    if p >= C_V:
                        if p == C_V:
                            pe.wait_ge(roped, r0 + ROPES)
                        v_transpose(12 * l, p - C_V, b4, p)
                v_transpose(12 * l, 3, b4, 27)

                s0, pv0 = SCORES1 * l, PV1 * l
                pe.wait_ge(roped, r0 + ROPES)
                pe.wait_ge(taken, N0 + 28 + RING)
                pe.wait_ge(v_set, 12 * l + 4)

                def pv_sparse(h):
                    pe.wait_ge(t_set, s0 + 4 * h + 4)
                    if h >= 4 and h % 2 == 0:
                        pe.wait_ge(o_ready, PV1 * l + h // 2 - 1)
                    o = bank[(h // 2) % 2]
                    rows = slice(64 * (h % 2), 64 * (h % 2) + 64)
                    for j in range(NQ):
                        ins = mm(o[rows, j * P:S], v_t[:, j * S + 64 * h:j * S + 64 * h + 64],
                                 pt[h % 2][:, j * S + j * P:(j + 1) * S], start=j == 0, stop=j == NQ - 1)
                    ins.then_inc(pv_mm, 1)

                for i in range(32 + 3):
                    if i < 32:
                        h, t = i // 4, i % 4
                        rows = slice(64 * (h % 2), 64 * (h % 2) + 64)
                        if i >= 2:
                            pe.wait_ge(s_min, s0 + i - 1)
                        mm(bank[S_BANK[i % 2]][:, 0:P * (t + 1)],
                           q_t[rows, (h // 2) * S + t * P:(h // 2) * S + (t + 1) * P],
                           k_t[rows, (h // 2) * S:(h // 2) * S + P * (t + 1)], start=True, stop=True).then_inc(s_mm, 1)
                    if 2 <= i < 34:
                        pe.wait_ge(p_norm, s0 + i - 1)
                        if i >= 4:
                            pe.wait_ge(t_set, s0 + i - 3)
                        transposes(t_mm, prob[i % 2], (i - 2) % 4 + 1, T_BANK[i % 2])
                    if i >= 3 and (i - 3) % 4 == 3:
                        pv_sparse((i - 3) // 4)
                    if i == 4:
                        pe.wait_ge(conv0, l + 1)
                        pe.wait_ge(conv1, l + 1)
                        mm(bank[2][:, :], ones, conv[0], start=True, stop=False)
                        mm(bank[2][:, :], ones, conv[1], start=False, stop=True).then_inc(ln_mean, 1)
                    if i == 8:
                        pe.wait_ge(ln_sq, 2 * l + 2)
                        for t in range(NQ):
                            for c in range(2):
                                ins = mm(bank[3][:, t:t + 1], y_buf[c][:, t * P:(t + 1) * P], one, start=c == 0, stop=c == 1)
                        ins.then_inc(ln_mm, 1)
                    if i == 12:
                        pe.wait_ge(ln_d, l + 1)
                        mm(bank[2][:, :], ones, rope_t, start=True, stop=True).then_inc(ln_bc, 1)

                pe.wait_ge(o_ready, PV1 * l + 4)
                pe.wait_ge(y_ready, 4 * l + 4)
                plain(L + O_OUT // 4, 8, h_hi, h_lo)

                b4, q = L + O_WQ // 4, 4 * l + 2
                for c in range(8):
                    if c < 2:
                        first_two(b4, q, c)
                    else:
                        chunk(b4 + c // 4, c % 4, u_hi, u_lo)
                    if 2 <= c < 6:
                        r = c - 2
                        pe.wait_ge(mem_n, l + 1)
                        if r >= 2:
                            pe.wait_ge(gm_ready, 8 * l + 2 * (r - 2) + 2)
                        for k in range(2):
                            for t in range(2):
                                ins = nc.tensor.transpose(bank[S_BANK[r % 2]][:, (2 * k + t) * P:(2 * k + t + 1) * P],
                                                          mem_in[:, t * D + (2 * r + k) * P:t * D + (2 * r + k + 1) * P], ident)
                        ins.then_inc(mem_tr, 1)
                pe.wait_ge(gm_ready, 8 * l + 8)
                plain(L + O_KV // 4, 8, h_hi, h_lo, n=MEM)
                b4 = L + O_KV // 4 + 2
                for c in range(8):
                    chunk(b4 + c // 4, c % 4, h_hi, h_lo, n=MEM)
                    if c >= 1:
                        v_transpose(12 * l, 4 + c - 1, b4, c - 1, 2, vx_t[(c - 1) % 2])
                v_transpose(12 * l, 4 + 7, b4, 7, 2, vx_t[1])

                s0, pv0 = SCORES1 * l + 32, PV1 * l + 8
                pe.wait_ge(taken, 4 * b4 + 8 + RING)
                pe.wait_ge(v_set, 12 * l + 12)
                for i in range(16 + 3):
                    if i < 16:
                        h, t = i // 4, i % 4
                        if i >= 2:
                            pe.wait_ge(p_exp, s0 + i - 1)
                        for c in range(2):
                            ins = mm(bank[S_BANK[i % 2]][:, 0:MEM], qx[:, (2 * h + c) * S + t * P:(2 * h + c) * S + (t + 1) * P],
                                     km[:, (2 * h + c) * MEM:(2 * h + c + 1) * MEM], start=c == 0, stop=c == 1)
                        ins.then_inc(s_mm, 1)
                    if 2 <= i < 18:
                        pe.wait_ge(p_norm, s0 + i - 1)
                        if i >= 4:
                            pe.wait_ge(t_set, s0 + i - 3)
                        transposes(t_mm, px[i % 2], 2, T_BANK[i % 2])
                    if i >= 3 and (i - 3) % 4 == 3:
                        h = (i - 3) // 4
                        pe.wait_ge(t_set, s0 + 4 * h + 4)
                        if h >= 2:
                            pe.wait_ge(o_ready, PV1 * l + 4 + 2 * (h - 2) + 2)
                        for d in range(2):
                            for j in range(2):
                                ins = mm(bank[2 * (h % 2) + d][:, :], vm[:, j * D + (2 * h + d) * P:j * D + (2 * h + d + 1) * P],
                                         ptx[h % 2][:, j * S:(j + 1) * S], start=j == 0, stop=j == 1)
                        ins.then_inc(pv_mm, 1)
                pe.wait_ge(o_ready, PV1 * l + 4 + 8)
                plain(L + O_WO // 4, 8, h_hi, h_lo)
                ffn(L + O_FFN2 // 4, 4 * l + 3, 2 * l + 1)

            stat(8)
            spread(8)

            for l in range(2):
                L = 2 * (N_L1 // 4) + l * (N_L2 // 4)
                q = 9 + 2 * l
                v0, e0 = 24 + 8 * l, 8 * l

                def retention(h):
                    for j in range(NQ + 1):
                        i = 4 * h + j
                        rows = slice(64 * (h % 2), 64 * (h % 2) + 64)
                        if j < NQ:
                            if i >= 2:
                                pe.wait_ge(r_dec, 16 * l + i - 1)
                            mm(bank[S_BANK[i % 2]][:, 0:S - j * P],
                               rk_t[rows, (h // 2) * S + j * P:(h // 2) * S + (j + 1) * P],
                               rq_t[rows, (h // 2) * S + j * P:(h // 2 + 1) * S], start=True, stop=True).then_inc(r_mm, 1)
                        if j >= 1:
                            pe.wait_ge(r_dec, 16 * l + i)
                            if j == 1 and h >= 1:
                                pe.wait_ge(z_sq, e0 + h)
                            ins = mm(bank[6][:, (j - 1) * P:S],
                                     rv_t[:, (j - 1) * S + h * P:(j - 1) * S + (h + 1) * P],
                                     sd[:, (j - 1) * S:j * S - (j - 1) * P], start=j == 1, stop=j == NQ)
                    ins.then_inc(rpv_mm, 1)

                def head_stat(h, first, to):
                    pe.wait_ge(z_sq, e0 + first + h + 1)
                    for t in range(NQ):
                        ins = mm(bank[to][:, 4 * h + t:4 * h + t + 1], zsq[h % 2][:, t * P:(t + 1) * P], one,
                                 start=True, stop=True)
                    ins.then_inc(z_mm, 1)

                def head_spread(h, first, banks):
                    pe.wait_ge(h_d, e0 + first + h + 1)
                    if h >= 2:
                        pe.wait_ge(z_norm, e0 + first + h - 1)
                    mm(bank[banks[h % 2]][:, :], ones, diag, start=True, stop=True).then_inc(h_bc, 1)

                for c in range(24):
                    if c < 2:
                        first_two(L, q, c)
                    else:
                        chunk(L + c // 4, c % 4, u_hi, u_lo)
                    p = c - 1
                    if R_V <= p < R_G:
                        v_transpose(v0, p - R_V, L, p)
                    if R_G <= c < D_Q:
                        if c == R_G:
                            pe.wait_ge(v_set, v0 + 4)
                        if c > R_G:
                            head_stat(c - R_G - 1, 0, 7)
                        retention(c - R_G)
                    if c == D_Q:
                        head_stat(3, 0, 7)
                    if D_Q < c <= D_Q + 4:
                        head_spread(c - D_Q - 1, 0, S_BANK)
                    if D_V <= p:
                        v_transpose(v0, 4 + p - D_V, L, p)
                v_transpose(v0, 7, L, 23)

                s0 = 2 * SCORES1 + 16 * l
                pe.wait_ge(taken, 4 * L + 24 + RING)
                pe.wait_ge(v_set, v0 + 8)
                pe.wait_ge(z_norm, e0 + 4)
                for i in range(16 + 2):
                    if i < 16:
                        h, t = i // 4, i % 4
                        if i >= 1:
                            pe.wait_ge(s_min, s0 + i)
                        for j in range(2):
                            rows = slice(64 * j, 64 * j + 64)
                            ins = mm(bank[S_BANK[j]][:, 0:P * (t + 1)], dq_t[rows, h * S + t * P:h * S + (t + 1) * P],
                                     dk_t[rows, h * S:h * S + P * (t + 1)], start=True, stop=True)
                        ins.then_inc(s_mm, 1)
                    if 1 <= i < 17:
                        pe.wait_ge(p_norm, s0 + i)
                        if i >= 3:
                            pe.wait_ge(t_set, s0 + i - 2)
                        transposes(t_mm, dp[(i - 1) % 2][0], (i - 1) % 4 + 1, T_BANK[(i - 1) % 2])
                    if i >= 2 and (i - 2) % 4 == 3:
                        h = (i - 2) // 4
                        pe.wait_ge(t_set, s0 + 4 * h + 4)
                        if h >= 2:
                            pe.wait_ge(z_sq, e0 + 4 + h - 1)
                        for j in range(NQ):
                            ins = mm(bank[2 + h % 2][:, j * P:S], dv_t[:, j * S + h * P:j * S + (h + 1) * P],
                                     d_pt[:, j * S + j * P:(j + 1) * S], start=j == 0, stop=j == NQ - 1)
                        ins.then_inc(pv_mm, 1)
                        if h >= 1:
                            head_stat(h - 1, 4, 0)
                head_stat(3, 4, 0)
                for h in range(4):
                    head_spread(h, 4, (1, 0))
                pe.wait_ge(o_ready, 2 * PV1 + 8 * l + 8)
                plain(L + O2_OUT // 4, 8, h_hi, h_lo)
                ffn(L + O2_FFN // 4, 10 + 2 * l, 4 + l)

            stat(13)
            spread(13)
            for k in range(KT):
                pe.wait_ge(x_set, 16 + k + 1)
                if k >= 4:
                    pe.wait_ge(x_set, 24 + k - 3)
                for t in range(NQ):
                    ins = nc.tensor.transpose(bank[k % 4][:, t * P:(t + 1) * P], x[:, k * S + t * P:k * S + (t + 1) * P], ident)
                ins.then_inc(x_tr, 1)

        @block.scalar
        def _(act):
            a = nc.scalar.activation
            chain = Chain(chain_a)

            def round_weights(b4, j, ahead=RING):
                act.wait_ge(raw_in[j], (b4 + (1 + ahead // 4)) * 16)
                if ahead:
                    act.wait_ge(tiles, 4 * b4 + j + 1)
                a(w_hi[:, j, :], raw[:, j, :], ACT.Copy).then_inc(rounded, 1)

            def finish(q, k, gain):
                a(tile(u_hi, k), tile(x, k), ACT.Copy, scale=col(gain)).then_inc(u_rounded, 1)

            def keep_rstd(q):
                act.wait_ge(stat_bc, q + 1)
                a(rstd[:, :], bank[7][:, :], ACT.Copy).then_inc(rstd_set, 1)

            def step(n4, j, more=True):
                if more:
                    round_weights(n4, j)

            def ffn(b4, q, f, gain, more=True):
                for g, (f0, fn) in enumerate(F_GROUPS):
                    def pair(b4, f_at, h_at, jj):
                        step(b4, 2 * jj)
                        act.wait_ge(taken, 4 * b4 + 2 * jj + RING + 1)
                        a(tanh_t, gate_t, ACT.Tanh, scale=0.5).then_inc(f_tanh, 1)
                        step(b4, 2 * jj + 1)
                        act.wait_ge(f_prod, F_TILES * f + f_at + 1)
                        a(tile(h_hi, h_at), gate_t, ACT.Copy).then_inc(f_rounded, 1)

                    if g == 0:
                        step(b4, 0)
                        step(b4, 1)
                        keep_rstd(q)
                        act.wait_ge(taken, 4 * b4 + RING + 1)
                        a(tanh_t, gate_t, ACT.Tanh, scale=0.5).then_inc(f_tanh, 1)
                        act.wait_ge(f_prod, F_TILES * f + 1)
                        a(tile(h_hi, 0), gate_t, ACT.Copy).then_inc(f_rounded, 1)
                        pair(b4, 1, 1, 1)
                    with act.Fori(1 if g == 0 else 0, fn // 2) as i:
                        for jj in range(2):
                            pair(b4 + i, i * 2 + (f0 + jj), i * 2 + jj, jj)
                    b4 = b4 + fn // 2
                    end = g == len(F_GROUPS) - 1

                    def down(b4, k, j, more):
                        step(b4, j, more)
                        if end:
                            act.wait_ge(taken, 4 * b4 + j + RING + 1)
                            finish(q + 1, k, gain + k)
                    with act.Fori(0, 1 if end and not more else 2) as i:
                        for j in range(4):
                            down(b4 + i, i * 4 + j, j, True)
                    if end and not more:
                        for j in range(4):
                            down(b4 + 1, 4 + j, j, False)
                    b4 = b4 + 2

            def plain_finish(b4, q, gain):
                with act.Fori(0, 2) as i:
                    for j in range(4):
                        step(b4 + i, j)
                        act.wait_ge(taken, 4 * (b4 + i) + j + RING + 1)
                        finish(q, i * 4 + j, i * 4 + (gain + j))

            def v_store(i, c, dst, blocks=NQ):
                act.wait_ge(v_tr, i + 1)
                a(dst, bank[T_BANK[c % 2]][:, 0:blocks * P].rearrange("p (j n) -> p j n", n=P), ACT.Copy)\
                    .then_inc(v_set, 1)

            for j in range(4):
                round_weights(0, j, 0)
            act.wait_ge(tab_set, 1)
            act.wait_ge(pool_set, 3)
            a(sin_t[:, :], cos_t[:, :], ACT.Sin, scale=0.5)
            a(rstd[:, :], cos_t[:, :], ACT.Sin, scale=0.5, bias=half_pi).then_inc(tab_sin, 1)
            act.wait_ge(par_set, 1)
            for k in range(KT):
                act.wait_ge(x_set, k + 1)
                finish(0, k, G_FFN1 + k)
            act.wait_ge(tab_set, 2)
            act.wait_ge(par_set, 2)
            a(lam_s, lam_s, ACT.Exp).then_inc(tab_sin, 1)

            for l in range(2):
                L = l * (N_L1 // 4)
                ffn(L, 4 * l, 2 * l, G_MIX + 8 * l)

                b4, q, r0 = L + O_MIX // 4, 4 * l + 1, ROPES * l
                N0 = 4 * b4
                for c in range(28):
                    step(b4 + c // 4, c % 4)
                    if c == 1:
                        keep_rstd(q)
                    p = c - 1
                    if p == 7:
                        for i in range(12):
                            act.wait_ge(idx_mm, 12 * l + i + 1)
                            if i >= 2:
                                act.wait_ge(idx_add, 12 * l + i - 1)
                            n = P * (i // 4 + 2)
                            a(relu_t[i % 2][:, 0:n], bank[S_BANK[i % 2]][:, 0:n], ACT.Relu).then_inc(idx_relu, 1)
                    if c in (C_AG, C_AG + 1):
                        act.wait_ge(taken, N0 + c + RING + 1)
                        a(y_buf[c % 2], y_buf[c % 2], ACT.Tanh, scale=0.5).then_inc(a_tanh, 1)
                    if c in (C_BH + 3, C_BH + 5):
                        i = (c - C_BH - 3) // 2
                        act.wait_ge(y_made, 2 * l + i + 1)
                        a(tile(h_hi, 2 + i), yb_t, ACT.Copy).then_inc(y_rounded, 1)
                    if p >= C_V:
                        i = p - C_V
                        v_store(12 * l + i, p, v_t.rearrange("p (j n) -> p j n", j=NQ)[:, :, i * P:(i + 1) * P])
                v_store(12 * l + 3, 27, v_t.rearrange("p (j n) -> p j n", j=NQ)[:, :, 3 * P:4 * P])

                act.wait_ge(conv0, l + 1)
                act.wait_ge(conv1, l + 1)
                s0 = SCORES1 * l
                for i in range(32 + 4):
                    if i < 32:
                        t = i % 4
                        act.wait_ge(s_min, s0 + i + 1)
                        if i >= 2:
                            act.wait_ge(t_mm, s0 + i - 1)
                        a(prob[i % 2][:, 0:P * (t + 1)], sp[i % 2][:, 0:P * (t + 1)], ACT.Exp, bias=neg_max[i % 4],
                          scale=-1.0, accum_out=row_sum[i % 4]).then_inc(p_exp, 1)
                    if 2 <= i < 34:
                        h, t = (i - 2) // 4, (i - 2) % 4
                        act.wait_ge(t_mm, s0 + i - 1)
                        if h >= 2 and t == 0:
                            act.wait_ge(pv_mm, PV1 * l + h - 1)
                        a(pt[h % 2].rearrange("p (j n) -> p j n", j=NQ)[:, 0:t + 1, t * P:(t + 1) * P],
                          bank[T_BANK[i % 2]][:, 0:(t + 1) * P].rearrange("p (j n) -> p j n", n=P), ACT.Copy)\
                            .then_inc(t_set, 1)
                    if i >= 4 and (i - 4) % 8 == 7:
                        g = (i - 4) // 8
                        act.wait_ge(pv_mm, PV1 * l + 2 * g + 2)
                        a(tile(h_hi, 4 + g), bank[g % 2][:, :], ACT.Copy).then_inc(o_rounded, 1)
                    if i == 13:
                        act.wait_ge(ln_y, 2 * l + 2)
                        for c in range(2):
                            a(conv[c], conv[c], ACT.Identity, scale=col(G_LNG + 2 * l + c), bias=col(G_LNB + 2 * l + c))\
                                .then_inc(ln_z, 1)
                        for c in range(2):
                            act.wait_ge(ln_z, 2 * l + c + 1)
                            a(y_buf[c], conv[c], ACT.Tanh, scale=0.5).then_inc(ln_t, 1)
                    if i == 16:
                        for c in range(2):
                            act.wait_ge(a_glu, 4 * l + 2 + c + 1)
                            a(tile(h_hi, c), conv[c], ACT.Copy, scale=0.5).then_inc(y_rounded, 1)

                plain_finish(L + O_OUT // 4, 4 * l + 2, G_XA + 8 * l)

                b4, q = L + O_WQ // 4, 4 * l + 2
                for c in range(8):
                    step(b4 + c // 4, c % 4)
                    if c == 0:
                        act.wait_ge(mem_landed, 16 * (l + 1))
                        for t in range(2):
                            a(ptx[t], mem_in[:, t * D:(t + 1) * D], ACT.Square, accum_out=mem_var[:, t:t + 1])\
                                .then_inc(mem_sq, 1)
                    if c == 1:
                        keep_rstd(q)
                    if 3 <= c < 7:
                        r = c - 3
                        act.wait_ge(mem_tr, 4 * l + r + 1)
                        for k in range(2 * r, 2 * r + 2):
                            a(h_hi[:, k * MEM:(k + 1) * MEM], bank[S_BANK[r % 2]][:, (k % 2) * MEM:(k % 2 + 1) * MEM],
                              ACT.Copy, scale=col(G_MEM + 8 * l + k)).then_inc(gm_rounded, 1)
                with act.Fori(0, 2) as i:
                    for j in range(4):
                        step(L + O_KV // 4 + i, j)
                b4 = L + O_KV // 4 + 2
                for c in range(8):
                    step(b4 + c // 4, c % 4)
                    if c >= 1:
                        i = c - 1
                        v_store(12 * l + 4 + i, i, vm.rearrange("p (j n) -> p j n", j=2)[:, :, i * P:(i + 1) * P], 2)
                v_store(12 * l + 11, 7, vm.rearrange("p (j n) -> p j n", j=2)[:, :, 7 * P:8 * P], 2)

                s0 = SCORES1 * l + 32
                for i in range(16 + 4):
                    if i < 16:
                        act.wait_ge(s_min, s0 + i + 1)
                        if i >= 2:
                            act.wait_ge(t_mm, s0 + i - 1)
                        a(px[i % 2], bank[S_BANK[i % 2]][:, 0:MEM], ACT.Exp, bias=neg_max[i % 4], scale=-1.0,
                          accum_out=row_sum[i % 4]).then_inc(p_exp, 1)
                    if 2 <= i < 18:
                        h, t = (i - 2) // 4, (i - 2) % 4
                        act.wait_ge(t_mm, s0 + i - 1)
                        if h >= 2 and t == 0:
                            act.wait_ge(pv_mm, PV1 * l + 8 + h - 1)
                        a(ptx[h % 2].rearrange("p (j n) -> p j n", j=2)[:, :, t * P:(t + 1) * P],
                          bank[T_BANK[i % 2]][:, 0:2 * P].rearrange("p (j n) -> p j n", n=P), ACT.Copy).then_inc(t_set, 1)
                    if i >= 4 and (i - 4) % 4 == 3:
                        h = (i - 4) // 4
                        act.wait_ge(pv_mm, PV1 * l + 8 + h + 1)
                        for d in range(2):
                            a(tile(h_hi, 2 * h + d), bank[2 * (h % 2) + d][:, :], ACT.Copy).then_inc(o_rounded, 1)
                plain_finish(L + O_WO // 4, 4 * l + 3, G_FFN2 + 8 * l)
                ffn(L + O_FFN2 // 4, 4 * l + 3, 2 * l + 1, G_FFN1 + 8 * (l + 1))

            keep_rstd(8)
            for k in range(KT):
                act.wait_ge(x_set, 8 + k + 1)
                finish(9, k, G_ATTN2 + k)

            for l in range(2):
                L = 2 * (N_L1 // 4) + l * (N_L2 // 4)
                q, v0, e0 = 9 + 2 * l, 24 + 8 * l, 8 * l

                def decay(h):
                    if h >= 2:
                        act.wait_ge(r_dec, 16 * l + 4 * (h - 2) + 4)
                    a(table[h % 2], const[:, C_DEC:C_DEC + S], ACT.Exp, scale=LOG_GAMMA[h]).then_inc(dec_set, 1)

                def head_square(h, first, done, to):
                    act.wait_ge(done, (4 * l if done is rpv_mm else 2 * PV1 + 4 * l) + h + 1)
                    if h >= 2:
                        act.wait_ge(z_mm, e0 + first + h - 1)
                    a(tile(z_t, h), bank[to][:, :], ACT.Copy)
                    a(zsq[h % 2], bank[to][:, :], ACT.Square).then_inc(z_sq, 1)

                def head_round(h, first):
                    act.wait_ge(z_norm, e0 + first + h + 1)
                    a(tile(h_hi, first + h), tile(z_t, h), ACT.Copy).then_inc(o_rounded, 1)

                for c in range(24):
                    step(L + c // 4, c % 4)
                    if c == 1:
                        keep_rstd(q)
                    if c == 2:
                        decay(0)
                        decay(1)
                    p = c - 1
                    if R_V <= p < R_G:
                        i = p - R_V
                        v_store(v0 + i, p, rv_t.rearrange("p (j n) -> p j n", j=NQ)[:, :, i * P:(i + 1) * P])
                    if R_G <= c < D_Q:
                        h = c - R_G
                        act.wait_ge(taken, 4 * L + c + RING + 1)
                        a(y_buf[c % 2], tile(gate_s, h), ACT.Tanh, scale=0.5).then_inc(g_tanh, 1)
                        head_square(h, 0, rpv_mm, 6)
                        if h < 2:
                            decay(h + 2)
                    if D_Q + 2 <= c < D_Q + 6:
                        head_round(c - D_Q - 2, 0)
                    if D_V <= p:
                        i = p - D_V
                        v_store(v0 + 4 + i, p, dv_t.rearrange("p (j n) -> p j n", j=NQ)[:, :, i * P:(i + 1) * P])
                v_store(v0 + 7, 23, dv_t.rearrange("p (j n) -> p j n", j=NQ)[:, :, 3 * P:4 * P])

                s0 = 2 * SCORES1 + 16 * l
                for i in range(16 + 3):
                    if i < 16:
                        t, b = i % 4, i % 2
                        act.wait_ge(s_min, s0 + i + 1)
                        if i >= 2:
                            act.wait_ge(t_mm, s0 + i - 1)
                        for j in range(2):
                            ins = a(dp[b][j][:, 0:P * (t + 1)], dsp[b][j][:, 0:P * (t + 1)], ACT.Exp, bias=neg_max[2 * b + j],
                                    scale=-1.0, accum_out=row_sum[2 * b + j])
                        ins.then_inc(p_exp, 1)
                    if 1 <= i < 17:
                        h, t = (i - 1) // 4, (i - 1) % 4
                        act.wait_ge(t_mm, s0 + i)
                        if h >= 1 and t == 0:
                            act.wait_ge(pv_mm, 2 * PV1 + 4 * l + h)
                        a(d_pt.rearrange("p (j n) -> p j n", j=NQ)[:, 0:t + 1, t * P:(t + 1) * P],
                          bank[T_BANK[(i - 1) % 2]][:, 0:(t + 1) * P].rearrange("p (j n) -> p j n", n=P), ACT.Copy)\
                            .then_inc(t_set, 1)
                    if i >= 3 and (i - 3) % 4 == 3:
                        head_square((i - 3) // 4, 4, pv_mm, 2 + (i - 3) // 4 % 2)
                for h in range(4):
                    head_round(h, 4)
                plain_finish(L + O2_OUT // 4, 10 + 2 * l, G_FFNN2 + 8 * l)
                ffn(L + O2_FFN // 4, 10 + 2 * l, 4 + l, G_ATTN2 + 8 * (l + 1), more=l == 0)
            keep_rstd(13)

        @block.vector
        def _(v):
            tt, ts, stt = nc.vector.tensor_tensor, nc.vector.tensor_scalar, nc.vector.scalar_tensor_tensor
            chain = Chain(chain_v)

            def rest_of_weights(b4, j, ahead=RING):
                v.wait_ge(rounded, 4 * b4 + j + ahead + 1)
                tt(w_lo[:, j, :], raw[:, j, :], f32(w_hi[:, j, :]), ALU.subtract).then_inc(split, 1)

            def rest(dst_hi, dst_lo, src, scale, e):
                stt(dst_lo, src, scale, f32(dst_hi), ALU.mult, ALU.subtract).then_inc(e, 1)

            def scaled(dst, b4, c, factor=1.0, rows=P):
                v.wait_ge(tiles, 4 * b4 + c + 1)
                stt(dst[0:rows, :], bank[c % 4][0:rows, :], factor, rstd[0:rows, :], ALU.mult, ALU.mult).then_inc(taken, 1)

            def make_diag(values, to, e):
                for t in range(NQ):
                    ins = ts(to[:, t * P:(t + 1) * P], ident, values[:, t:t + 1], None, ALU.mult)
                ins.then_inc(e, 1)

            def norm_scale(q):
                v.wait_ge(stat_mm, q + 1)
                ts(var, bank[7][:, 0:NQ], 1.0 / D, EPS, ALU.mult, ALU.add).then_inc(stat_var, 1)
                v.wait_ge(stat_inv, q + 1)
                make_diag(inv, diag, stat_diag)

            def finish(q, k, gain):
                v.wait_ge(u_rounded, k + 8 * q + 1)
                rest(tile(u_hi, k), tile(u_lo, k), tile(x, k), col(gain), u_ready)

            def residual(b4, j, k, factor):
                v.wait_ge(tiles, 4 * b4 + j + 1)
                stt(tile(x, k), bank[j][:, :], factor, tile(x, k), ALU.mult, ALU.add).then_inc(taken, 1)

            def ffn(b4, q, f, gain, factor, more=True):
                for g, (f0, fn) in enumerate(F_GROUPS):
                    def gate(b4, j, f_at):
                        if f_at is not None:
                            v.wait_ge(f_ready, F_TILES * f + (f_at - 1) + 1)
                        v.wait_ge(tiles, 4 * b4 + j + 1)
                        tt(gate_t, bank[j][:, :], rstd[:, :], ALU.mult).then_inc(taken, 1)

                    def up(b4, j, f_at, h_at):
                        v.wait_ge(tiles, 4 * b4 + j + 1)
                        tt(up_t, bank[j][:, :], rstd[:, :], ALU.mult).then_inc(taken, 1)
                        v.wait_ge(f_tanh, F_TILES * f + f_at + 1)
                        chain.done(v, stt(gate_t, tanh_t, 1.0, gate_t, ALU.add, ALU.mult))
                        tt(gate_t, gate_t, up_t, ALU.mult).then_inc(f_prod, 1)
                        v.wait_ge(f_rounded, F_TILES * f + f_at + 1)
                        rest(tile(h_hi, h_at), tile(h_lo, h_at), gate_t, 1.0, f_ready)

                    if g == 0:
                        rest_of_weights(b4, 0)
                        norm_scale(q)
                        rest_of_weights(b4, 1)
                        v.wait_ge(rstd_set, q + 1)
                        gate(b4, 0, None)
                        up(b4, 1, 0, 0)
                        rest_of_weights(b4, 2)
                        gate(b4, 2, 1)
                        rest_of_weights(b4, 3)
                        up(b4, 3, 1, 1)
                    with chain.loop(v, 1 if g == 0 else 0, fn // 2, 2) as i:
                        for jj in range(2):
                            rest_of_weights(b4 + i, 2 * jj)
                            gate(b4 + i, 2 * jj, i * 2 + (f0 + jj))
                            rest_of_weights(b4 + i, 2 * jj + 1)
                            up(b4 + i, 2 * jj + 1, i * 2 + (f0 + jj), i * 2 + jj)
                    b4 = b4 + fn // 2
                    end = g == len(F_GROUPS) - 1
                    with v.Fori(0, 1 if end and not more else 2) as i:
                        for j in range(4):
                            rest_of_weights(b4 + i, j)
                            residual(b4 + i, j, i * 4 + j, factor)
                            if end:
                                finish(q + 1, i * 4 + j, i * 4 + (gain + j))
                    if end and not more:
                        for j in range(4):
                            residual(b4 + 1, j, 4 + j, factor)
                            finish(q + 1, 4 + j, gain + 4 + j)
                    b4 = b4 + 2

            def plain_finish(b4, q, gain):
                with v.Fori(0, 2) as i:
                    for j in range(4):
                        rest_of_weights(b4 + i, j)
                        residual(b4 + i, j, i * 4 + j, 1.0)
                        finish(q, i * 4 + j, i * 4 + (gain + j))

            def normalise(i, p, s_at):
                v.wait_ge(p_exp, s_at + 1)
                chain.done(v, nc.vector.reciprocal(row_inv[i % 4], row_sum[i % 4]))
                ts(p, p, row_inv[i % 4], None, ALU.mult).then_inc(p_norm, 1)

            v.sem_inc(split, RING)
            v.sem_inc(taken, RING)
            for j in range(4):
                rest_of_weights(0, j, 0)
            v.wait_ge(par_tr, 1)
            chain.done(v, nc.vector.tensor_copy(par[:, :], bank[3][:, 0:G_N]))
            ts(par[:, G_DW:G_DWB], par[:, G_DW:G_DWB], 0.5, None, ALU.mult)
            for l in range(2):
                ins = ts(par[:, G_DIF + l:G_DIF + l + 1], par[:, G_DIF + l:G_DIF + l + 1], 1.0 - LAM_INIT[l], None, ALU.mult)
            ins.then_inc(par_set, 1)
            v.wait_ge(par_set, 1)
            for k in range(KT):
                v.wait_ge(x_tr, k + 1)
                nc.vector.tensor_copy(tile(x, k), bank[4 + k % 4][:, :]).then_inc(x_set, 1)
            ang, turns = y_buf[0], conv[0]
            v.wait_ge(setup_in, 16 * 22)
            chain.done(v, nc.vector.tensor_copy(ang, pos_i))
            chain.done(v, ts(ang, ang, const[:, C_INV:C_INV + 1], None, ALU.mult))
            chain.done(v, ts(turns, ang, 1.0 / (2 * math.pi), ROUND, ALU.mult, ALU.add))
            chain.done(v, ts(turns, turns, ROUND, None, ALU.subtract))
            chain.done(v, stt(ang, turns, -TWO_PI[0], ang, ALU.mult, ALU.add))
            chain.done(v, stt(ang, turns, -TWO_PI[1], ang, ALU.mult, ALU.add))
            stt(cos_t[:, :], turns, -TWO_PI[2], ang, ALU.mult, ALU.add).then_inc(tab_set, 1)
            v.wait_ge(tab_sin, 1)
            chain.done(v, stt(cos_t[:, :], sin_t[:, :], -2.0, sin_t[:, :], ALU.mult, ALU.mult))
            chain.done(v, ts(cos_t[:, :], cos_t[:, :], 1.0, None, ALU.add))
            stt(sin_t[:, :], sin_t[:, :], 2.0, rstd[:, :], ALU.mult, ALU.mult).then_inc(tab_set, 1)
            for i in range(2):
                pr = lam_in[:, 2 * i * P:(2 * i + 1) * P]
                chain.done(v, tt(pr, pr, lam_in[:, (2 * i + 1) * P:(2 * i + 2) * P], ALU.mult))
                ins = nc.vector.tensor_reduce(lam_s[:, 2 * i:2 * i + 2], pr.rearrange("p (l d) -> p l d", l=2), AX_X, ALU.add)
                if i == 0:
                    chain.done(v, ins)
            ins.then_inc(par_set, 1)
            v.wait_ge(tab_sin, 2)
            chain.done(v, tt(neg_lam, lam_s[:, 2:4], lam_s[:, 0:2], ALU.subtract))
            for l in range(2):
                chain.done(v, ts(neg_lam[:, l:l + 1], neg_lam[:, l:l + 1], -LAM_INIT[l], None, ALU.add))
            for k in range(KT):
                finish(0, k, G_FFN1 + k)

            for l in range(2):
                L = l * (N_L1 // 4)
                ffn(L, 4 * l, 2 * l, G_MIX + 8 * l, 0.25)

                b4, q, r0 = L + O_MIX // 4, 4 * l + 1, ROPES * l
                N0 = 4 * b4

                def combine(r, p, dst, rows=P):
                    v.wait_ge(rot_mm, r0 + r + 1)
                    chain.done(v, tt(rope_t[0:rows, :], bank[6][0:rows, :], sin_t[0:rows, :], ALU.mult))
                    v.wait_ge(cos_mul, r0 + r + 1)
                    tt(dst[0:rows, :], rope_t[0:rows, :], y_buf[p % 2][0:rows, :], ALU.add).then_inc(roped, 1)
                    v.wait_ge(roped, r0 + r + 1)

                def top_rounds(first, last):
                    for n in range(first, min(last, 3 * ROUNDS)):
                        w = work[1 + n // ROUNDS]
                        chain.done(v, nc.vector.max(max8, w))
                        chain.done(v, nc.vector.match_replace(w, max8, w, TAKEN))

                def taps(first, last):
                    for j in range(first, min(last, TAPS)):
                        w, src = col(G_DW + 2 * (TAPS * l + j)), a_pad[0][:, j:j + S]
                        if j == 0:
                            ins = ts(conv[0], src, w, col(G_DWB + 2 * l), ALU.mult, ALU.add)
                        else:
                            ins = stt(conv[0], src, w, conv[0], ALU.mult, ALU.add)
                        if j < TAPS - 1:
                            chain.done(v, ins)
                        else:
                            ins.then_inc(conv0, 1)

                def take(c):
                    if c == 0:
                        scaled(y_buf[0], b4, c, rows=64)
                    elif c == 1:
                        scaled(w_idx_t, b4, c, 1.0 / 16, rows=4)
                    elif c < 6:
                        scaled(y_buf[c % 2], b4, c, rows=64)
                    elif c < C_AG:
                        if c == C_AV:
                            v.wait_ge(pads, l + 1)
                        scaled(a_pad[c % 2][:, PAD:], b4, c)
                    elif c < C_BG:
                        scaled(y_buf[c % 2], b4, c)
                    elif c < C_CG:
                        scaled(b_gate[c % 2], b4, c)
                    elif c < C_BH:
                        if c == C_CG:
                            for i in range(2):
                                chain.done(v, nc.vector.memset(c_pad[i][:, 0:SC_PAD], 0.0))
                        scaled(c_pad[c % 2][:, SC_PAD:], b4, c)
                    elif c < C_Q:
                        scaled(y_buf[c % 2], b4, c)
                        v.wait_ge(taken, N0 + c + RING + 1)
                        cp = c_pad[c % 2][:, SC_PAD:]
                        chain.done(v, tt(cp, cp, y_buf[c % 2], ALU.mult))
                    elif c < C_K:
                        scaled(y_buf[c % 2], b4, c, -0.125)
                    else:
                        if c >= C_V + 2:
                            v.wait_ge(v_tr, 12 * l + c - 2 - C_V + 1)
                        scaled(y_buf[c % 2], b4, c)

                for c in range(28):
                    rest_of_weights(b4 + c // 4, c % 4)
                    if c == 0:
                        norm_scale(q)
                        continue
                    if c == 1:
                        v.wait_ge(rstd_set, q + 1)
                        take(0)
                    take(c)
                    p = c - 1
                    if p == 0:
                        combine(0, 0, k_idx, 64)
                    if p == 1:
                        v.wait_ge(wi_tr, l + 1)
                        nc.vector.tensor_copy(w_idx, bank[7][:, 0:16]).then_inc(wi_set, 1)
                    if 2 <= p < 6:
                        combine(p - 1, p, q_idx[p - 2], 64)
                    if p == 7:
                        v.wait_ge(wi_set, l + 1)
                        for i in range(12):
                            t, h = 1 + i // 4, i % 4
                            v.wait_ge(idx_relu, 12 * l + i + 1)
                            if h:
                                v.wait_ge(idx_add, 12 * l + i)
                            n = P * (t + 1)
                            base = work[t] if h else const[:, C_NEG + S - n:C_NEG + S]
                            stt(work[t], relu_t[i % 2][:, 0:n], w_idx[:, 4 * t + h:4 * t + h + 1], base, ALU.mult, ALU.add)\
                                .then_inc(idx_add, 1)
                        v.wait_ge(idx_add, 12 * l + 12)
                    if p in (C_AG, C_AG + 1):
                        i = p - C_AG
                        v.wait_ge(a_tanh, 2 * l + i + 1)
                        ap = a_pad[i][:, PAD:]
                        stt(ap, y_buf[p % 2], 1.0, ap, ALU.add, ALU.mult).then_inc(a_glu, 1)
                        v.wait_ge(a_glu, 4 * l + i + 1)
                    if p in (C_BH + 1, C_BH + 3):
                        i = (p - C_BH - 1) // 2
                        if i:
                            v.wait_ge(y_ready, 4 * l + 1)
                        g = G_SC + 2 * SC_TAPS * l + i
                        chain.done(v, ts(yb_t, c_pad[i][:, 0:S], col(g), None, ALU.mult))
                        for j in (1, 2):
                            chain.done(v, stt(yb_t, c_pad[i][:, j:j + S], col(g + 2 * j), yb_t, ALU.mult, ALU.add))
                        tt(yb_t, yb_t, b_gate[i], ALU.mult).then_inc(y_made, 1)
                    if p in (C_BH + 2, C_BH + 4):
                        i = (p - C_BH - 2) // 2
                        v.wait_ge(y_rounded, 4 * l + i + 1)
                        rest(tile(h_hi, 2 + i), tile(h_lo, 2 + i), yb_t, 1.0, y_ready)
                    if C_Q <= p < C_K:
                        combine(5 + p - C_Q, p, tile(q_t, p - C_Q))
                    if C_K <= p < C_V:
                        combine(5 + p - C_Q, p, tile(k_t, p - C_K))
                    if p >= 8:
                        n = p - 8
                        top_rounds(n * 48 // 19, (n + 1) * 48 // 19)
                    if p >= C_AG + 1:
                        n = p - C_AG - 1
                        taps(n * TAPS // 18, (n + 1) * TAPS // 18)
                for t in range(1, NQ):
                    ins = ts(work[t], work[t], TAKEN / 2, BIG, ALU.is_gt, ALU.mult)
                ins.then_inc(masked, 1)
                v.wait_ge(masked, l + 1)

                s0 = SCORES1 * l
                for i in range(32 + 4):
                    if i < 32:
                        t = i % 4
                        n = P * (t + 1)
                        v.wait_ge(s_mm, s0 + i + 1)
                        mask = work[t] if t else const[:, C_BIG:C_BIG + P]
                        nc.vector.tensor_tensor_reduce(sp[i % 2][:, 0:n], bank[S_BANK[i % 2]][:, 0:n], mask, 1.0, BIG,
                                                       ALU.add, ALU.min, neg_max[i % 4]).then_inc(s_min, 1)
                    if 1 <= i < 33:
                        normalise(i - 1, prob[(i - 1) % 2][:, 0:P * ((i - 1) % 4 + 1)], s0 + i - 1)
                    if i >= 4 and (i - 4) % 8 == 7:
                        g = (i - 4) // 8
                        v.wait_ge(o_rounded, PV1 * l + g + 1)
                        rest(tile(h_hi, 4 + g), tile(h_lo, 4 + g), bank[g % 2][:, :], 1.0, o_ready)
                    if i == 5:
                        v.wait_ge(ln_mean, l + 1)
                        for c in range(2):
                            stt(conv[c], bank[2][:, :], -1.0 / 256, conv[c], ALU.mult, ALU.add).then_inc(ln_cent, 1)
                    if i == 9:
                        v.wait_ge(ln_mm, l + 1)
                        ts(ln_var, bank[3][:, 0:NQ], 1.0 / 256, LN_EPS, ALU.mult, ALU.add).then_inc(ln_v, 1)
                    if i == 11:
                        v.wait_ge(ln_i, l + 1)
                        make_diag(ln_inv, rope_t, ln_d)
                    if i == 13:
                        v.wait_ge(ln_bc, l + 1)
                        for c in range(2):
                            tt(conv[c], bank[2][:, :], conv[c], ALU.mult).then_inc(ln_y, 1)
                    if i == 15:
                        for c in range(2):
                            v.wait_ge(ln_t, 2 * l + c + 1)
                            stt(conv[c], y_buf[c], 1.0, conv[c], ALU.add, ALU.mult).then_inc(a_glu, 1)
                    if i == 17:
                        for c in range(2):
                            v.wait_ge(y_rounded, 4 * l + 2 + c + 1)
                            rest(tile(h_hi, c), tile(h_lo, c), conv[c], 0.5, y_ready)

                plain_finish(L + O_OUT // 4, 4 * l + 2, G_XA + 8 * l)

                b4, q = L + O_WQ // 4, 4 * l + 2
                for c in range(8):
                    rest_of_weights(b4 + c // 4, c % 4)
                    if c == 0:
                        norm_scale(q)
                        continue
                    if c == 1:
                        v.wait_ge(rstd_set, q + 1)
                        scaled(tile(qx, 0), b4, 0, -1.0 / 16)
                    scaled(tile(qx, c), b4, c, -1.0 / 16)
                    if c == 1:
                        v.wait_ge(mem_i, l + 1)
                        for t in range(2):
                            mt = mem_in[:, t * D:(t + 1) * D]
                            ins = ts(mt, mt, mem_inv[:, t:t + 1], None, ALU.mult)
                        ins.then_inc(mem_n, 1)
                    if 3 <= c < 7:
                        r = c - 3
                        for k in range(2 * r, 2 * r + 2):
                            v.wait_ge(gm_rounded, 8 * l + 2 * r + 2)
                            ks = slice(k * MEM, (k + 1) * MEM)
                            rest(h_hi[:, ks], h_lo[:, ks], bank[S_BANK[r % 2]][:, (k % 2) * MEM:(k % 2 + 1) * MEM],
                                 col(G_MEM + 8 * l + k), gm_ready)
                with v.Fori(0, 2) as i:
                    for j in range(4):
                        rest_of_weights(L + O_KV // 4 + i, j)
                        v.wait_ge(tiles, 4 * (L + O_KV // 4 + i) + j + 1)
                        nc.vector.tensor_copy(km[:, bass.ds((i * 4 + j) * MEM, MEM)], bank[j][:, 0:MEM]).then_inc(taken, 1)
                b4 = L + O_KV // 4 + 2
                for c in range(8):
                    rest_of_weights(b4 + c // 4, c % 4)
                    v.wait_ge(tiles, 4 * b4 + c + 1)
                    if c >= 2:
                        v.wait_ge(v_tr, 12 * l + 4 + c - 1)
                    nc.vector.tensor_copy(vx_t[c % 2], bank[c % 4][:, 0:MEM]).then_inc(taken, 1)

                s0 = SCORES1 * l + 32
                for i in range(16 + 4):
                    if i < 16:
                        v.wait_ge(s_mm, s0 + i + 1)
                        nc.vector.tensor_reduce(neg_max[i % 4], bank[S_BANK[i % 2]][:, 0:MEM], AX_X, ALU.min).then_inc(s_min, 1)
                    if 1 <= i < 17:
                        normalise(i - 1, px[(i - 1) % 2], s0 + i - 1)
                    if i >= 4 and (i - 4) % 4 == 3:
                        h = (i - 4) // 4
                        for d in range(2):
                            k = 2 * h + d
                            v.wait_ge(o_rounded, PV1 * l + 4 + k + 1)
                            rest(tile(h_hi, k), tile(h_lo, k), bank[2 * (h % 2) + d][:, :], 1.0, o_ready)
                plain_finish(L + O_WO // 4, 4 * l + 3, G_FFN2 + 8 * l)
                ffn(L + O_FFN2 // 4, 4 * l + 3, 2 * l + 1, G_FFN1 + 8 * (l + 1), 0.25)

            def normed(q, first, k):
                chain.done(v, tt(tile(x, k), f32(tile(u_hi, k)), f32(tile(u_lo, k)), ALU.add))
                tt(tile(x, k), tile(x, k), rstd[:, :], ALU.mult).then_inc(x_set, 1)

            norm_scale(8)
            v.wait_ge(rstd_set, 9)
            for k in range(KT):
                normed(8, 8, k)
                v.wait_ge(x_set, 8 + k + 1)
                finish(9, k, G_ATTN2 + k)

            for l in range(2):
                L = 2 * (N_L1 // 4) + l * (N_L2 // 4)
                q, v0, e0 = 9 + 2 * l, 24 + 8 * l, 8 * l

                def head_var(n, src):
                    v.wait_ge(z_mm, e0 + 4 * n + 4)
                    ts(h_var, src, 1.0 / P, EPS, ALU.mult, ALU.add).then_inc(h_v, 1)

                def head_diag(h, first):
                    if h == 0:
                        v.wait_ge(h_i, 2 * l + first // 4 + 1)
                    make_diag(h_inv[:, 4 * h:4 * h + 4], diag, h_d)

                def head_norm(h, first, gain, src):
                    v.wait_ge(h_bc, e0 + first + h + 1)
                    z = tile(z_t, h)
                    ins = stt(z, z, col(gain + l), src, ALU.mult, ALU.mult)
                    if first == 0:
                        chain.done(v, ins)
                        ins = stt(z, z, 0.5, tile(gate_s, h), ALU.mult, ALU.mult)
                    ins.then_inc(z_norm, 1)

                def head_rest(h, first):
                    v.wait_ge(o_rounded, 2 * PV1 + e0 + first + h + 1)
                    rest(tile(h_hi, first + h), tile(h_lo, first + h), tile(z_t, h), 1.0, o_ready)

                def take2(c):
                    if c < R_K:
                        scaled(tile(rq_t, c), L, c)
                    elif c < R_V:
                        scaled(tile(rk_t, c - R_K), L, c, 0.125)
                    elif c < R_G:
                        if c >= R_V + 2:
                            v.wait_ge(v_tr, v0 + c - 2 - R_V + 1)
                        scaled(y_buf[c % 2], L, c)
                    elif c < D_Q:
                        scaled(tile(gate_s, c - R_G), L, c)
                    elif c < D_K:
                        scaled(tile(dq_t, c - D_Q), L, c, -0.125)
                    elif c < D_V:
                        scaled(tile(dk_t, c - D_K), L, c)
                    else:
                        if c >= D_V + 2:
                            v.wait_ge(v_tr, v0 + 4 + c - 2 - D_V + 1)
                        scaled(y_buf[c % 2], L, c)

                for c in range(24):
                    if D_Q + 2 <= c < D_Q + 6:
                        head_norm(c - D_Q - 2, 0, G_RET, bank[S_BANK[(c - D_Q - 2) % 2]][:, :])
                    if D_Q + 1 <= c < D_Q + 5:
                        head_diag(c - D_Q - 1, 0)
                    rest_of_weights(L + c // 4, c % 4)
                    if c == 0:
                        norm_scale(q)
                        continue
                    if c == 1:
                        v.wait_ge(rstd_set, q + 1)
                        take2(0)
                    take2(c)
                    if R_G <= c < D_Q:
                        h = c - R_G
                        v.wait_ge(dec_set, 4 * l + h + 1)
                        if h:
                            v.wait_ge(rpv_mm, 4 * l + h)
                        for j in range(NQ):
                            i = 4 * h + j
                            v.wait_ge(r_mm, 16 * l + i + 1)
                            tt(sd[:, j * S:(j + 1) * S - j * P], bank[S_BANK[i % 2]][:, 0:S - j * P],
                               table[h % 2][:, 0:S - j * P], ALU.mult).then_inc(r_dec, 1)
                        v.wait_ge(g_tanh, 4 * l + h + 1)
                        gs = tile(gate_s, h)
                        chain.done(v, stt(gs, y_buf[c % 2], 1.0, gs, ALU.add, ALU.mult))
                    if c == D_Q:
                        head_var(0, bank[7][:, 0:16])
                    if D_Q + 3 <= c < D_Q + 7:
                        head_rest(c - D_Q - 3, 0)

                s0 = 2 * SCORES1 + 16 * l
                for i in range(16 + 1):
                    if i < 16:
                        h, t, b = i // 4, i % 4, i % 2
                        if t == 0 and i:
                            v.wait_ge(s_min, s0 + i)
                        if t == 0:
                            chain.done(v, stt(table[0], const[:, C_DIST:C_DIST + S], SLOPE[h], const[:, C_NEG:C_NEG + S],
                                              ALU.mult, ALU.subtract))
                        n = P * (t + 1)
                        v.wait_ge(s_mm, s0 + i + 1)
                        for j in range(2):
                            ins = nc.vector.tensor_tensor_reduce(
                                dsp[b][j][:, 0:n], bank[S_BANK[j]][:, 0:n], table[0][:, S - n:S], 1.0, 2 * BIG,
                                ALU.add, ALU.min, neg_max[2 * b + j])
                        ins.then_inc(s_min, 1)
                    if i >= 1:
                        b, n = (i - 1) % 2, P * ((i - 1) % 4 + 1)
                        p0, p1 = dp[b][0][:, 0:n], dp[b][1][:, 0:n]
                        r0_, r1_ = row_inv[2 * b], row_inv[2 * b + 1]
                        v.wait_ge(p_exp, s0 + i)
                        chain.done(v, nc.vector.reciprocal(small[:, 16 + 2 * b:18 + 2 * b], small[:, 8 + 2 * b:10 + 2 * b]))
                        chain.done(v, ts(r1_, r1_, neg_lam[:, l:l + 1], None, ALU.mult))
                        chain.done(v, ts(p1, p1, r1_, None, ALU.mult))
                        stt(p0, p0, r0_, p1, ALU.mult, ALU.add).then_inc(p_norm, 1)
                head_var(1, bank[0][:, 0:16])
                for h in range(4):
                    head_diag(h, 4)
                    head_norm(h, 4, G_DIF, bank[1 - h % 2][:, :])
                for h in range(4):
                    head_rest(h, 4)
                plain_finish(L + O2_OUT // 4, 10 + 2 * l, G_FFNN2 + 8 * l)
                ffn(L + O2_FFN // 4, 10 + 2 * l, 4 + l, G_ATTN2 + 8 * (l + 1), 0.5, more=l == 0)

            norm_scale(13)
            v.wait_ge(rstd_set, 14)
            for k in range(KT):
                normed(13, 16, k)
            for k in range(KT):
                v.wait_ge(x_tr, 8 + k + 1)
                nc.vector.tensor_copy(y_out.rearrange("p (t d) -> p t d", t=NQ)[:, :, k * P:(k + 1) * P],
                                      bank[k % 4][:, :].rearrange("p (t n) -> p t n", n=P)).then_inc(x_set, 1)

        @block.gpsimd
        def _(pool):
            tt, ts = nc.gpsimd.tensor_tensor, nc.gpsimd.tensor_scalar
            chain = Chain(chain_p)

            def add_square(k):
                chain.done(pool, tt(square, tile(x, k), tile(x, k), ALU.mult))
                tt(sumsq, sumsq, square, ALU.add).then_inc(sq_sum, 1)

            def clear_sum():
                chain.done(pool, nc.gpsimd.memset(sumsq, 0.0))

            def squares(b4, q):
                pool.wait_ge(taken, 4 * b4 + RING + 1)
                clear_sum()
                with chain.loop(pool, 0, 2, 4) as i:
                    for j in range(4):
                        pool.wait_ge(taken, 4 * (b4 + i) + j + RING + 1)
                        if j:
                            pool.wait_ge(sq_sum, 8 * q + 4 * i + (j - 1) + 1)
                        add_square(i * 4 + j)
                    pool.wait_ge(sq_sum, 8 * q + 4 * i + 4)

            def norm_inv(q):
                pool.wait_ge(stat_var, q + 1)
                tt(inv, var, minus_half[:, 0:NQ], ALU.pow).then_inc(stat_inv, 1)

            nc.gpsimd.memset(par_in[:, 2 * P:3 * P], 0.0).then_inc(pool_set, 1)
            nc.gpsimd.memset(minus_half, -0.5).then_inc(pool_set, 1)
            nc.gpsimd.memset(half_pi, math.pi / 2).then_inc(pool_set, 1)
            pool.wait_ge(pool_set, 3)
            pool.wait_ge(tab_sin, 1)
            clear_sum()
            for k in range(KT):
                pool.wait_ge(x_set, k + 1)
                add_square(k)
                pool.wait_ge(sq_sum, k + 1)
            norm_inv(0)

            for l in range(2):
                L = l * (N_L1 // 4)
                last_down = L + (N_FFN - 8) // 4
                squares(last_down, 4 * l + 1)

                b4, r0 = L + O_MIX // 4, ROPES * l
                norm_inv(4 * l + 1)
                for i in range(2):
                    ins = nc.gpsimd.memset(a_pad[i][:, 0:PAD], 0.0)
                ins.then_inc(pads, 1)

                def times_cos(r, p, rows=P):
                    pool.wait_ge(rot_mm, r0 + r + 1)
                    y = y_buf[p % 2][0:rows, :]
                    tt(y, y, cos_t[0:rows, :], ALU.mult).then_inc(cos_mul, 1)

                def taps(first, last):
                    for j in range(first, last):
                        w, src = col(G_DW + 2 * (TAPS * l + j) + 1), a_pad[1][:, j:j + S]
                        if j == 0:
                            chain.done(pool, ts(conv[1], src, w, col(G_DWB + 2 * l + 1), ALU.mult, ALU.add))
                            continue
                        chain.done(pool, ts(tap_t, src, w, None, ALU.mult))
                        ins = tt(conv[1], conv[1], tap_t, ALU.add)
                        if j < TAPS - 1:
                            chain.done(pool, ins)
                        else:
                            ins.then_inc(conv1, 1)

                times_cos(0, 0, 64)
                for p in range(2, 6):
                    times_cos(p - 1, p, 64)
                pool.wait_ge(idx_mm, 12 * l + 12)
                pool.wait_ge(a_glu, 4 * l + 2)
                taps(0, 15)
                for p in range(C_Q, C_V):
                    times_cos(5 + p - C_Q, p)
                    taps(15 + 2 * (p - C_Q), 17 + 2 * (p - C_Q))
                for c in range(2):
                    pool.wait_ge(ln_cent, 2 * l + c + 1)
                    tt(y_buf[c], conv[c], conv[c], ALU.mult).then_inc(ln_sq, 1)
                pool.wait_ge(ln_v, l + 1)
                tt(ln_inv, ln_var, minus_half[:, 0:NQ], ALU.pow).then_inc(ln_i, 1)

                squares(L + O_OUT // 4, 4 * l + 2)
                norm_inv(4 * l + 2)
                pool.wait_ge(mem_sq, 2 * l + 2)
                chain.done(pool, ts(mem_var, mem_var, 1.0 / D, EPS, ALU.mult, ALU.add))
                tt(mem_inv, mem_var, minus_half[:, 0:2], ALU.pow).then_inc(mem_i, 1)
                squares(L + O_WO // 4, 4 * l + 3)
                norm_inv(4 * l + 3)
                squares(L + (O_FFN2 + N_FFN - 8) // 4, 4 * l + 4)
                norm_inv(4 * l + 4)

            clear_sum()
            for k in range(KT):
                pool.wait_ge(x_set, 8 + k + 1)
                add_square(k)
                pool.wait_ge(sq_sum, 72 + k + 1)
            norm_inv(9)

            for l in range(2):
                L = 2 * (N_L1 // 4) + l * (N_L2 // 4)
                if l:
                    norm_inv(9 + 2 * l)
                for n in range(2):
                    pool.wait_ge(h_v, 2 * l + n + 1)
                    tt(h_inv, h_var, minus_half, ALU.pow).then_inc(h_i, 1)
                squares(L + O2_OUT // 4, 10 + 2 * l)
                norm_inv(10 + 2 * l)
                squares(L + (O2_FFN + N_FFN - 8) // 4, 11 + 2 * l)
            norm_inv(13)


INPUTS = [
    "x", "mem", "positions", "ffn1_norm", "ffn1_w_gate", "ffn1_w_up", "ffn1_w_down", "mix_norm", "w_in", "conf_dw",
    "conf_dw_b", "conf_ln_g", "conf_ln_b", "sc_dw", "w_out", "xa_norm", "mem_norm", "xa_wq", "xa_wkv", "xa_wo",
    "ffn2_norm", "ffn2_w_gate", "ffn2_w_up", "ffn2_w_down", "final_norm", "attn_norm_2", "w_in_2", "ret_norm_2",
    "lambda_q1_2", "lambda_k1_2", "lambda_q2_2", "lambda_k2_2", "diff_norm_2", "w_out_2", "ffn_norm_2",
    "w_gate_2", "w_up_2", "w_down_2", "final_norm_2",
]


def kernel(**inputs):
    import concourse.bacc as bacc
    from concourse.bass_utils import run_bass_kernel_spmd as run

    nc = bacc.Bacc("TRN2", target_bir_lowering=False, num_devices=1)
    arrays = {f"in_{name}": np.ascontiguousarray(inputs[name]) for name in INPUTS}
    arrays["in_consts"] = constants()
    aps = {name[3:]: nc.dram_tensor(name, a.shape, mybir.dt.from_np(a.dtype), kind="ExternalInput").ap()
           for name, a in arrays.items()}
    out = nc.dram_tensor("out", (1, S, D), F32, kind="ExternalOutput").ap()
    two_blocks(nc, aps, out)
    r = run(nc, [arrays], core_ids=[0])
    return r.results[0]["out"]
```

```python
import math
from contextlib import ExitStack, contextmanager

import numpy as np

import concourse.bass as bass
from concourse import mybir

F32 = mybir.dt.float32
F32R = mybir.dt.float32r
I32 = mybir.dt.int32
ACT = mybir.ActivationFunctionType
ALU = mybir.AluOpType
AX_X = mybir.AxisListType.X

P = 128
S = 512
D = 1024
F = 2816
KT = D // P
NQ = S // P
MEM = 256
RING = 4
CH = KT * P
BIG = 1e30
TAKEN = -3e38
EPS = 1e-6
LN_EPS = 1e-5
TAPS, SC_TAPS = 31, 3
TOPK = 128
ROUNDS = TOPK // 8
PAD, SC_PAD = TAPS - 1, SC_TAPS - 1
LOG_GAMMA = [math.log(1.0 - 2.0 ** (-5 - h)) for h in range(4)]
SLOPE = [2.0 ** (-8.0 * (h + 1) / 4) for h in range(4)]
LAM_INIT = [0.8 - 0.6 * math.exp(-0.3 * m) for m in range(2)]
TWO_PI = (6.28125, 0.0019350051879882812, 2 * math.pi - 6.28125 - 0.0019350051879882812)
ROUND = 1.5 * 2 ** 23

C_ID, C_ONE, C_ROT, C_DIST, C_NEG, C_DEC, C_BIG, C_INV = 0, 128, 256, 384, 896, 1408, 1920, 2048
C_N = C_INV + 1

G_FFN1, G_FINAL, G_MIX, G_XA, G_MEM, G_FFN2, G_ATTN2, G_FINAL2, G_FFNN2 = 0, 16, 24, 40, 56, 72, 88, 104, 112
G_DW, G_DWB = 128, 252
G_JOINT = 280
G_LNG, G_LNB, G_SC, G_RET, G_DIF = 256, 260, 264, 276, 278
G_N = 3 * P

IN1 = ([(3072, 64), (3136, 4)] + [(2816 + 64 * h, 64) for h in range(4)]
       + [(128 * c, 128) for c in range(10)]
       + [(1280 + 128 * c, 128) for c in range(12)])
C_AV, C_AG, C_BG, C_CG, C_BH, C_Q, C_K, C_V = 6, 8, 10, 12, 14, 16, 20, 24
R_Q, R_K, R_V, R_G, D_Q, D_K, D_V = 0, 2, 4, 8, 12, 16, 20

F_GROUPS = [(0, 8), (8, 8), (16, 6)]
F_TILES = F // P
N_FFN = 2 * F_TILES + KT * len(F_GROUPS)
O_MIX = N_FFN
O_OUT = O_MIX + len(IN1)
O_WQ = O_OUT + 8
O_KV = O_WQ + 8
O_WO = O_KV + 16
O_FFN2 = O_WO + 8
N_L1 = O_FFN2 + N_FFN
O2_OUT = 24
O2_FFN = O2_OUT + 8
N_L2 = O2_FFN + N_FFN
N_ALL = 2 * N_L1 + 2 * N_L2
for _n in (N_FFN, O_MIX, O_OUT, O_WQ, O_KV, O_WO, O_FFN2, N_L1, O2_OUT, O2_FFN, N_L2):
    assert _n % RING == 0

LAG = 3
ROPES, SCORES1, PV1 = 13, 48, 12
WTILES = [0, 128, 384, 768]


def constants():
    c = np.zeros((P, C_N), np.float32)
    p = np.arange(P)[:, None]
    m = np.arange(S)[None, :]
    c[:, C_ID:C_ID + P] = np.eye(P)
    for j in range(P):
        c[j + 32 if j % 64 < 32 else j - 32, C_ROT + j] = -1.0 if j % 64 < 32 else 1.0
    dist = 384 + p - m
    c[:, C_DIST:C_DIST + S] = dist
    c[:, C_NEG:C_NEG + S] = np.where(dist >= 0, 0.0, -BIG)
    c[:, C_DEC:C_DEC + S] = np.where(m - p >= 0, m - p, 1e9)
    c[:, C_BIG:C_BIG + P] = np.where(np.arange(P)[None, :] <= p, 0.0, BIG)
    inv = (10000.0 ** (-np.arange(0, 64, 2) / 64)).astype(np.float32)
    c[:, C_INV] = inv[np.arange(P) % 32]
    c[:, C_ONE:C_ONE + P] = 1.0
    return c


class Chain:

    def __init__(self, sem):
        self.sem, self.base, self.k = sem, 0, 0

    def done(self, eng, ins):
        ins.then_inc(self.sem, 1)
        self.k += 1
        eng.wait_ge(self.sem, self.base + self.k)

    @contextmanager
    def loop(self, eng, start, end, per):
        base, k = self.base, self.k
        with eng.Fori(start, end) as i:
            self.base = base + (i - start) * per
            yield i
            assert self.k == k + per, f"per should be {self.k - k}"
        self.base, self.k = base, k + per * (end - start)


def two_blocks(nc, A, out):
    ctx = ExitStack()
    with ctx:
        def sb(name, shape, dt=F32):
            return ctx.enter_context(nc.sbuf_tensor(name, shape, dt))

        def sem(name):
            return ctx.enter_context(nc.semaphore(name))

        x = sb("x", [P, KT * S])
        raw = sb("raw", [P, RING, CH])
        w_hi, w_lo = sb("w_hi", [P, RING, CH], F32R), sb("w_lo", [P, RING, CH], F32R)
        const = sb("const", [P, C_N])
        par = sb("par", [P, G_N])
        cos_t, sin_t = sb("cos_t", [P, S]), sb("sin_t", [P, S])
        rstd = sb("rstd", [P, S])
        small = sb("small", [P, 128])
        mem = sb("mem", [P, 16140])
        with ExitStack() as operands:
            u_hi, u_lo, h_hi, h_lo = (
                operands.enter_context(nc.sbuf_tensor(n, [P, KT * S], F32R)) for n in ("u_hi", "u_lo", "h_hi", "h_lo"))
        spare = sb("spare", [P, 4 * KT * S])
        U_HI, U_LO, H_HI = 0, KT, 2 * KT
        bank = [ctx.enter_context(nc.psum_tensor(f"bank{i}", [P, S], F32)) for i in range(8)]

        def view(at, n):
            return mem[:, at:at + n]

        def tile(t, k, n=1):
            if isinstance(k, int):
                return t[:, k * S:(k + n) * S]
            return t[:, bass.ds(k * S, n * S)]

        def col(k):
            return par[:, k:k + 1] if isinstance(k, int) else par[:, bass.ds(k, 1)]

        def f32(ap):
            return ap.bitcast(F32)

        ident, rot = const[:, C_ID:C_ID + P], const[:, C_ROT:C_ROT + P]
        ones = const[:, C_ONE:C_ONE + P]
        one = const[:, C_ONE:C_ONE + 1]

        y_buf = [view(13572, S), view(14084, S)]
        square, diag = y_buf
        rope_t = view(14596, S)
        sumsq = rope_t
        conv = [view(15108, S), view(15620, S)]
        gate_t, tanh_t, up_t = view(0, S), view(S, S), view(2 * S, S)
        sp = [tile(spare, U_HI + i) for i in range(4)]
        prob = [tile(spare, U_HI + 4 + i) for i in range(4)]
        px = [p_[:, 0:MEM] for p_ in prob]
        dsp = [[tile(spare, U_HI + 2 * b + i) for i in range(2)] for b in range(4)]
        dp = [[tile(spare, U_LO + 2 * b + i) for i in range(2)] for b in range(4)]
        q_t, k_t, v_t = view(0, 2048), view(2048, 2048), view(4096, 2048)
        work = [view(6144 + WTILES[t], P * (t + 1)) for t in range(NQ)]
        pt = [view(11520, 2048), view(7424, 2048)]
        q_idx = [view(7424 + S * h, S) for h in range(4)]
        a_pad = [view(9472 + (PAD + S) * i, PAD + S) for i in range(2)]
        k_idx = view(10556, S)
        yb_t = k_idx
        w_idx_t = conv[0]
        tap_t = tile(spare, H_HI + 7)
        relu_t = [view(11520 + S * i, S) for i in range(2)]
        c_pad = [view(11520 + (SC_PAD + S) * i, SC_PAD + S) for i in range(2)]
        b_gate = [view(12548 + S * i, S) for i in range(2)]
        qx = view(0, 4096)
        km, vm = view(4096, 2048), view(6144, 2048)
        mem_in = view(8192, 2048)
        ptx = [view(10240 + 1024 * i, 1024) for i in range(2)]
        vx_t = [view(12800 + MEM * i, MEM) for i in range(2)]
        rq_t, rk_t, rv_t = view(0, 1024), view(1024, 1024), view(2048, 2048)
        dq_t, dk_t, dv_t = view(0, 2048), view(2048, 2048), view(9216, 2048)
        z_t = view(4096, 2048)
        table = [view(6144 + S * i, S) for i in range(2)]
        sd = view(7168, 2048)
        d_pt = sd
        gate_s = view(9216, 2048)
        zsq = conv
        x_in = view(0, 4096)
        par_in = view(8192, G_N)
        pos_i = view(9216, S).bitcast(I32)
        ang, turns, cos_half, x_sq = view(9728, S), view(10752, S), view(11264, S), view(11776, NQ * D)
        lam_in = view(10240, 2 * 4 * 64)
        y_out = tile(spare, U_HI, KT)
        z_in = view(2048, 4096)
        j_sq, j_sum = view(2048, 4096), view(6144, S)
        j_diag, j_scale = y_buf[0], view(11264, S)

        neg_max = [small[:, i:i + 1] for i in range(8)]
        row_sum = [small[:, 8 + i:9 + i] for i in range(8)]
        row_inv = [small[:, 16 + i:17 + i] for i in range(8)]
        var, inv = small[:, 24:28], small[:, 28:32]
        ln_var, ln_inv = small[:, 32:36], small[:, 36:40]
        w_idx = small[:, 40:56]
        max8 = small[:, 56:64]
        h_var, h_inv = small[:, 64:80], small[:, 80:96]
        minus_half = small[:, 96:112]
        neg_lam = small[:, 112:114]
        lam_s = small[:, 114:118]
        half_pi = small[:, 118:119]
        mem_var, mem_inv = small[:, 120:122], small[:, 122:124]
        j_var, j_inv = ln_var, ln_inv

        D_BANK = ((4, 5), (0, 1))
        S_BANK, T_BANK = (4, 5, 3), (6, 7)

        raw_in = [sem(f"raw_in{i}") for i in range(RING)]
        setup_in, x_landed, mem_landed, stored = sem("setup_in"), [sem(f"x_landed{t}") for t in range(NQ)], sem("mem_landed"), sem("stored")
        j_squared, j_diag_set, j_bc, j_set, z_rounded = (sem(n) for n in ("j_squared", "j_diag_set", "j_bc", "j_set", "z_rounded"))
        y_scaled = [sem(f"y_scaled{t}") for t in range(NQ)]
        par_in_set, x_squared = sem("par_in_set"), sem("x_squared")
        rounded = sem("rounded")
        split = sem("split")
        tiles = sem("tiles")
        taken = sem("taken")
        u_rounded, u_ready = sem("u_rounded"), sem("u_ready")
        sq_sum = sem("sq_sum")
        stat_mm, stat_var, stat_inv, stat_diag, stat_bc, rstd_set = (
            sem(n) for n in ("stat_mm", "stat_var", "stat_inv", "stat_diag", "stat_bc", "rstd_set"))
        x_set, x_tr = sem("x_set"), sem("x_tr")
        par_tr, par_set, tab_set, pool_set = sem("par_tr"), sem("par_set"), sem("tab_set"), sem("pool_set")
        tab_sin = sem("tab_sin")
        f_tanh, f_prod, f_rounded, f_ready = sem("f_tanh"), sem("f_prod"), sem("f_rounded"), sem("f_ready")
        rot_mm, cos_mul, roped = sem("rot_mm"), sem("cos_mul"), sem("roped")
        wi_tr, wi_set = sem("wi_tr"), sem("wi_set")
        idx_mm, idx_relu, idx_add = sem("idx_mm"), sem("idx_relu"), sem("idx_add")
        pads, a_tanh, a_glu = sem("pads"), sem("a_tanh"), sem("a_glu")
        conv0, conv1 = sem("conv0"), sem("conv1")
        y_made, y_rounded, y_ready = sem("y_made"), sem("y_rounded"), sem("y_ready")
        v_tr, v_set = sem("v_tr"), sem("v_set")
        ln_mean, ln_cent, ln_sq, ln_mm, ln_v, ln_i, ln_d, ln_bc, ln_y, ln_z, ln_t = (
            sem(n) for n in ("ln_mean", "ln_cent", "ln_sq", "ln_mm", "ln_v", "ln_i", "ln_d", "ln_bc", "ln_y", "ln_z", "ln_t"))
        masked = sem("masked")
        s_mm, s_min, p_exp, p_norm, t_mm, t_set, pv_mm = (
            sem(n) for n in ("s_mm", "s_min", "p_exp", "p_norm", "t_mm", "t_set", "pv_mm"))
        o_rounded, o_ready = sem("o_rounded"), sem("o_ready")
        mem_sq, mem_v, mem_i, mem_n, mem_tr, gm_rounded, gm_ready = (
            sem(n) for n in ("mem_sq", "mem_v", "mem_i", "mem_n", "mem_tr", "gm_rounded", "gm_ready"))
        r_mm, r_dec, dec_set, rpv_mm, z_sq, z_mm = (sem(n) for n in ("r_mm", "r_dec", "dec_set", "rpv_mm", "z_sq", "z_mm"))
        h_v, h_i, h_d, h_bc, z_norm, g_tanh, al_set = (
            sem(n) for n in ("h_v", "h_i", "h_d", "h_bc", "z_norm", "g_tanh", "al_set"))
        chain_v, chain_a, chain_p = sem("chain_v"), sem("chain_a"), sem("chain_p")

        W = {n: A[n].rearrange("l (k p) n -> l p k n", p=P) for n in (
            "ffn1_w_gate", "ffn1_w_up", "ffn1_w_down", "w_in", "w_out", "xa_wq", "xa_wkv", "xa_wo",
            "ffn2_w_gate", "ffn2_w_up", "ffn2_w_down", "w_in_2", "w_out_2", "w_gate_2", "w_up_2", "w_down_2")}

        block = ctx.enter_context(nc.Block())

        @block.sync
        def _(sp_e):
            def load(b4, j, w, l, k0, kn, c, width=P):
                sp_e.wait_ge(split, 4 * b4 + j + 1)
                dst = raw[:, j % RING, 0:kn * P].rearrange("p (k n) -> p k n", n=P)[:, :, 0:width]
                cols = slice(c, c + width) if isinstance(c, int) else bass.ds(c, width)
                sp_e.dma_start(dst, w[l, :, k0:k0 + kn, cols]).then_inc(raw_in[j % RING], 16)

            def load_ffn(b4, l, gate, up, down):
                for f0, fn in F_GROUPS:
                    with sp_e.Fori(0, fn // 2) as i:
                        for j in range(4):
                            load(b4 + i, j, W[up if j % 2 else gate], l, 0, KT, (i * 2 + (f0 + j // 2)) * P)
                    b4 = b4 + fn // 2
                    with sp_e.Fori(0, 2) as i:
                        for j in range(4):
                            load(b4 + i, j, W[down], l, f0, fn, (i * 4 + j) * P)
                    b4 = b4 + 2

            def load_plain(b4, l, name, chunks):
                with sp_e.Fori(0, chunks // 4) as i:
                    for j in range(4):
                        load(b4 + i, j, W[name], l, 0, KT, (i * 4 + j) * P)

            for t in range(NQ):
                sp_e.dma_start(x_in[:, t * D:(t + 1) * D], A["x"][0, t * P:(t + 1) * P, :]).then_inc(x_landed[t], 16)

            for l in range(2):
                b4 = l * (N_L1 // 4)
                load_ffn(b4, l, "ffn1_w_gate", "ffn1_w_up", "ffn1_w_down")
                for c, (first, width) in enumerate(IN1):
                    load(b4 + O_MIX // 4 + c // 4, c % 4, W["w_in"], l, 0, KT, first, width)
                load_plain(b4 + O_OUT // 4, l, "w_out", 8)
                sp_e.wait_ge(o_ready, PV1 * l + 4)
                sp_e.dma_start(mem_in.rearrange("p (t d) -> p t d", t=2),
                               A["mem"][0].rearrange("(t p) d -> p t d", p=P)).then_inc(mem_landed, 16)
                load_plain(b4 + O_WQ // 4, l, "xa_wq", 8)
                load_plain(b4 + O_KV // 4, l, "xa_wkv", 16)
                load_plain(b4 + O_WO // 4, l, "xa_wo", 8)
                load_ffn(b4 + O_FFN2 // 4, l, "ffn2_w_gate", "ffn2_w_up", "ffn2_w_down")
            for l in range(2):
                b4 = 2 * (N_L1 // 4) + l * (N_L2 // 4)
                load_plain(b4, l, "w_in_2", 24)
                load_plain(b4 + O2_OUT // 4, l, "w_out_2", 8)
                load_ffn(b4 + O2_FFN // 4, l, "w_gate_2", "w_up_2", "w_down_2")
            for t in (0, 2, 1, 3):
                sp_e.wait_ge(y_scaled[t], 1)
                sp_e.dma_start(out[0, t * P:(t + 1) * P, :], y_out[:, t * D:(t + 1) * D]).then_inc(stored, 16)
            sp_e.wait_ge(stored, 16 * NQ)

        @block.tensor
        def _(pe):
            mm = nc.tensor.matmul

            def chunk(b4, j, rhs_hi, rhs_lo, kn=KT, last=None, n=S, ks=None):
                at = 4 * b4 + j
                ks = ks or range(kn)
                if ks[0] == 0:
                    pe.wait_ge(split, at + RING + 1)
                    pe.wait_ge(taken, at + 1)
                s = j % RING
                for k in ks:
                    if last is not None and k >= kn - 2:
                        pe.wait_ge(last[0], last[1] - (kn - 1 - k))
                    w = slice(k * P, (k + 1) * P)
                    r = slice(k * n, (k + 1) * n)
                    o = bank[s][:, 0:n]
                    mm(o, w_hi[:, s, w], rhs_hi[:, r], start=k == 0, stop=False)
                    mm(o, w_hi[:, s, w], rhs_lo[:, r], start=False, stop=False)
                    ins = mm(o, w_lo[:, s, w], rhs_hi[:, r], start=False, stop=k == kn - 1)
                if ks[-1] == kn - 1:
                    ins.then_inc(tiles, 1)

            def stat(q):
                pe.wait_ge(sq_sum, 8 * q)
                for t in range(NQ):
                    ins = mm(bank[7][:, t:t + 1], sumsq[:, t * P:(t + 1) * P], one, start=True, stop=True)
                if q == 8:
                    for t in range(NQ):
                        ins = mm(bank[7][:, NQ + t:NQ + t + 1], j_sum[:, t * P:(t + 1) * P], one, start=True, stop=True)
                ins.then_inc(stat_mm, 1)

            def spread(q):
                pe.wait_ge(stat_diag, q + 1)
                mm(bank[7][:, :], ones, diag, start=True, stop=True).then_inc(stat_bc, 1)

            def first_two(b4, q, j, **kw):
                last = (u_ready, 8 * q + 8)
                if j == 0:
                    pe.wait_ge(u_ready, 8 * q + 6)
                chunk(b4, j, u_hi, u_lo, last=last if j == 0 else None)
                if j == 0 and q:
                    stat(q)
                if j == 1 and q:
                    spread(q)

            def result_transpose(k):
                pe.wait_ge(z_rounded, k + 1)
                if k >= 2:
                    pe.wait_ge(x_set, 16 + k - 1)
                for t in range(NQ):
                    ins = nc.tensor.transpose(bank[4 + k % 2][:, t * P:(t + 1) * P], z_in[:, k * S + t * P:k * S + (t + 1) * P], ident)
                ins.then_inc(x_tr, 1)

            def ffn(b4, q, f, end=False):
                for g, (f0, fn) in enumerate(F_GROUPS):
                    if g == 0:
                        if not q:
                            for k in range(KT):
                                pe.wait_ge(u_ready, k + 1)
                                chunk(b4, 0, u_hi, u_lo, ks=range(k, k + 1))
                            spread(0)
                        for j in range(0 if q else 1, 4):
                            first_two(b4, q, j)
                    with pe.Fori(1 if g == 0 else 0, fn // 2) as i:
                        for j in range(4):
                            chunk(b4 + i, j, u_hi, u_lo)
                    b4 = b4 + fn // 2
                    pe.wait_ge(f_ready, F_TILES * f + f0 + fn - 2)
                    if end and g == len(F_GROUPS) - 1:
                        for k in range(KT):
                            chunk(b4, k, h_hi, h_lo, kn=fn, last=(f_ready, F_TILES * f + (f0 + fn)) if k == 0 else None)
                            if k >= 2:
                                result_transpose(k - 2)
                        result_transpose(6)
                        result_transpose(7)
                        continue
                    with pe.Fori(0, 2) as i:
                        for j in range(4):
                            chunk(b4 + i, j, h_hi, h_lo, kn=fn,
                                  last=(f_ready, F_TILES * f + (f0 + fn)) if j == 0 else None)
                    b4 = b4 + 2

            def plain(b4, chunks, hi, lo, n=S, last=None):
                if last is not None:
                    pe.wait_ge(last[0], last[1] - 2)
                    for j in range(4):
                        chunk(b4, j, hi, lo, n=n, last=last if j == 0 else None)
                with pe.Fori(0 if last is None else 1, chunks // 4) as i:
                    for j in range(4):
                        chunk(b4 + i, j, hi, lo, n=n)

            def rotate(r0, r, b4, c, src, rows=P):
                pe.wait_ge(taken, 4 * b4 + c + RING + 1)
                if r:
                    pe.wait_ge(roped, r0 + r)
                mm(bank[6][0:rows, :], rot[0:rows, 0:rows], src[0:rows, :], start=True, stop=True).then_inc(rot_mm, 1)

            def transposes(e, src, blocks, to, width=P):
                for j in range(blocks):
                    ins = nc.tensor.transpose(bank[to][:, j * P:(j + 1) * P], src[:, j * P:(j + 1) * P], ident)
                ins.then_inc(e, 1)

            def v_transpose(v0, i, b4, c, blocks=NQ, src=None):
                pe.wait_ge(taken, 4 * b4 + c + RING + 1)
                if i >= 2:
                    pe.wait_ge(v_set, v0 + i - 1)
                transposes(v_tr, src if src is not None else y_buf[c % 2], blocks, T_BANK[c % 2])

            pe.wait_ge(par_in_set, 16 * 17)
            for t in range(3):
                ins = nc.tensor.transpose(bank[3][:, t * P:(t + 1) * P], par_in[:, t * P:(t + 1) * P], ident)
            ins.then_inc(par_tr, 1)
            for t in range(NQ):
                pe.wait_ge(x_landed[t], 16)
            for k in range(KT):
                if k >= 4:
                    pe.wait_ge(x_set, k - 3)
                for t in range(NQ):
                    ins = nc.tensor.transpose(bank[4 + k % 4][:, t * P:(t + 1) * P],
                                              x_in[:, t * D + k * P:t * D + (k + 1) * P], ident)
                ins.then_inc(x_tr, 1)

            for l in range(2):
                L = l * (N_L1 // 4)
                ffn(L, 4 * l, 2 * l)

                b4, q, r0 = L + O_MIX // 4, 4 * l + 1, ROPES * l
                N0 = 4 * b4
                for c in range(len(IN1)):
                    if c < 2:
                        first_two(b4, q, c)
                    else:
                        chunk(b4 + c // 4, c % 4, u_hi, u_lo)
                    p = c - 1
                    if p == 0:
                        rotate(r0, 0, b4, 0, y_buf[0], 64)
                    if p == 1:
                        pe.wait_ge(taken, N0 + 2 + RING)
                        for t in range(NQ):
                            ins = nc.tensor.transpose(bank[7][:, 4 * t:4 * t + 4], w_idx_t[0:4, t * P:(t + 1) * P],
                                                      const[0:4, C_ID:C_ID + 4])
                        ins.then_inc(wi_tr, 1)
                    if 2 <= p < 6:
                        rotate(r0, p - 1, b4, p, y_buf[p % 2], 64)
                    if C_Q <= p < C_V:
                        rotate(r0, 5 + p - C_Q, b4, p, y_buf[p % 2])
                    if p == 7:
                        pe.wait_ge(roped, r0 + 5)
                        for i in range(12):
                            t, h = 1 + i // 4, i % 4
                            if i >= 2:
                                pe.wait_ge(idx_relu, 12 * l + i - 1)
                            mm(bank[S_BANK[i % 2]][:, 0:P * (t + 1)], q_idx[h][0:64, t * P:(t + 1) * P],
                               k_idx[0:64, 0:P * (t + 1)], start=True, stop=True).then_inc(idx_mm, 1)
                    if p >= C_V:
                        if p == C_V:
                            pe.wait_ge(roped, r0 + ROPES)
                        v_transpose(12 * l, p - C_V, b4, p)
                v_transpose(12 * l, 3, b4, 27)

                s0, pv0 = SCORES1 * l, PV1 * l
                pe.wait_ge(roped, r0 + ROPES)
                pe.wait_ge(taken, N0 + 28 + RING)
                pe.wait_ge(v_set, 12 * l + 4)

                def pv_sparse(h):
                    pe.wait_ge(t_set, s0 + 4 * h + 4)
                    if h >= 4 and h % 2 == 0:
                        pe.wait_ge(o_ready, PV1 * l + h // 2 - 1)
                    o = bank[(h // 2) % 2]
                    rows = slice(64 * (h % 2), 64 * (h % 2) + 64)
                    for j in range(NQ):
                        ins = mm(o[rows, j * P:S], v_t[:, j * S + 64 * h:j * S + 64 * h + 64],
                                 pt[h % 2][:, j * S + j * P:(j + 1) * S], start=j == 0, stop=j == NQ - 1)
                    ins.then_inc(pv_mm, 1)

                for i in range(32 + LAG + 1):
                    if i < 32:
                        h, t = i // 4, i % 4
                        rows = slice(64 * (h % 2), 64 * (h % 2) + 64)
                        if i >= 3:
                            pe.wait_ge(s_min, s0 + i - 2)
                        mm(bank[S_BANK[i % 3]][:, 0:P * (t + 1)],
                           q_t[rows, (h // 2) * S + t * P:(h // 2) * S + (t + 1) * P],
                           k_t[rows, (h // 2) * S:(h // 2) * S + P * (t + 1)], start=True, stop=True).then_inc(s_mm, 1)
                    n = i - LAG
                    if 0 <= n < 32:
                        pe.wait_ge(p_norm, s0 + n + 1)
                        if n >= 2:
                            pe.wait_ge(t_set, s0 + n - 1)
                        transposes(t_mm, prob[n % 4], n % 4 + 1, T_BANK[n % 2])
                    if n >= 1 and n % 4 == 0:
                        pv_sparse(n // 4 - 1)
                    if i == 20:
                        pe.wait_ge(conv0, l + 1)
                        pe.wait_ge(conv1, l + 1)
                        mm(bank[2][:, :], ones, conv[0], start=True, stop=False)
                        mm(bank[2][:, :], ones, conv[1], start=False, stop=True).then_inc(ln_mean, 1)
                    if i == 23:
                        pe.wait_ge(ln_sq, 2 * l + 2)
                        for t in range(NQ):
                            for c in range(2):
                                ins = mm(bank[2][:, t:t + 1], y_buf[c][:, t * P:(t + 1) * P], one, start=c == 0, stop=c == 1)
                        ins.then_inc(ln_mm, 1)
                    if i == 26:
                        pe.wait_ge(ln_d, l + 1)
                        mm(bank[2][:, :], ones, rope_t, start=True, stop=True).then_inc(ln_bc, 1)

                pe.wait_ge(y_ready, 4 * l + 4)
                plain(L + O_OUT // 4, 8, h_hi, h_lo, last=(o_ready, PV1 * l + 4))

                b4, q = L + O_WQ // 4, 4 * l + 2
                for c in range(8):
                    if c < 2:
                        first_two(b4, q, c)
                    else:
                        chunk(b4 + c // 4, c % 4, u_hi, u_lo)
                    if 2 <= c < 6:
                        r = c - 2
                        pe.wait_ge(mem_n, l + 1)
                        if r >= 2:
                            pe.wait_ge(gm_ready, 8 * l + 2 * (r - 2) + 2)
                        for k in range(2):
                            for t in range(2):
                                ins = nc.tensor.transpose(bank[S_BANK[r % 2]][:, (2 * k + t) * P:(2 * k + t + 1) * P],
                                                          mem_in[:, t * D + (2 * r + k) * P:t * D + (2 * r + k + 1) * P], ident)
                        ins.then_inc(mem_tr, 1)
                pe.wait_ge(gm_ready, 8 * l + 8)
                plain(L + O_KV // 4, 8, h_hi, h_lo, n=MEM)
                b4 = L + O_KV // 4 + 2
                for c in range(8):
                    chunk(b4 + c // 4, c % 4, h_hi, h_lo, n=MEM)
                    if c >= 1:
                        v_transpose(12 * l, 4 + c - 1, b4, c - 1, 2, vx_t[(c - 1) % 2])
                v_transpose(12 * l, 4 + 7, b4, 7, 2, vx_t[1])

                s0, pv0 = SCORES1 * l + 32, PV1 * l + 8
                pe.wait_ge(taken, 4 * b4 + 8 + RING)
                pe.wait_ge(v_set, 12 * l + 12)
                for i in range(16 + LAG + 1):
                    if i < 16:
                        h, t = i // 4, i % 4
                        if i >= 3:
                            pe.wait_ge(p_exp, s0 + i - 2)
                        for c in range(2):
                            ins = mm(bank[S_BANK[i % 3]][:, 0:MEM], qx[:, (2 * h + c) * S + t * P:(2 * h + c) * S + (t + 1) * P],
                                     km[:, (2 * h + c) * MEM:(2 * h + c + 1) * MEM], start=c == 0, stop=c == 1)
                        ins.then_inc(s_mm, 1)
                    n = i - LAG
                    if 0 <= n < 16:
                        pe.wait_ge(p_norm, s0 + n + 1)
                        if n >= 2:
                            pe.wait_ge(t_set, s0 + n - 1)
                        transposes(t_mm, px[n % 4], 2, T_BANK[n % 2])
                    if n >= 1 and n % 4 == 0:
                        h = n // 4 - 1
                        pe.wait_ge(t_set, s0 + 4 * h + 4)
                        for d in range(2):
                            if 2 * h + d >= 3:
                                pe.wait_ge(o_ready, PV1 * l + 4 + 2 * h + d - 2)
                            for j in range(2):
                                ins = mm(bank[(2 * h + d + 1) % 3][:, :], vm[:, j * D + (2 * h + d) * P:j * D + (2 * h + d + 1) * P],
                                         ptx[h % 2][:, j * S:(j + 1) * S], start=j == 0, stop=j == 1)
                        ins.then_inc(pv_mm, 1)
                plain(L + O_WO // 4, 8, h_hi, h_lo, last=(o_ready, PV1 * l + 4 + 8))
                ffn(L + O_FFN2 // 4, 4 * l + 3, 2 * l + 1)

            for l in range(2):
                L = 2 * (N_L1 // 4) + l * (N_L2 // 4)
                q = 8 + 2 * l
                v0, e0 = 24 + 8 * l, 8 * l

                def retention(h):
                    for j in range(NQ + 1):
                        i = 4 * h + j
                        rows = slice(64 * (h % 2), 64 * (h % 2) + 64)
                        if j < NQ:
                            if i >= 2:
                                pe.wait_ge(r_dec, 16 * l + i - 1)
                            mm(bank[S_BANK[i % 2]][:, 0:S - j * P],
                               rk_t[rows, (h // 2) * S + j * P:(h // 2) * S + (j + 1) * P],
                               rq_t[rows, (h // 2) * S + j * P:(h // 2 + 1) * S], start=True, stop=True).then_inc(r_mm, 1)
                        if j >= 1:
                            pe.wait_ge(r_dec, 16 * l + i)
                            if j == 1 and h >= 1:
                                pe.wait_ge(z_sq, e0 + h)
                            ins = mm(bank[6][:, (j - 1) * P:S],
                                     rv_t[:, (j - 1) * S + h * P:(j - 1) * S + (h + 1) * P],
                                     sd[:, (j - 1) * S:j * S - (j - 1) * P], start=j == 1, stop=j == NQ)
                    ins.then_inc(rpv_mm, 1)

                def head_stat(h, first, to):
                    pe.wait_ge(z_sq, e0 + first + h + 1)
                    if first and h:
                        pe.wait_ge(z_norm, e0 + first + h)
                    for t in range(NQ):
                        ins = mm(bank[to][:, 4 * h + t:4 * h + t + 1], zsq[h % 2][:, t * P:(t + 1) * P], one,
                                 start=True, stop=True)
                    ins.then_inc(z_mm, 1)

                def head_spread(h, first, banks):
                    pe.wait_ge(h_d, e0 + first + h + 1)
                    if h >= 2 and not first:
                        pe.wait_ge(z_norm, e0 + first + h - 1)
                    mm(bank[banks[h % 2]][:, :], ones, diag, start=True, stop=True).then_inc(h_bc, 1)

                for c in range(24):
                    if c < 2:
                        first_two(L, q, c)
                    else:
                        chunk(L + c // 4, c % 4, u_hi, u_lo)
                    p = c - 1
                    if l == 0 and c == 2:
                        pe.wait_ge(j_diag_set, 1)
                        pe.wait_ge(rstd_set, q + 1)
                        mm(bank[7][:, :], ones, j_diag, start=True, stop=True).then_inc(j_bc, 1)
                    if l == 0 and p == R_V:
                        pe.wait_ge(j_set, 1)
                    if R_V <= p < R_G:
                        v_transpose(v0, p - R_V, L, p)
                    if R_G <= c < D_Q:
                        if c == R_G:
                            pe.wait_ge(v_set, v0 + 4)
                        if c > R_G:
                            head_stat(c - R_G - 1, 0, 7)
                        retention(c - R_G)
                    if c == D_Q:
                        head_stat(3, 0, 7)
                    if D_Q < c <= D_Q + 4:
                        head_spread(c - D_Q - 1, 0, S_BANK)
                    if D_V <= p:
                        v_transpose(v0, 4 + p - D_V, L, p)
                v_transpose(v0, 7, L, 23)

                s0 = 2 * SCORES1 + 16 * l
                pe.wait_ge(taken, 4 * L + 24 + RING)
                pe.wait_ge(v_set, v0 + 8)
                pe.wait_ge(z_norm, e0 + 4)
                for i in range(16 + LAG + 1):
                    if i < 16:
                        h, t = i // 4, i % 4
                        if i >= 2:
                            pe.wait_ge(s_min, s0 + i - 1)
                        for j in range(2):
                            rows = slice(64 * j, 64 * j + 64)
                            ins = mm(bank[D_BANK[i % 2][j]][:, 0:P * (t + 1)], dq_t[rows, h * S + t * P:h * S + (t + 1) * P],
                                     dk_t[rows, h * S:h * S + P * (t + 1)], start=True, stop=True)
                        ins.then_inc(s_mm, 1)
                    n = i - LAG
                    if 0 <= n < 16:
                        pe.wait_ge(p_norm, s0 + n + 1)
                        if n >= 2:
                            pe.wait_ge(t_set, s0 + n - 1)
                        transposes(t_mm, dp[n % 4][0], n % 4 + 1, T_BANK[n % 2])
                    if n >= 1 and n % 4 == 0:
                        h = n // 4 - 1
                        pe.wait_ge(t_set, s0 + 4 * h + 4)
                        if h >= 1:
                            pe.wait_ge(z_sq, e0 + 4 + h)
                        for j in range(NQ):
                            ins = mm(bank[2][:, j * P:S], dv_t[:, j * S + h * P:j * S + (h + 1) * P],
                                     d_pt[:, j * S + j * P:(j + 1) * S], start=j == 0, stop=j == NQ - 1)
                        ins.then_inc(pv_mm, 1)
                    if n >= 6 and n % 4 == 2:
                        head_stat(n // 4 - 1, 4, 3)
                    if n >= 9 and n % 4 == 1:
                        head_spread(n // 4 - 2, 4, (3, 3))
                first = (o_ready, 2 * PV1 + 8 * l + 8)
                most, last = range(KT - 1), range(KT - 1, KT)
                b4 = L + O2_OUT // 4
                head_spread(2, 4, (3, 3))
                head_stat(3, 4, 3)
                pe.wait_ge(o_ready, 2 * PV1 + 8 * l + 6)
                chunk(b4, 0, h_hi, h_lo, ks=most, last=first)
                head_spread(3, 4, (3, 3))
                chunk(b4, 1, h_hi, h_lo, ks=most)
                chunk(b4, 2, h_hi, h_lo, ks=most)
                chunk(b4, 0, h_hi, h_lo, ks=last, last=first)
                chunk(b4, 1, h_hi, h_lo, ks=last)
                chunk(b4, 2, h_hi, h_lo, ks=last)
                pe.wait_ge(z_norm, e0 + 8)
                chunk(b4, 3, h_hi, h_lo)
                plain(b4 + 1, 4, h_hi, h_lo)
                ffn(L + O2_FFN // 4, 9 + 2 * l, 4 + l, end=l == 1)

            stat(12)

        @block.scalar
        def _(act):
            a = nc.scalar.activation
            chain = Chain(chain_a)

            def round_weights(b4, j, ahead=RING):
                act.wait_ge(raw_in[j], (b4 + (1 + ahead // 4)) * 16)
                if ahead:
                    act.wait_ge(tiles, 4 * b4 + j + 1)
                a(w_hi[:, j, :], raw[:, j, :], ACT.Copy).then_inc(rounded, 1)

            def finish(q, k, gain):
                a(tile(u_hi, k), tile(x, k), ACT.Copy, scale=col(gain)).then_inc(u_rounded, 1)

            def keep_rstd(q):
                act.wait_ge(stat_bc, q + 1)
                a(rstd[:, :], bank[7][:, :], ACT.Copy).then_inc(rstd_set, 1)

            def step(n4, j, more=True):
                if more:
                    round_weights(n4, j)

            def ffn(b4, q, f, gain, more=True, joint=False):
                for g, (f0, fn) in enumerate(F_GROUPS):
                    def pair(b4, f_at, h_at, jj):
                        step(b4, 2 * jj)
                        act.wait_ge(taken, 4 * b4 + 2 * jj + RING + 1)
                        a(tanh_t, gate_t, ACT.Tanh, scale=0.5).then_inc(f_tanh, 1)
                        step(b4, 2 * jj + 1)
                        act.wait_ge(f_prod, F_TILES * f + f_at + 1)
                        a(tile(h_hi, h_at), gate_t, ACT.Copy).then_inc(f_rounded, 1)

                    if g == 0:
                        step(b4, 0)
                        step(b4, 1)
                        if q:
                            keep_rstd(q)
                        act.wait_ge(taken, 4 * b4 + RING + 1)
                        a(tanh_t, gate_t, ACT.Tanh, scale=0.5).then_inc(f_tanh, 1)
                        act.wait_ge(f_prod, F_TILES * f + 1)
                        a(tile(h_hi, 0), gate_t, ACT.Copy).then_inc(f_rounded, 1)
                        pair(b4, 1, 1, 1)
                    with act.Fori(1 if g == 0 else 0, fn // 2) as i:
                        for jj in range(2):
                            pair(b4 + i, i * 2 + (f0 + jj), i * 2 + jj, jj)
                    b4 = b4 + fn // 2
                    end = g == len(F_GROUPS) - 1

                    def down(b4, k, j, more):
                        step(b4, j, more)
                        if end:
                            act.wait_ge(taken, 4 * b4 + j + RING + 1)
                            finish(q + 1, k, gain + k)
                        if end and joint:
                            a(tile(j_sq, k), tile(x, k), ACT.Square, scale=col(G_FINAL + k)).then_inc(j_squared, 1)
                    if end and not more:
                        for k in range(KT):
                            step(b4, k, k < 4)
                            act.wait_ge(taken, 4 * b4 + k + RING + 1)
                            a(tile(z_in, k), tile(x, k), ACT.Copy, scale=col(gain + k)).then_inc(z_rounded, 1)
                        continue
                    with act.Fori(0, 2) as i:
                        for j in range(4):
                            down(b4 + i, i * 4 + j, j, True)
                    b4 = b4 + 2

            def plain_finish(b4, q, gain):
                with act.Fori(0, 2) as i:
                    for j in range(4):
                        step(b4 + i, j)
                        act.wait_ge(taken, 4 * (b4 + i) + j + RING + 1)
                        finish(q, i * 4 + j, i * 4 + (gain + j))

            def v_store(i, c, dst, blocks=NQ):
                act.wait_ge(v_tr, i + 1)
                a(dst, bank[T_BANK[c % 2]][:, 0:blocks * P].rearrange("p (j n) -> p j n", n=P), ACT.Copy)\
                    .then_inc(v_set, 1)

            act.dma_start(const[:, 0:2 * P], A["consts"][:, 0:2 * P]).then_inc(par_in_set, 16)
            act.wait_ge(pool_set, 1)
            rows = [("ffn1_norm", 0, 0), ("final_norm", 0, 16), ("mix_norm", 0, 24), ("xa_norm", 0, 40),
                    ("mem_norm", 0, 56), ("ffn2_norm", 0, 72), ("attn_norm_2", 0, 88), ("final_norm_2", 0, 104),
                    ("ffn_norm_2", 0, 112), ("conf_dw", 1, 0), ("conf_dw_b", 1, 124), ("conf_ln_g", 2, 0),
                    ("conf_ln_b", 2, 4), ("sc_dw", 2, 8), ("ret_norm_2", 2, 20), ("diff_norm_2", 2, 22)]
            for name, t, r in rows:
                src = A[name]
                if len(src.shape) == 3:
                    src = src.rearrange("l j (i c) -> (l j i) c", c=P)
                elif len(src.shape) == 2:
                    src = src.rearrange("l (i c) -> (l i) c", c=P)
                else:
                    src = src.rearrange("(i c) -> i c", c=P)
                act.dma_start(par_in[r:r + src.shape[0], t * P:(t + 1) * P], src).then_inc(par_in_set, 16)
            act.dma_start(pos_i, A["positions"].to_broadcast([P, S])).then_inc(setup_in, 16)
            for i, name in enumerate(("lambda_q1_2", "lambda_k1_2", "lambda_q2_2", "lambda_k2_2")):
                act.dma_start(lam_in[:, i * P:(i + 1) * P],
                               A[name].rearrange("(o l) d -> o (l d)", o=1).to_broadcast([P, P])).then_inc(setup_in, 16)
            act.dma_start(const[:, 2 * P:C_N], A["consts"][:, 2 * P:C_N]).then_inc(setup_in, 16)
            for t in range(NQ):
                act.wait_ge(x_landed[t], 16)
                a(x_sq[:, t * D:(t + 1) * D], x_in[:, t * D:(t + 1) * D], ACT.Square, accum_out=var[:, t:t + 1]).then_inc(x_squared, 1)
            for k in range(KT):
                act.wait_ge(x_tr, k + 1)
                a(tile(x, k), bank[4 + k % 4][:, :], ACT.Copy).then_inc(x_set, 1)
                if k == 0:
                    act.wait_ge(par_set, 1)
                act.wait_ge(x_set, k + 1)
                finish(0, k, G_FFN1 + k)
                if k % 2:
                    round_weights(0, k // 2, 0)
            keep_rstd(0)
            act.wait_ge(tab_set, 1)
            act.wait_ge(pool_set, 3)
            a(sin_t[:, :], cos_t[:, :], ACT.Sin, scale=0.5)
            a(cos_half, cos_t[:, :], ACT.Sin, scale=0.5, bias=half_pi).then_inc(tab_sin, 1)
            act.wait_ge(par_set, 2)
            a(lam_s, lam_s, ACT.Exp).then_inc(tab_sin, 1)

            for l in range(2):
                L = l * (N_L1 // 4)
                ffn(L, 4 * l, 2 * l, G_MIX + 8 * l)

                b4, q, r0 = L + O_MIX // 4, 4 * l + 1, ROPES * l
                N0 = 4 * b4
                for c in range(28):
                    step(b4 + c // 4, c % 4)
                    if c == 1:
                        keep_rstd(q)
                    p = c - 1
                    if p == 7:
                        for i in range(12):
                            act.wait_ge(idx_mm, 12 * l + i + 1)
                            if i >= 2:
                                act.wait_ge(idx_add, 12 * l + i - 1)
                            n = P * (i // 4 + 2)
                            a(relu_t[i % 2][:, 0:n], bank[S_BANK[i % 2]][:, 0:n], ACT.Relu).then_inc(idx_relu, 1)
                    if c in (C_AG, C_AG + 1):
                        act.wait_ge(taken, N0 + c + RING + 1)
                        a(y_buf[c % 2], y_buf[c % 2], ACT.Tanh, scale=0.5).then_inc(a_tanh, 1)
                    if c in (C_BH + 3, C_BH + 5):
                        i = (c - C_BH - 3) // 2
                        act.wait_ge(y_made, 2 * l + i + 1)
                        a(tile(h_hi, 2 + i), yb_t, ACT.Copy).then_inc(y_rounded, 1)
                    if p >= C_V:
                        i = p - C_V
                        v_store(12 * l + i, p, v_t.rearrange("p (j n) -> p j n", j=NQ)[:, :, i * P:(i + 1) * P])
                v_store(12 * l + 3, 27, v_t.rearrange("p (j n) -> p j n", j=NQ)[:, :, 3 * P:4 * P])

                s0 = SCORES1 * l
                for i in range(32 + LAG + 2):
                    if i < 32:
                        t = i % 4
                        act.wait_ge(s_min, s0 + i + 1)
                        if i >= 4:
                            act.wait_ge(t_mm, s0 + i - 3)
                        a(prob[i % 4][:, 0:P * (t + 1)], sp[i % 4][:, 0:P * (t + 1)], ACT.Exp, bias=neg_max[i % 4],
                          scale=-1.0, accum_out=row_sum[i % 4]).then_inc(p_exp, 1)
                    n = i - LAG
                    if 0 <= n < 32:
                        h, t = n // 4, n % 4
                        act.wait_ge(t_mm, s0 + n + 1)
                        if h >= 2 and t == 0:
                            act.wait_ge(pv_mm, PV1 * l + h - 1)
                        a(pt[h % 2].rearrange("p (j n) -> p j n", j=NQ)[:, 0:t + 1, t * P:(t + 1) * P],
                          bank[T_BANK[n % 2]][:, 0:(t + 1) * P].rearrange("p (j n) -> p j n", n=P), ACT.Copy)\
                            .then_inc(t_set, 1)
                    if n >= 2 and (n - 2) % 8 == 7:
                        g = (n - 2) // 8
                        act.wait_ge(pv_mm, PV1 * l + 2 * g + 2)
                        a(tile(h_hi, 4 + g), bank[g % 2][:, :], ACT.Copy).then_inc(o_rounded, 1)
                    if i == 27:
                        act.wait_ge(ln_y, 2 * l + 2)
                        for c in range(2):
                            a(conv[c], conv[c], ACT.Identity, scale=col(G_LNG + 2 * l + c), bias=col(G_LNB + 2 * l + c))\
                                .then_inc(ln_z, 1)
                        for c in range(2):
                            act.wait_ge(ln_z, 2 * l + c + 1)
                            a(y_buf[c], conv[c], ACT.Tanh, scale=0.5).then_inc(ln_t, 1)
                    if i == 30:
                        for c in range(2):
                            act.wait_ge(a_glu, 4 * l + 2 + c + 1)
                            a(tile(h_hi, c), conv[c], ACT.Copy, scale=0.5).then_inc(y_rounded, 1)

                plain_finish(L + O_OUT // 4, 4 * l + 2, G_XA + 8 * l)

                b4, q = L + O_WQ // 4, 4 * l + 2
                for c in range(8):
                    step(b4 + c // 4, c % 4)
                    if c == 0:
                        act.wait_ge(mem_landed, 16 * (l + 1))
                        for t in range(2):
                            a(ptx[t], mem_in[:, t * D:(t + 1) * D], ACT.Square, accum_out=mem_var[:, t:t + 1])\
                                .then_inc(mem_sq, 1)
                    if c == 1:
                        keep_rstd(q)
                    if 3 <= c < 7:
                        r = c - 3
                        act.wait_ge(mem_tr, 4 * l + r + 1)
                        for k in range(2 * r, 2 * r + 2):
                            a(h_hi[:, k * MEM:(k + 1) * MEM], bank[S_BANK[r % 2]][:, (k % 2) * MEM:(k % 2 + 1) * MEM],
                              ACT.Copy, scale=col(G_MEM + 8 * l + k)).then_inc(gm_rounded, 1)
                with act.Fori(0, 2) as i:
                    for j in range(4):
                        step(L + O_KV // 4 + i, j)
                b4 = L + O_KV // 4 + 2
                for c in range(8):
                    step(b4 + c // 4, c % 4)
                    if c >= 1:
                        i = c - 1
                        v_store(12 * l + 4 + i, i, vm.rearrange("p (j n) -> p j n", j=2)[:, :, i * P:(i + 1) * P], 2)
                v_store(12 * l + 11, 7, vm.rearrange("p (j n) -> p j n", j=2)[:, :, 7 * P:8 * P], 2)

                s0 = SCORES1 * l + 32
                for i in range(16 + LAG + 2):
                    if i < 16:
                        act.wait_ge(s_min, s0 + i + 1)
                        if i >= 4:
                            act.wait_ge(t_mm, s0 + i - 3)
                        a(px[i % 4], bank[S_BANK[i % 3]][:, 0:MEM], ACT.Exp, bias=neg_max[i % 4], scale=-1.0,
                          accum_out=row_sum[i % 4]).then_inc(p_exp, 1)
                    n = i - LAG
                    if 0 <= n < 16:
                        h, t = n // 4, n % 4
                        act.wait_ge(t_mm, s0 + n + 1)
                        if h >= 2 and t == 0:
                            act.wait_ge(pv_mm, PV1 * l + 8 + h - 1)
                        a(ptx[h % 2].rearrange("p (j n) -> p j n", j=2)[:, :, t * P:(t + 1) * P],
                          bank[T_BANK[n % 2]][:, 0:2 * P].rearrange("p (j n) -> p j n", n=P), ACT.Copy).then_inc(t_set, 1)
                    if n >= 2 and (n - 2) % 4 == 3:
                        h = (n - 2) // 4
                        act.wait_ge(pv_mm, PV1 * l + 8 + h + 1)
                        for d in range(2):
                            a(tile(h_hi, 2 * h + d), bank[(2 * h + d + 1) % 3][:, :], ACT.Copy).then_inc(o_rounded, 1)
                plain_finish(L + O_WO // 4, 4 * l + 3, G_FFN2 + 8 * l)
                ffn(L + O_FFN2 // 4, 4 * l + 3, 2 * l + 1, G_JOINT if l else G_FFN1 + 8, joint=l == 1)

            for l in range(2):
                L = 2 * (N_L1 // 4) + l * (N_L2 // 4)
                q, v0, e0 = 8 + 2 * l, 24 + 8 * l, 8 * l

                def decay(h):
                    if h >= 2:
                        act.wait_ge(r_dec, 16 * l + 4 * (h - 2) + 4)
                    a(table[h % 2], const[:, C_DEC:C_DEC + S], ACT.Exp, scale=LOG_GAMMA[h]).then_inc(dec_set, 1)

                def head_square(h, first, done, to):
                    act.wait_ge(done, (4 * l if done is rpv_mm else 2 * PV1 + 4 * l) + h + 1)
                    if h >= 2:
                        act.wait_ge(z_mm, e0 + first + h - 1)
                    a(tile(z_t, h), bank[to][:, :], ACT.Copy)
                    a(zsq[h % 2], bank[to][:, :], ACT.Square).then_inc(z_sq, 1)

                def head_round(h, first):
                    act.wait_ge(z_norm, e0 + first + h + 1)
                    a(tile(h_hi, first + h), tile(z_t, h), ACT.Copy).then_inc(o_rounded, 1)

                for c in range(24):
                    step(L + c // 4, c % 4)
                    if c == 1:
                        keep_rstd(q)
                    if l == 0 and c == 2:
                        act.wait_ge(j_bc, 1)
                        a(j_scale, bank[7][:, :], ACT.Copy).then_inc(j_set, 1)
                    if c == 2:
                        decay(0)
                        decay(1)
                    p = c - 1
                    if R_V <= p < R_G:
                        i = p - R_V
                        v_store(v0 + i, p, rv_t.rearrange("p (j n) -> p j n", j=NQ)[:, :, i * P:(i + 1) * P])
                    if R_G <= c < D_Q:
                        h = c - R_G
                        act.wait_ge(taken, 4 * L + c + RING + 1)
                        a(y_buf[c % 2], tile(gate_s, h), ACT.Tanh, scale=0.5).then_inc(g_tanh, 1)
                        head_square(h, 0, rpv_mm, 6)
                        if h < 2:
                            decay(h + 2)
                    if D_Q + 2 <= c < D_Q + 6:
                        head_round(c - D_Q - 2, 0)
                    if D_V <= p:
                        i = p - D_V
                        v_store(v0 + 4 + i, p, dv_t.rearrange("p (j n) -> p j n", j=NQ)[:, :, i * P:(i + 1) * P])
                v_store(v0 + 7, 23, dv_t.rearrange("p (j n) -> p j n", j=NQ)[:, :, 3 * P:4 * P])

                s0 = 2 * SCORES1 + 16 * l
                for i in range(16 + LAG + 2):
                    if i < 16:
                        t, b = i % 4, i % 4
                        act.wait_ge(s_min, s0 + i + 1)
                        if i >= 4:
                            act.wait_ge(t_mm, s0 + i - 3)
                        for j in range(2):
                            ins = a(dp[b][j][:, 0:P * (t + 1)], dsp[b][j][:, 0:P * (t + 1)], ACT.Exp, bias=neg_max[2 * b + j],
                                    scale=-1.0, accum_out=row_sum[2 * b + j])
                        ins.then_inc(p_exp, 1)
                    n = i - LAG
                    if 0 <= n < 16:
                        h, t = n // 4, n % 4
                        act.wait_ge(t_mm, s0 + n + 1)
                        if h >= 1 and t == 0:
                            act.wait_ge(pv_mm, 2 * PV1 + 4 * l + h)
                        a(d_pt.rearrange("p (j n) -> p j n", j=NQ)[:, 0:t + 1, t * P:(t + 1) * P],
                          bank[T_BANK[n % 2]][:, 0:(t + 1) * P].rearrange("p (j n) -> p j n", n=P), ACT.Copy)\
                            .then_inc(t_set, 1)
                    if n >= 1 and n % 4 == 0:
                        head_square(n // 4 - 1, 4, pv_mm, 2)
                    if n >= 10 and n % 4 == 2:
                        head_round(n // 4 - 2, 4)
                head_round(2, 4)
                head_round(3, 4)
                plain_finish(L + O2_OUT // 4, 9 + 2 * l, G_FFNN2 + 8 * l)
                ffn(L + O2_FFN // 4, 9 + 2 * l, 4 + l, G_ATTN2 + 8 * (l + 1), more=l == 0)
            act.wait_ge(stat_inv, 13)
            act.wait_ge(x_set, 24)
            for t in range(2):
                yt = y_out[:, t * D:(t + 1) * D]
                a(yt, yt, ACT.Copy, scale=inv[:, t:t + 1]).then_inc(y_scaled[t], 1)

        @block.vector
        def _(v):
            tt, ts, stt = nc.vector.tensor_tensor, nc.vector.tensor_scalar, nc.vector.scalar_tensor_tensor
            chain = Chain(chain_v)

            def rest_of_weights(b4, j, ahead=RING):
                v.wait_ge(rounded, 4 * b4 + j + ahead + 1)
                tt(w_lo[:, j, :], raw[:, j, :], f32(w_hi[:, j, :]), ALU.subtract).then_inc(split, 1)

            def rest(dst_hi, dst_lo, src, scale, e):
                stt(dst_lo, src, scale, f32(dst_hi), ALU.mult, ALU.subtract).then_inc(e, 1)

            def scaled(dst, b4, c, factor=1.0, rows=P):
                v.wait_ge(tiles, 4 * b4 + c + 1)
                stt(dst[0:rows, :], bank[c % 4][0:rows, :], factor, rstd[0:rows, :], ALU.mult, ALU.mult).then_inc(taken, 1)

            def make_diag(values, to, e):
                for t in range(NQ):
                    ins = ts(to[:, t * P:(t + 1) * P], ident, values[:, t:t + 1], None, ALU.mult)
                ins.then_inc(e, 1)

            def norm_scale(q):
                v.wait_ge(stat_mm, q)
                ins = ts(var, bank[7][:, 0:NQ], 1.0 / D, EPS, ALU.mult, ALU.add)
                if q == 8:
                    chain.done(v, ins)
                    chain.done(v, nc.vector.reciprocal(j_var, var))
                    chain.done(v, stt(j_var, bank[7][:, NQ:2 * NQ], 1.0 / D, j_var, ALU.mult, ALU.mult))
                    ins = ts(j_var, j_var, EPS, None, ALU.add)
                ins.then_inc(stat_var, 1)
                v.wait_ge(stat_inv, q + 1)
                if q == 8:
                    chain.done(v, tt(j_inv, j_inv, inv, ALU.mult))
                make_diag(j_inv if q == 8 else inv, diag, stat_diag)
                if q == 8:
                    make_diag(inv, j_diag, j_diag_set)

            def finish(q, k, gain):
                v.wait_ge(u_rounded, k + 8 * q + 1)
                rest(tile(u_hi, k), tile(u_lo, k), tile(x, k), col(gain), u_ready)

            def residual(b4, j, k, factor):
                v.wait_ge(tiles, 4 * b4 + j + 1)
                stt(tile(x, k), bank[j][:, :], factor, tile(x, k), ALU.mult, ALU.add).then_inc(taken, 1)

            def result(k):
                v.wait_ge(x_tr, 8 + k + 1)
                nc.vector.tensor_copy(y_out.rearrange("p (t d) -> p t d", t=NQ)[:, :, k * P:(k + 1) * P],
                                      bank[4 + k % 2][:, :].rearrange("p (t n) -> p t n", n=P)).then_inc(x_set, 1)

            def ffn(b4, q, f, gain, factor, more=True):
                for g, (f0, fn) in enumerate(F_GROUPS):
                    def gate(b4, j, f_at):
                        if f_at is not None:
                            v.wait_ge(f_ready, F_TILES * f + (f_at - 1) + 1)
                        v.wait_ge(tiles, 4 * b4 + j + 1)
                        tt(gate_t, bank[j][:, :], rstd[:, :], ALU.mult).then_inc(taken, 1)

                    def up(b4, j, f_at, h_at):
                        v.wait_ge(tiles, 4 * b4 + j + 1)
                        tt(up_t, bank[j][:, :], rstd[:, :], ALU.mult).then_inc(taken, 1)
                        v.wait_ge(f_tanh, F_TILES * f + f_at + 1)
                        chain.done(v, stt(gate_t, tanh_t, 1.0, gate_t, ALU.add, ALU.mult))
                        tt(gate_t, gate_t, up_t, ALU.mult).then_inc(f_prod, 1)
                        rest_of_weights(b4, j)
                        v.wait_ge(f_rounded, F_TILES * f + f_at + 1)
                        rest(tile(h_hi, h_at), tile(h_lo, h_at), gate_t, 1.0, f_ready)

                    if g == 0:
                        rest_of_weights(b4, 0)
                        if q:
                            norm_scale(q)
                        v.wait_ge(rstd_set, q + 1)
                        gate(b4, 0, None)
                        up(b4, 1, 0, 0)
                        rest_of_weights(b4, 2)
                        gate(b4, 2, 1)
                        up(b4, 3, 1, 1)
                    with chain.loop(v, 1 if g == 0 else 0, fn // 2, 2) as i:
                        for jj in range(2):
                            rest_of_weights(b4 + i, 2 * jj)
                            gate(b4 + i, 2 * jj, i * 2 + (f0 + jj))
                            up(b4 + i, 2 * jj + 1, i * 2 + (f0 + jj), i * 2 + jj)
                    b4 = b4 + fn // 2
                    end = g == len(F_GROUPS) - 1
                    if end and not more:
                        for k in range(KT):
                            residual(b4 + k // 4, k % 4, k, factor)
                            if k < 4:
                                rest_of_weights(b4, k)
                            if k >= 3:
                                result(k - 3)
                        for k in range(5, KT):
                            result(k)
                        continue
                    with v.Fori(0, 2) as i:
                        for j in range(4):
                            residual(b4 + i, j, i * 4 + j, factor)
                            rest_of_weights(b4 + i, j)
                            if end:
                                finish(q + 1, i * 4 + j, i * 4 + (gain + j))
                    b4 = b4 + 2

            def plain_finish(b4, q, gain):
                with v.Fori(0, 2) as i:
                    for j in range(4):
                        residual(b4 + i, j, i * 4 + j, 1.0)
                        rest_of_weights(b4 + i, j)
                        finish(q, i * 4 + j, i * 4 + (gain + j))

            def normalise(i, p, s_at):
                v.wait_ge(p_exp, s_at + 1)
                chain.done(v, nc.vector.reciprocal(row_inv[i % 4], row_sum[i % 4]))
                ts(p, p, row_inv[i % 4], None, ALU.mult).then_inc(p_norm, 1)

            v.sem_inc(split, RING)
            v.sem_inc(taken, RING)
            v.wait_ge(x_squared, NQ)
            ts(var, var, 1.0 / D, EPS, ALU.mult, ALU.add).then_inc(stat_var, 1)
            v.wait_ge(par_tr, 1)
            chain.done(v, nc.vector.tensor_copy(par[:, :], bank[3][:, 0:G_N]))
            ts(par[:, G_DW:G_DWB], par[:, G_DW:G_DWB], 0.5, None, ALU.mult)
            for l in range(2):
                ts(par[:, G_DIF + l:G_DIF + l + 1], par[:, G_DIF + l:G_DIF + l + 1], 1.0 - LAM_INIT[l], None, ALU.mult)
            ins = tt(par[:, G_JOINT:G_JOINT + KT], par[:, G_FINAL:G_FINAL + KT], par[:, G_ATTN2:G_ATTN2 + KT], ALU.mult)
            ins.then_inc(par_set, 1)
            v.wait_ge(par_set, 1)
            for k in range(KT):
                if k == 2:
                    v.wait_ge(stat_inv, 1)
                    make_diag(inv, diag, stat_diag)
                finish(0, k, G_FFN1 + k)
                if k % 2:
                    rest_of_weights(0, k // 2, 0)
            v.wait_ge(setup_in, 16 * 6)
            chain.done(v, nc.vector.tensor_copy(ang, pos_i))
            chain.done(v, ts(ang, ang, const[:, C_INV:C_INV + 1], None, ALU.mult))
            chain.done(v, ts(turns, ang, 1.0 / (2 * math.pi), ROUND, ALU.mult, ALU.add))
            chain.done(v, ts(turns, turns, ROUND, None, ALU.subtract))
            chain.done(v, stt(ang, turns, -TWO_PI[0], ang, ALU.mult, ALU.add))
            chain.done(v, stt(ang, turns, -TWO_PI[1], ang, ALU.mult, ALU.add))
            stt(cos_t[:, :], turns, -TWO_PI[2], ang, ALU.mult, ALU.add).then_inc(tab_set, 1)
            v.wait_ge(tab_sin, 1)
            chain.done(v, stt(cos_t[:, :], sin_t[:, :], -2.0, sin_t[:, :], ALU.mult, ALU.mult))
            chain.done(v, ts(cos_t[:, :], cos_t[:, :], 1.0, None, ALU.add))
            stt(sin_t[:, :], sin_t[:, :], 2.0, cos_half, ALU.mult, ALU.mult).then_inc(tab_set, 1)
            for i in range(2):
                pr = lam_in[:, 2 * i * P:(2 * i + 1) * P]
                chain.done(v, tt(pr, pr, lam_in[:, (2 * i + 1) * P:(2 * i + 2) * P], ALU.mult))
                ins = nc.vector.tensor_reduce(lam_s[:, 2 * i:2 * i + 2], pr.rearrange("p (l d) -> p l d", l=2), AX_X, ALU.add)
                if i == 0:
                    chain.done(v, ins)
            ins.then_inc(par_set, 1)
            v.wait_ge(tab_sin, 2)
            chain.done(v, tt(neg_lam, lam_s[:, 2:4], lam_s[:, 0:2], ALU.subtract))
            for l in range(2):
                chain.done(v, ts(neg_lam[:, l:l + 1], neg_lam[:, l:l + 1], -LAM_INIT[l], None, ALU.add))

            for l in range(2):
                L = l * (N_L1 // 4)
                ffn(L, 4 * l, 2 * l, G_MIX + 8 * l, 0.25)

                b4, q, r0 = L + O_MIX // 4, 4 * l + 1, ROPES * l
                N0 = 4 * b4

                def combine(r, p, dst, rows=P, between=None):
                    v.wait_ge(rot_mm, r0 + r + 1)
                    chain.done(v, tt(rope_t[0:rows, :], bank[6][0:rows, :], sin_t[0:rows, :], ALU.mult))
                    if between:
                        between()
                    v.wait_ge(cos_mul, r0 + r + 1)
                    tt(dst[0:rows, :], rope_t[0:rows, :], y_buf[p % 2][0:rows, :], ALU.add).then_inc(roped, 1)
                    v.wait_ge(roped, r0 + r + 1)

                def top_rounds(first, last):
                    for n in range(first, min(last, 3 * ROUNDS)):
                        w = work[1 + n // ROUNDS]
                        chain.done(v, nc.vector.max(max8, w))
                        chain.done(v, nc.vector.match_replace(w, max8, w, TAKEN))

                EARLY = 13

                def taps(first, last):
                    for j in range(first, min(last, TAPS)):
                        w, src = col(G_DW + 2 * (TAPS * l + j)), a_pad[0][:, j:j + S]
                        if j == 0:
                            ins = ts(conv[0], src, w, col(G_DWB + 2 * l), ALU.mult, ALU.add)
                        else:
                            ins = stt(conv[0], src, w, conv[0], ALU.mult, ALU.add)
                        if j < TAPS - 1:
                            chain.done(v, ins)
                        else:
                            ins.then_inc(conv0, 1)

                def take(c):
                    if c == 0:
                        scaled(y_buf[0], b4, c, rows=64)
                    elif c == 1:
                        scaled(w_idx_t, b4, c, 1.0 / 16, rows=4)
                    elif c < 6:
                        scaled(y_buf[c % 2], b4, c, rows=64)
                    elif c < C_AG:
                        if c == C_AV:
                            v.wait_ge(pads, l + 1)
                        scaled(a_pad[c % 2][:, PAD:], b4, c)
                    elif c < C_BG:
                        scaled(y_buf[c % 2], b4, c)
                    elif c < C_CG:
                        scaled(b_gate[c % 2], b4, c)
                    elif c < C_BH:
                        if c == C_CG:
                            for i in range(2):
                                chain.done(v, nc.vector.memset(c_pad[i][:, 0:SC_PAD], 0.0))
                        scaled(c_pad[c % 2][:, SC_PAD:], b4, c)
                    elif c < C_Q:
                        scaled(y_buf[c % 2], b4, c)
                        v.wait_ge(taken, N0 + c + RING + 1)
                        cp = c_pad[c % 2][:, SC_PAD:]
                        chain.done(v, tt(cp, cp, y_buf[c % 2], ALU.mult))
                    elif c < C_K:
                        scaled(y_buf[c % 2], b4, c, -0.125)
                    else:
                        if c >= C_V + 2:
                            v.wait_ge(v_tr, 12 * l + c - 2 - C_V + 1)
                        scaled(y_buf[c % 2], b4, c)

                def rounds():
                    n = p - 8
                    top_rounds(n * 48 // 19, (n + 1) * 48 // 19)

                for c in range(28):
                    if c == 0:
                        rest_of_weights(b4, 0)
                        norm_scale(q)
                        continue
                    if c == 1:
                        v.wait_ge(rstd_set, q + 1)
                        take(0)
                    take(c)
                    rest_of_weights(b4 + c // 4, c % 4)
                    p = c - 1
                    if p == 0:
                        combine(0, 0, k_idx, 64)
                    if p == 1:
                        v.wait_ge(wi_tr, l + 1)
                        nc.vector.tensor_copy(w_idx, bank[7][:, 0:16]).then_inc(wi_set, 1)
                    if 2 <= p < 6:
                        combine(p - 1, p, q_idx[p - 2], 64)
                    if p == 7:
                        v.wait_ge(wi_set, l + 1)
                        for i in range(12):
                            t, h = 1 + i // 4, i % 4
                            v.wait_ge(idx_relu, 12 * l + i + 1)
                            if h:
                                v.wait_ge(idx_add, 12 * l + i)
                            n = P * (t + 1)
                            base = work[t] if h else const[:, C_NEG + S - n:C_NEG + S]
                            stt(work[t], relu_t[i % 2][:, 0:n], w_idx[:, 4 * t + h:4 * t + h + 1], base, ALU.mult, ALU.add)\
                                .then_inc(idx_add, 1)
                        v.wait_ge(idx_add, 12 * l + 12)
                    if p in (C_AG, C_AG + 1):
                        i = p - C_AG
                        v.wait_ge(a_tanh, 2 * l + i + 1)
                        ap = a_pad[i][:, PAD:]
                        stt(ap, y_buf[p % 2], 1.0, ap, ALU.add, ALU.mult).then_inc(a_glu, 1)
                        v.wait_ge(a_glu, 4 * l + i + 1)
                    if p in (C_BH + 1, C_BH + 3):
                        i = (p - C_BH - 1) // 2
                        if i:
                            v.wait_ge(y_ready, 4 * l + 1)
                        g = G_SC + 2 * SC_TAPS * l + i
                        chain.done(v, ts(yb_t, c_pad[i][:, 0:S], col(g), None, ALU.mult))
                        for j in (1, 2):
                            chain.done(v, stt(yb_t, c_pad[i][:, j:j + S], col(g + 2 * j), yb_t, ALU.mult, ALU.add))
                        tt(yb_t, yb_t, b_gate[i], ALU.mult).then_inc(y_made, 1)
                    if p in (C_BH + 2, C_BH + 4):
                        i = (p - C_BH - 2) // 2
                        v.wait_ge(y_rounded, 4 * l + i + 1)
                        rest(tile(h_hi, 2 + i), tile(h_lo, 2 + i), yb_t, 1.0, y_ready)
                    if C_Q <= p < C_K:
                        combine(5 + p - C_Q, p, tile(q_t, p - C_Q), between=rounds)
                    if C_K <= p < C_V:
                        combine(5 + p - C_Q, p, tile(k_t, p - C_K), between=rounds)
                    if p >= 8 and not C_Q <= p < C_V:
                        rounds()
                    if p >= C_AG + 1:
                        n = p - C_AG - 1
                        taps(n * EARLY // 18, (n + 1) * EARLY // 18)
                for t in range(1, NQ):
                    ins = ts(work[t], work[t], TAKEN / 2, BIG, ALU.is_gt, ALU.mult)
                ins.then_inc(masked, 1)
                v.wait_ge(masked, l + 1)

                s0 = SCORES1 * l
                for i in range(32 + LAG + 2):
                    if i < 32:
                        t = i % 4
                        n = P * (t + 1)
                        v.wait_ge(s_mm, s0 + i + 1)
                        mask = work[t] if t else const[:, C_BIG:C_BIG + P]
                        nc.vector.tensor_tensor_reduce(sp[i % 4][:, 0:n], bank[S_BANK[i % 3]][:, 0:n], mask, 1.0, BIG,
                                                       ALU.add, ALU.min, neg_max[i % 4]).then_inc(s_min, 1)
                    if 1 <= i < 33:
                        normalise(i - 1, prob[(i - 1) % 4][:, 0:P * ((i - 1) % 4 + 1)], s0 + i - 1)
                    taps(EARLY + 2 * i, EARLY + 2 * i + 2)
                    n = i - LAG - 2
                    if n >= 0 and n % 8 == 7:
                        g = n // 8
                        v.wait_ge(o_rounded, PV1 * l + g + 1)
                        rest(tile(h_hi, 4 + g), tile(h_lo, 4 + g), bank[g % 2][:, :], 1.0, o_ready)
                    if i == 21:
                        v.wait_ge(ln_mean, l + 1)
                        for c in range(2):
                            stt(conv[c], bank[2][:, :], -1.0 / 256, conv[c], ALU.mult, ALU.add).then_inc(ln_cent, 1)
                    if i == 24:
                        v.wait_ge(ln_mm, l + 1)
                        ts(ln_var, bank[2][:, 0:NQ], 1.0 / 256, LN_EPS, ALU.mult, ALU.add).then_inc(ln_v, 1)
                    if i == 25:
                        v.wait_ge(ln_i, l + 1)
                        make_diag(ln_inv, rope_t, ln_d)
                    if i == 27:
                        v.wait_ge(ln_bc, l + 1)
                        for c in range(2):
                            tt(conv[c], bank[2][:, :], conv[c], ALU.mult).then_inc(ln_y, 1)
                    if i == 29:
                        for c in range(2):
                            v.wait_ge(ln_t, 2 * l + c + 1)
                            stt(conv[c], y_buf[c], 1.0, conv[c], ALU.add, ALU.mult).then_inc(a_glu, 1)
                    if i == 31:
                        for c in range(2):
                            v.wait_ge(y_rounded, 4 * l + 2 + c + 1)
                            rest(tile(h_hi, c), tile(h_lo, c), conv[c], 0.5, y_ready)

                plain_finish(L + O_OUT // 4, 4 * l + 2, G_XA + 8 * l)

                b4, q = L + O_WQ // 4, 4 * l + 2
                for c in range(8):
                    rest_of_weights(b4 + c // 4, c % 4)
                    if c == 0:
                        norm_scale(q)
                        continue
                    if c == 1:
                        v.wait_ge(rstd_set, q + 1)
                        scaled(tile(qx, 0), b4, 0, -1.0 / 16)
                    scaled(tile(qx, c), b4, c, -1.0 / 16)
                    if c == 1:
                        v.wait_ge(mem_i, l + 1)
                        for t in range(2):
                            mt = mem_in[:, t * D:(t + 1) * D]
                            ins = ts(mt, mt, mem_inv[:, t:t + 1], None, ALU.mult)
                        ins.then_inc(mem_n, 1)
                    if 3 <= c < 7:
                        r = c - 3
                        for k in range(2 * r, 2 * r + 2):
                            v.wait_ge(gm_rounded, 8 * l + 2 * r + 2)
                            ks = slice(k * MEM, (k + 1) * MEM)
                            rest(h_hi[:, ks], h_lo[:, ks], bank[S_BANK[r % 2]][:, (k % 2) * MEM:(k % 2 + 1) * MEM],
                                 col(G_MEM + 8 * l + k), gm_ready)
                with v.Fori(0, 2) as i:
                    for j in range(4):
                        rest_of_weights(L + O_KV // 4 + i, j)
                        v.wait_ge(tiles, 4 * (L + O_KV // 4 + i) + j + 1)
                        nc.vector.tensor_copy(km[:, bass.ds((i * 4 + j) * MEM, MEM)], bank[j][:, 0:MEM]).then_inc(taken, 1)
                b4 = L + O_KV // 4 + 2
                for c in range(8):
                    rest_of_weights(b4 + c // 4, c % 4)
                    v.wait_ge(tiles, 4 * b4 + c + 1)
                    if c >= 2:
                        v.wait_ge(v_tr, 12 * l + 4 + c - 1)
                    nc.vector.tensor_copy(vx_t[c % 2], bank[c % 4][:, 0:MEM]).then_inc(taken, 1)

                s0 = SCORES1 * l + 32
                for i in range(16 + LAG + 2):
                    if i < 16:
                        v.wait_ge(s_mm, s0 + i + 1)
                        nc.vector.tensor_reduce(neg_max[i % 4], bank[S_BANK[i % 3]][:, 0:MEM], AX_X, ALU.min).then_inc(s_min, 1)
                    if 1 <= i < 17:
                        normalise(i - 1, px[(i - 1) % 4], s0 + i - 1)
                    n = i - LAG - 2
                    if n >= 0 and n % 4 == 3:
                        h = n // 4
                        for d in range(2):
                            k = 2 * h + d
                            v.wait_ge(o_rounded, PV1 * l + 4 + k + 1)
                            rest(tile(h_hi, k), tile(h_lo, k), bank[(2 * h + d + 1) % 3][:, :], 1.0, o_ready)
                plain_finish(L + O_WO // 4, 4 * l + 3, G_FFN2 + 8 * l)
                ffn(L + O_FFN2 // 4, 4 * l + 3, 2 * l + 1, G_JOINT if l else G_FFN1 + 8, 0.25)

            for l in range(2):
                L = 2 * (N_L1 // 4) + l * (N_L2 // 4)
                q, v0, e0 = 8 + 2 * l, 24 + 8 * l, 8 * l

                def head_var(heads, h0, h1, to):
                    v.wait_ge(z_mm, e0 + heads)
                    ts(h_var[:, 4 * h0:4 * h1], bank[to][:, 4 * h0:4 * h1], 1.0 / P, EPS, ALU.mult, ALU.add).then_inc(h_v, 1)

                def head_diag(h, first):
                    v.wait_ge(h_i, 5 * l + (2 + h if first else 1))
                    make_diag(h_inv[:, 4 * h:4 * h + 4], diag, h_d)

                def head_norm(h, first, gain, src):
                    v.wait_ge(h_bc, e0 + first + h + 1)
                    z = tile(z_t, h)
                    ins = stt(z, z, col(gain + l), src, ALU.mult, ALU.mult)
                    if first == 0:
                        chain.done(v, ins)
                        ins = stt(z, z, 0.5, tile(gate_s, h), ALU.mult, ALU.mult)
                    ins.then_inc(z_norm, 1)

                def head_rest(h, first):
                    v.wait_ge(o_rounded, 2 * PV1 + e0 + first + h + 1)
                    rest(tile(h_hi, first + h), tile(h_lo, first + h), tile(z_t, h), 1.0, o_ready)

                def take2(c):
                    if c < R_K:
                        scaled(tile(rq_t, c), L, c)
                    elif c < R_V:
                        scaled(tile(rk_t, c - R_K), L, c, 0.125)
                    elif c < R_G:
                        if c >= R_V + 2:
                            v.wait_ge(v_tr, v0 + c - 2 - R_V + 1)
                        scaled(y_buf[c % 2], L, c)
                    elif c < D_Q:
                        scaled(tile(gate_s, c - R_G), L, c)
                    elif c < D_K:
                        scaled(tile(dq_t, c - D_Q), L, c, -0.125)
                    elif c < D_V:
                        scaled(tile(dk_t, c - D_K), L, c)
                    else:
                        if c >= D_V + 2:
                            v.wait_ge(v_tr, v0 + 4 + c - 2 - D_V + 1)
                        scaled(y_buf[c % 2], L, c)

                for c in range(24):
                    if D_Q + 2 <= c < D_Q + 6:
                        head_norm(c - D_Q - 2, 0, G_RET, bank[S_BANK[(c - D_Q - 2) % 2]][:, :])
                    if D_Q + 1 <= c < D_Q + 5:
                        head_diag(c - D_Q - 1, 0)
                    rest_of_weights(L + c // 4, c % 4)
                    if c == 0:
                        norm_scale(q)
                        continue
                    if c == 1:
                        v.wait_ge(rstd_set, q + 1)
                        take2(0)
                    take2(c)
                    if l == 0 and 3 <= c < 11:
                        k = c - 3
                        if k == 0:
                            v.wait_ge(j_set, 1)
                        stt(tile(x, k), tile(x, k), col(G_FINAL + k), j_scale, ALU.mult, ALU.mult).then_inc(x_set, 1)
                    if R_G <= c < D_Q:
                        h = c - R_G
                        v.wait_ge(dec_set, 4 * l + h + 1)
                        if h:
                            v.wait_ge(rpv_mm, 4 * l + h)
                        for j in range(NQ):
                            i = 4 * h + j
                            v.wait_ge(r_mm, 16 * l + i + 1)
                            tt(sd[:, j * S:(j + 1) * S - j * P], bank[S_BANK[i % 2]][:, 0:S - j * P],
                               table[h % 2][:, 0:S - j * P], ALU.mult).then_inc(r_dec, 1)
                        v.wait_ge(g_tanh, 4 * l + h + 1)
                        gs = tile(gate_s, h)
                        chain.done(v, stt(gs, y_buf[c % 2], 1.0, gs, ALU.add, ALU.mult))
                    if c == D_Q:
                        head_var(4, 0, 4, 7)
                    if D_Q + 3 <= c < D_Q + 7:
                        head_rest(c - D_Q - 3, 0)

                s0 = 2 * SCORES1 + 16 * l
                for i in range(16 + LAG + 1):
                    if i < 16:
                        h, t, b = i // 4, i % 4, i % 4
                        if t == 0 and i:
                            v.wait_ge(s_min, s0 + i)
                        if t == 0:
                            chain.done(v, stt(table[h % 2], const[:, C_DIST:C_DIST + S], SLOPE[h], const[:, C_NEG:C_NEG + S],
                                              ALU.mult, ALU.subtract))
                        n = P * (t + 1)
                        v.wait_ge(s_mm, s0 + i + 1)
                        for j in range(2):
                            ins = nc.vector.tensor_tensor_reduce(
                                dsp[b][j][:, 0:n], bank[D_BANK[i % 2][j]][:, 0:n], table[h % 2][:, S - n:S], 1.0, 2 * BIG,
                                ALU.add, ALU.min, neg_max[2 * b + j])
                        ins.then_inc(s_min, 1)
                    if 1 <= i < 17:
                        b, n = (i - 1) % 4, P * ((i - 1) % 4 + 1)
                        p0, p1 = dp[b][0][:, 0:n], dp[b][1][:, 0:n]
                        r0_, r1_ = row_inv[2 * b], row_inv[2 * b + 1]
                        v.wait_ge(p_exp, s0 + i)
                        chain.done(v, nc.vector.reciprocal(small[:, 16 + 2 * b:18 + 2 * b], small[:, 8 + 2 * b:10 + 2 * b]))
                        chain.done(v, ts(r1_, r1_, neg_lam[:, l:l + 1], None, ALU.mult))
                        chain.done(v, ts(p1, p1, r1_, None, ALU.mult))
                        stt(p0, p0, r0_, p1, ALU.mult, ALU.add).then_inc(p_norm, 1)
                    n = i - LAG
                    if n >= 6 and n % 4 == 2:
                        head_var(4 + n // 4, n // 4 - 1, n // 4, 3)
                        head_diag(n // 4 - 1, 4)
                    if n >= 9 and n % 4 == 1:
                        head_norm(n // 4 - 2, 4, G_DIF, bank[3][:, :])
                    if n >= 11 and n % 4 == 3:
                        head_rest(n // 4 - 2, 4)
                head_norm(2, 4, G_DIF, bank[3][:, :])
                head_var(8, 3, 4, 3)
                head_diag(3, 4)
                head_rest(2, 4)
                head_norm(3, 4, G_DIF, bank[3][:, :])
                head_rest(3, 4)
                plain_finish(L + O2_OUT // 4, 9 + 2 * l, G_FFNN2 + 8 * l)
                ffn(L + O2_FFN // 4, 9 + 2 * l, 4 + l, G_ATTN2 + 8 * (l + 1), 0.5, more=l == 0)

            v.wait_ge(stat_mm, 12)
            ts(var, bank[7][:, 0:NQ], 1.0 / D, EPS, ALU.mult, ALU.add).then_inc(stat_var, 1)
            v.wait_ge(stat_inv, 13)
            v.wait_ge(x_set, 24)
            for t in range(2, NQ):
                yt = y_out[:, t * D:(t + 1) * D]
                ts(yt, yt, inv[:, t:t + 1], None, ALU.mult).then_inc(y_scaled[t], 1)

        @block.gpsimd
        def _(pool):
            tt, ts = nc.gpsimd.tensor_tensor, nc.gpsimd.tensor_scalar
            chain = Chain(chain_p)

            def add_square(k):
                chain.done(pool, tt(square, tile(x, k), tile(x, k), ALU.mult))
                tt(sumsq, sumsq, square, ALU.add).then_inc(sq_sum, 1)

            def clear_sum():
                chain.done(pool, nc.gpsimd.memset(sumsq, 0.0))

            def squares(b4, q):
                pool.wait_ge(taken, 4 * b4 + RING + 1)
                clear_sum()
                if q == 8:
                    chain.done(pool, nc.gpsimd.memset(j_sum, 0.0))
                with chain.loop(pool, 0, 2, 8 if q == 8 else 4) as i:
                    for j in range(4):
                        if q == 8:
                            pool.wait_ge(j_squared, i * 4 + (j + 1))
                            chain.done(pool, tt(j_sum, j_sum, tile(j_sq, i * 4 + j), ALU.add))
                        pool.wait_ge(taken, 4 * (b4 + i) + j + RING + 1)
                        if j:
                            pool.wait_ge(sq_sum, 8 * (q - 1) + 4 * i + (j - 1) + 1)
                        add_square(i * 4 + j)
                    pool.wait_ge(sq_sum, 8 * (q - 1) + 4 * i + 4)

            def norm_inv(q):
                pool.wait_ge(stat_var, q + 1)
                if q == 8:
                    chain.done(pool, tt(j_inv, j_var, minus_half[:, 0:NQ], ALU.pow))
                tt(inv, var, minus_half[:, 0:NQ], ALU.pow).then_inc(stat_inv, 1)

            nc.gpsimd.memset(par_in[:, 2 * P:3 * P], 0.0).then_inc(pool_set, 1)
            nc.gpsimd.memset(minus_half, -0.5).then_inc(pool_set, 1)
            nc.gpsimd.memset(half_pi, math.pi / 2).then_inc(pool_set, 1)
            pool.wait_ge(pool_set, 3)
            norm_inv(0)

            for l in range(2):
                L = l * (N_L1 // 4)
                last_down = L + (N_FFN - 8) // 4
                squares(last_down, 4 * l + 1)

                b4, r0 = L + O_MIX // 4, ROPES * l
                norm_inv(4 * l + 1)
                for i in range(2):
                    ins = nc.gpsimd.memset(a_pad[i][:, 0:PAD], 0.0)
                ins.then_inc(pads, 1)

                def times_cos(r, p, rows=P):
                    pool.wait_ge(rot_mm, r0 + r + 1)
                    y = y_buf[p % 2][0:rows, :]
                    tt(y, y, cos_t[0:rows, :], ALU.mult).then_inc(cos_mul, 1)

                def taps(first, last):
                    for j in range(first, last):
                        w, src = col(G_DW + 2 * (TAPS * l + j) + 1), a_pad[1][:, j:j + S]
                        if j == 0:
                            chain.done(pool, ts(conv[1], src, w, col(G_DWB + 2 * l + 1), ALU.mult, ALU.add))
                            continue
                        chain.done(pool, ts(tap_t, src, w, None, ALU.mult))
                        ins = tt(conv[1], conv[1], tap_t, ALU.add)
                        if j < TAPS - 1:
                            chain.done(pool, ins)
                        else:
                            ins.then_inc(conv1, 1)

                times_cos(0, 0, 64)
                for p in range(2, 6):
                    times_cos(p - 1, p, 64)
                pool.wait_ge(a_glu, 4 * l + 2)
                taps(0, 9)
                for p in range(C_Q, C_V):
                    times_cos(5 + p - C_Q, p)
                    taps(9 + (p - C_Q), 10 + (p - C_Q))
                taps(17, TAPS)
                for c in range(2):
                    pool.wait_ge(ln_cent, 2 * l + c + 1)
                    tt(y_buf[c], conv[c], conv[c], ALU.mult).then_inc(ln_sq, 1)
                pool.wait_ge(ln_v, l + 1)
                tt(ln_inv, ln_var, minus_half[:, 0:NQ], ALU.pow).then_inc(ln_i, 1)

                squares(L + O_OUT // 4, 4 * l + 2)
                norm_inv(4 * l + 2)
                pool.wait_ge(mem_sq, 2 * l + 2)
                chain.done(pool, ts(mem_var, mem_var, 1.0 / D, EPS, ALU.mult, ALU.add))
                tt(mem_inv, mem_var, minus_half[:, 0:2], ALU.pow).then_inc(mem_i, 1)
                squares(L + O_WO // 4, 4 * l + 3)
                norm_inv(4 * l + 3)
                squares(L + (O_FFN2 + N_FFN - 8) // 4, 4 * l + 4)
                norm_inv(4 * l + 4)

            for l in range(2):
                L = 2 * (N_L1 // 4) + l * (N_L2 // 4)
                if l:
                    norm_inv(8 + 2 * l)
                pool.wait_ge(h_v, 5 * l + 1)
                tt(h_inv, h_var, minus_half, ALU.pow).then_inc(h_i, 1)
                for h in range(4):
                    pool.wait_ge(h_v, 5 * l + 2 + h)
                    c = slice(4 * h, 4 * h + 4)
                    tt(h_inv[:, c], h_var[:, c], minus_half[:, c], ALU.pow).then_inc(h_i, 1)
                squares(L + O2_OUT // 4, 9 + 2 * l)
                norm_inv(9 + 2 * l)
                squares(L + (O2_FFN + N_FFN - 8) // 4, 10 + 2 * l)
            norm_inv(12)


INPUTS = [
    "x", "mem", "positions", "ffn1_norm", "ffn1_w_gate", "ffn1_w_up", "ffn1_w_down", "mix_norm", "w_in", "conf_dw",
    "conf_dw_b", "conf_ln_g", "conf_ln_b", "sc_dw", "w_out", "xa_norm", "mem_norm", "xa_wq", "xa_wkv", "xa_wo",
    "ffn2_norm", "ffn2_w_gate", "ffn2_w_up", "ffn2_w_down", "final_norm", "attn_norm_2", "w_in_2", "ret_norm_2",
    "lambda_q1_2", "lambda_k1_2", "lambda_q2_2", "lambda_k2_2", "diff_norm_2", "w_out_2", "ffn_norm_2",
    "w_gate_2", "w_up_2", "w_down_2", "final_norm_2",
]


def kernel(**inputs):
    import concourse.bacc as bacc
    from concourse.bass_utils import run_bass_kernel_spmd as run

    nc = bacc.Bacc("TRN2", target_bir_lowering=False, num_devices=1)
    arrays = {f"in_{name}": np.ascontiguousarray(inputs[name]) for name in INPUTS}
    arrays["in_consts"] = constants()
    aps = {name[3:]: nc.dram_tensor(name, a.shape, mybir.dt.from_np(a.dtype), kind="ExternalInput").ap()
           for name, a in arrays.items()}
    out = nc.dram_tensor("out", (1, S, D), F32, kind="ExternalOutput").ap()
    two_blocks(nc, aps, out)
    r = run(nc, [arrays], core_ids=[0])
    return r.results[0]["out"]
```

```python
import math
from contextlib import ExitStack, contextmanager

import numpy as np

import concourse.bass as bass
from concourse import mybir

F32 = mybir.dt.float32
F32R = mybir.dt.float32r
I32 = mybir.dt.int32
ACT = mybir.ActivationFunctionType
ALU = mybir.AluOpType
AX_X = mybir.AxisListType.X

P = 128
S = 512
D = 1024
F = 2816
KT = D // P
NQ = S // P
MEM = 256
RING = 4
CH = KT * P
BIG = 1e30
TAKEN = -3e38
EPS = 1e-6
LN_EPS = 1e-5
TAPS, SC_TAPS = 31, 3
TOPK = 128
ROUNDS = TOPK // 8
PAD, SC_PAD = TAPS - 1, SC_TAPS - 1
MADE, ADDED = 2 * TAPS, 2 * TAPS - 2
LOG_GAMMA = [math.log(1.0 - 2.0 ** (-5 - h)) for h in range(4)]
SLOPE = [2.0 ** (-8.0 * (h + 1) / 4) for h in range(4)]
LAM_INIT = [0.8 - 0.6 * math.exp(-0.3 * m) for m in range(2)]
TWO_PI = (6.28125, 0.0019350051879882812, 2 * math.pi - 6.28125 - 0.0019350051879882812)
ROUND = 1.5 * 2 ** 23

C_ID, C_ONE, C_ROT, C_DIST, C_NEG, C_DEC, C_BIG, C_INV = 0, 128, 256, 384, 896, 1408, 1920, 2048
C_N = C_INV + 1

G_FFN1, G_FINAL, G_MIX, G_XA, G_MEM, G_FFN2, G_ATTN2, G_FINAL2, G_FFNN2 = 0, 16, 24, 40, 56, 72, 88, 104, 112
G_DW, G_DWB = 128, 252
G_JOINT = 280
G_LNG, G_LNB, G_SC, G_RET, G_DIF = 256, 260, 264, 276, 278
G_N = 3 * P

IN1 = ([(3072, 64), (3136, 4)] + [(2816 + 64 * h, 64) for h in range(4)]
       + [(128 * c, 128) for c in range(10)]
       + [(1280 + 128 * c, 128) for c in range(12)])
C_AV, C_AG, C_BG, C_CG, C_BH, C_Q, C_K, C_V = 6, 8, 10, 12, 14, 16, 20, 24
R_Q, R_K, R_V, R_G, D_Q, D_K, D_V = 0, 2, 4, 8, 12, 16, 20
NORM0 = R_G + 9

F_GROUPS = [(0, 8), (8, 8), (16, 6)]
F_TILES = F // P
N_FFN = 2 * F_TILES + KT * len(F_GROUPS)
O_MIX = N_FFN
O_OUT = O_MIX + len(IN1)
O_WQ = O_OUT + 8
O_KV = O_WQ + 8
O_WO = O_KV + 16
O_FFN2 = O_WO + 8
N_L1 = O_FFN2 + N_FFN
O2_OUT = 24
O2_FFN = O2_OUT + 8
N_L2 = O2_FFN + N_FFN
for _n in (N_FFN, O_MIX, O_OUT, O_WQ, O_KV, O_WO, O_FFN2, N_L1, O2_OUT, O2_FFN, N_L2):
    assert _n % RING == 0

LAG = 3
ROPES, SCORES1, PV1 = 13, 48, 12
TAP_STEPS = range(10, 27)


def taps_at(c):
    n = len(TAP_STEPS)
    return range((c - TAP_STEPS[0]) * MADE // n, (c - TAP_STEPS[0] + 1) * MADE // n) if c in TAP_STEPS else range(0)


def rounds_before(p):
    return min(3 * ROUNDS, 3 * (p - 8) if p < 16 else 24 + 9 * (p - 16) // 4 if p < 24 else 42 + 2 * (p - 24))


WTILES = [0, 128, 384, 768]


def constants():
    c = np.zeros((P, C_N), np.float32)
    p = np.arange(P)[:, None]
    m = np.arange(S)[None, :]
    c[:, C_ID:C_ID + P] = np.eye(P)
    for j in range(P):
        c[j + 32 if j % 64 < 32 else j - 32, C_ROT + j] = -1.0 if j % 64 < 32 else 1.0
    dist = 384 + p - m
    c[:, C_DIST:C_DIST + S] = dist
    c[:, C_NEG:C_NEG + S] = np.where(dist >= 0, 0.0, -BIG)
    c[:, C_DEC:C_DEC + S] = np.where(m - p >= 0, m - p, 1e9)
    c[:, C_BIG:C_BIG + P] = np.where(np.arange(P)[None, :] <= p, 0.0, BIG)
    inv = (10000.0 ** (-np.arange(0, 64, 2) / 64)).astype(np.float32)
    c[:, C_INV] = inv[np.arange(P) % 32]
    c[:, C_ONE:C_ONE + P] = 1.0
    return c


class Chain:

    def __init__(self, sem):
        self.sem, self.base, self.k = sem, 0, 0

    def done(self, eng, ins):
        ins.then_inc(self.sem, 1)
        self.k += 1
        eng.wait_ge(self.sem, self.base + self.k)

    @contextmanager
    def loop(self, eng, start, end, per):
        base, k = self.base, self.k
        with eng.Fori(start, end) as i:
            self.base = base + (i - start) * per
            yield i
            assert self.k == k + per, f"per should be {self.k - k}"
        self.base, self.k = base, k + per * (end - start)


def two_blocks(nc, A, out):
    ctx = ExitStack()
    with ctx:
        def sb(name, shape, dt=F32):
            return ctx.enter_context(nc.sbuf_tensor(name, shape, dt))

        def sem(name):
            return ctx.enter_context(nc.semaphore(name))

        x = sb("x", [P, KT * S])
        raw = sb("raw", [P, RING, CH])
        w_hi, w_lo = sb("w_hi", [P, RING, CH], F32R), sb("w_lo", [P, RING, CH], F32R)
        const = sb("const", [P, C_N])
        par = sb("par", [P, G_N])
        cos_t, sin_t = sb("cos_t", [P, S]), sb("sin_t", [P, S])
        rstd = sb("rstd", [P, S])
        small = sb("small", [P, 128])
        mem = sb("mem", [P, 16140])
        with ExitStack() as operands:
            u_hi, u_lo, h_hi, h_lo = (
                operands.enter_context(nc.sbuf_tensor(n, [P, KT * S], F32R)) for n in ("u_hi", "u_lo", "h_hi", "h_lo"))
        spare = sb("spare", [P, 4 * KT * S])
        U_HI, U_LO, H_HI = 0, KT, 2 * KT
        bank = [ctx.enter_context(nc.psum_tensor(f"bank{i}", [P, S], F32)) for i in range(8)]

        def view(at, n):
            return mem[:, at:at + n]

        def tile(t, k, n=1):
            if isinstance(k, int):
                return t[:, k * S:(k + n) * S]
            return t[:, bass.ds(k * S, n * S)]

        def col(k):
            return par[:, k:k + 1] if isinstance(k, int) else par[:, bass.ds(k, 1)]

        def f32(ap):
            return ap.bitcast(F32)

        ident, rot = const[:, C_ID:C_ID + P], const[:, C_ROT:C_ROT + P]
        ones = const[:, C_ONE:C_ONE + P]
        one = const[:, C_ONE:C_ONE + 1]

        y_buf = [view(13572, S), view(14084, S)]
        square, diag = y_buf
        rope_t = view(14596, S)
        sumsq = rope_t
        conv = [view(15108, S), view(15620, S)]
        gate_t, tanh_t, up_t = view(0, S), view(S, S), view(2 * S, S)
        sp = [tile(spare, U_HI + i) for i in range(4)]
        prob = [tile(spare, U_HI + 4 + i) for i in range(4)]
        px = [p_[:, 0:MEM] for p_ in prob]
        dsp = [[tile(spare, U_HI + 2 * b + i) for i in range(2)] for b in range(4)]
        dp = [[tile(spare, U_LO + 2 * b + i) for i in range(2)] for b in range(4)]
        q_t, k_t, v_t = view(0, 2048), view(2048, 2048), view(4096, 2048)
        work = [view(6144 + WTILES[t], P * (t + 1)) for t in range(NQ)]
        pt = [view(11520, 2048), view(7424, 2048)]
        q_idx = [view(7424 + S * h, S) for h in range(4)]
        a_pad = [view(9472 + (PAD + S) * i, PAD + S) for i in range(2)]
        k_idx = view(10556, S)
        yb_t = k_idx
        w_idx_t = conv[0]
        tap_t = [tile(spare, H_HI + 6 + i) for i in (0, 1, KT, KT + 1)]
        relu_t = [view(11520 + S * i, S) for i in range(2)]
        c_pad = [view(11520 + (SC_PAD + S) * i, SC_PAD + S) for i in range(2)]
        b_gate = [view(12548 + S * i, S) for i in range(2)]
        qx = view(0, 4096)
        km, vm = view(4096, 2048), view(6144, 2048)
        mem_in = view(8192, 2048)
        ptx = [view(10240 + 1024 * i, 1024) for i in range(2)]
        vx_t = [view(12800 + MEM * i, MEM) for i in range(2)]
        rq_t, rk_t, rv_t = view(0, 1024), view(1024, 1024), view(2048, 2048)
        dq_t, dk_t, dv_t = view(11264, 2048), view(2048, 2048), view(0, 2048)
        head_d = rope_t
        z_t = view(4096, 2048)
        table = [view(6144 + S * i, S) for i in range(2)]
        sd = view(7168, 2048)
        d_pt = [sd, view(9216, 2048)]
        gate_s = view(9216, 2048)
        zsq = conv
        x_in = view(0, 4096)
        par_in = view(8192, G_N)
        pos_i = view(9216, S).bitcast(I32)
        ang, turns, cos_half, x_sq = view(9728, S), view(10752, S), view(11264, S), view(11776, NQ * D)
        lam_in = view(10240, 2 * 4 * 64)
        y_out = tile(spare, U_HI, KT)
        z_in = view(2048, 4096)
        j_sq, j_sum = view(2048, 4096), view(6144, S)
        j_diag, j_scale = y_buf[0], view(11264, S)

        neg_max = [small[:, i:i + 1] for i in range(8)]
        row_sum = [small[:, 8 + i:9 + i] for i in range(8)]
        row_inv = [small[:, 16 + i:17 + i] for i in range(8)]
        var, inv = small[:, 24:28], small[:, 28:32]
        ln_var, ln_inv = small[:, 32:36], small[:, 36:40]
        w_idx = small[:, 40:56]
        max8 = small[:, 56:64]
        h_var, h_inv = small[:, 64:80], small[:, 80:96]
        minus_half = small[:, 96:112]
        neg_lam = small[:, 112:114]
        lam_s = small[:, 114:118]
        half_pi = small[:, 118:119]
        mem_var, mem_inv = small[:, 120:122], small[:, 122:124]
        j_var, j_inv = ln_var, ln_inv

        D_BANK = ((4, 5), (0, 1))
        V_BANK = (7, 4)
        R_BANK = (6, 5)
        S_BANK, T_BANK = (4, 5, 3), (6, 7)

        raw_in = [sem(f"raw_in{i}") for i in range(RING)]
        setup_in, x_landed, mem_landed, stored = sem("setup_in"), [sem(f"x_landed{t}") for t in range(NQ)], sem("mem_landed"), sem("stored")
        j_squared, j_diag_set, j_bc, j_set, z_rounded = (sem(n) for n in ("j_squared", "j_diag_set", "j_bc", "j_set", "z_rounded"))
        y_scaled = [sem(f"y_scaled{t}") for t in range(NQ)]
        first_in, par_in_set, x_squared = sem("first_in"), sem("par_in_set"), sem("x_squared")
        rounded = sem("rounded")
        split = sem("split")
        tiles = sem("tiles")
        taken = sem("taken")
        u_rounded, u_ready = sem("u_rounded"), sem("u_ready")
        sq_sum = sem("sq_sum")
        stat_mm, stat_var, stat_inv, stat_diag, stat_bc, rstd_set = (
            sem(n) for n in ("stat_mm", "stat_var", "stat_inv", "stat_diag", "stat_bc", "rstd_set"))
        x_set, x_tr = sem("x_set"), sem("x_tr")
        par_tr, par_set, tab_set, pool_set = sem("par_tr"), sem("par_set"), sem("tab_set"), sem("pool_set")
        tab_sin = sem("tab_sin")
        f_tanh, f_prod, f_rounded, f_ready = sem("f_tanh"), sem("f_prod"), sem("f_rounded"), sem("f_ready")
        rot_mm, cos_mul, roped = sem("rot_mm"), sem("cos_mul"), sem("roped")
        wi_tr, wi_set = sem("wi_tr"), sem("wi_set")
        idx_mm, idx_relu, idx_add = sem("idx_mm"), sem("idx_relu"), sem("idx_add")
        pads, a_tanh, a_glu = sem("pads"), sem("a_tanh"), sem("a_glu")
        tap_made, tap_added = sem("tap_made"), sem("tap_added")
        y_made, y_rounded, y_ready = sem("y_made"), sem("y_rounded"), sem("y_ready")
        v_tr, v_set = sem("v_tr"), sem("v_set")
        ln_mean, ln_cent, ln_sq, ln_mm, ln_v, ln_i, ln_d, ln_bc, ln_y, ln_z, ln_t = (
            sem(n) for n in ("ln_mean", "ln_cent", "ln_sq", "ln_mm", "ln_v", "ln_i", "ln_d", "ln_bc", "ln_y", "ln_z", "ln_t"))
        masked = sem("masked")
        s_mm, s_min, p_exp, p_norm, t_mm, t_set, pv_mm = (
            sem(n) for n in ("s_mm", "s_min", "p_exp", "p_norm", "t_mm", "t_set", "pv_mm"))
        o_rounded, o_ready = sem("o_rounded"), sem("o_ready")
        mem_sq, mem_v, mem_i, mem_n, mem_tr, gm_rounded, gm_ready = (
            sem(n) for n in ("mem_sq", "mem_v", "mem_i", "mem_n", "mem_tr", "gm_rounded", "gm_ready"))
        r_mm, r_dec, dec_set, rpv_mm, z_sq, z_mm = (sem(n) for n in ("r_mm", "r_dec", "dec_set", "rpv_mm", "z_sq", "z_mm"))
        h_v, h_i, h_d, h_bc, z_norm, g_tanh, al_set = (
            sem(n) for n in ("h_v", "h_i", "h_d", "h_bc", "z_norm", "g_tanh", "al_set"))
        chain_v, chain_a, chain_p = sem("chain_v"), sem("chain_a"), sem("chain_p")

        W = {n: A[n].rearrange("l (k p) n -> l p k n", p=P) for n in (
            "ffn1_w_gate", "ffn1_w_up", "ffn1_w_down", "w_in", "w_out", "xa_wq", "xa_wkv", "xa_wo",
            "ffn2_w_gate", "ffn2_w_up", "ffn2_w_down", "w_in_2", "w_out_2", "w_gate_2", "w_up_2", "w_down_2")}

        block = ctx.enter_context(nc.Block())

        @block.sync
        def _(sp_e):
            def load(b4, j, w, l, k0, kn, c, width=P):
                sp_e.wait_ge(split, 4 * b4 + j + 1)
                dst = raw[:, j % RING, 0:kn * P].rearrange("p (k n) -> p k n", n=P)[:, :, 0:width]
                cols = slice(c, c + width) if isinstance(c, int) else bass.ds(c, width)
                sp_e.dma_start(dst, w[l, :, k0:k0 + kn, cols]).then_inc(raw_in[j % RING], 16)

            def load_ffn(b4, l, gate, up, down, ahead=0):
                for f0, fn in F_GROUPS:
                    with sp_e.Fori(0 if f0 else ahead, fn // 2) as i:
                        for j in range(4):
                            load(b4 + i, j, W[up if j % 2 else gate], l, 0, KT, (i * 2 + (f0 + j // 2)) * P)
                    b4 = b4 + fn // 2
                    with sp_e.Fori(0, 2) as i:
                        for j in range(4):
                            load(b4 + i, j, W[down], l, f0, fn, (i * 4 + j) * P)
                    b4 = b4 + 2

            def load_plain(b4, l, name, chunks):
                with sp_e.Fori(0, chunks // 4) as i:
                    for j in range(4):
                        load(b4 + i, j, W[name], l, 0, KT, (i * 4 + j) * P)

            sp_e.dma_start(const[:, 0:2 * P], A["consts"][:, 0:2 * P]).then_inc(first_in, 16)
            sp_e.dma_start(par_in[0:2 * KT, 0:P], A["ffn1_norm"].rearrange("l (i c) -> (l i) c", c=P)).then_inc(first_in, 16)
            for t in range(NQ):
                sp_e.dma_start(x_in[:, t * D:(t + 1) * D], A["x"][0, t * P:(t + 1) * P, :]).then_inc(x_landed[t], 16)

            for j in range(4):
                load(0, j, W["ffn1_w_up" if j % 2 else "ffn1_w_gate"], 0, 0, KT, j // 2 * P)
            sp_e.wait_ge(pool_set, 1)
            rows = [("final_norm", 0, 16), ("mix_norm", 0, 24), ("xa_norm", 0, 40),
                    ("mem_norm", 0, 56), ("ffn2_norm", 0, 72), ("attn_norm_2", 0, 88), ("final_norm_2", 0, 104),
                    ("ffn_norm_2", 0, 112), ("conf_dw", 1, 0), ("conf_dw_b", 1, 124), ("conf_ln_g", 2, 0),
                    ("conf_ln_b", 2, 4), ("sc_dw", 2, 8), ("ret_norm_2", 2, 20), ("diff_norm_2", 2, 22)]
            for name, t, r in rows:
                src = A[name]
                if len(src.shape) == 3:
                    src = src.rearrange("l j (i c) -> (l j i) c", c=P)
                elif len(src.shape) == 2:
                    src = src.rearrange("l (i c) -> (l i) c", c=P)
                else:
                    src = src.rearrange("(i c) -> i c", c=P)
                sp_e.dma_start(par_in[r:r + src.shape[0], t * P:(t + 1) * P], src).then_inc(par_in_set, 16)
            sp_e.dma_start(pos_i, A["positions"].to_broadcast([P, S])).then_inc(setup_in, 16)
            for i, name in enumerate(("lambda_q1_2", "lambda_k1_2", "lambda_q2_2", "lambda_k2_2")):
                sp_e.dma_start(lam_in[:, i * P:(i + 1) * P],
                               A[name].rearrange("(o l) d -> o (l d)", o=1).to_broadcast([P, P])).then_inc(setup_in, 16)
            sp_e.dma_start(const[:, 2 * P:C_N], A["consts"][:, 2 * P:C_N]).then_inc(setup_in, 16)
            for l in range(2):
                b4 = l * (N_L1 // 4)
                load_ffn(b4, l, "ffn1_w_gate", "ffn1_w_up", "ffn1_w_down", ahead=1 - l)
                for c, (first, width) in enumerate(IN1):
                    load(b4 + O_MIX // 4 + c // 4, c % 4, W["w_in"], l, 0, KT, first, width)
                load_plain(b4 + O_OUT // 4, l, "w_out", 8)
                sp_e.wait_ge(o_ready, PV1 * l + 4)
                sp_e.dma_start(mem_in.rearrange("p (t d) -> p t d", t=2),
                               A["mem"][0].rearrange("(t p) d -> p t d", p=P)).then_inc(mem_landed, 16)
                load_plain(b4 + O_WQ // 4, l, "xa_wq", 8)
                load_plain(b4 + O_KV // 4, l, "xa_wkv", 16)
                load_plain(b4 + O_WO // 4, l, "xa_wo", 8)
                load_ffn(b4 + O_FFN2 // 4, l, "ffn2_w_gate", "ffn2_w_up", "ffn2_w_down")
            for l in range(2):
                b4 = 2 * (N_L1 // 4) + l * (N_L2 // 4)
                load_plain(b4, l, "w_in_2", 24)
                load_plain(b4 + O2_OUT // 4, l, "w_out_2", 8)
                load_ffn(b4 + O2_FFN // 4, l, "w_gate_2", "w_up_2", "w_down_2")
            for t in (0, 2, 1, 3):
                sp_e.wait_ge(y_scaled[t], 1)
                sp_e.dma_start(out[0, t * P:(t + 1) * P, :], y_out[:, t * D:(t + 1) * D]).then_inc(stored, 16)
            sp_e.wait_ge(stored, 16 * NQ)

        @block.tensor
        def _(pe):
            mm = nc.tensor.matmul

            def chunk(b4, j, rhs_hi, rhs_lo, kn=KT, last=None, n=S, ks=None):
                at = 4 * b4 + j
                ks = ks or range(kn)
                if ks[0] == 0:
                    pe.wait_ge(split, at + RING + 1)
                    pe.wait_ge(taken, at + 1)
                s = j % RING
                for k in ks:
                    if last is not None and k >= kn - 2:
                        pe.wait_ge(last[0], last[1] - (kn - 1 - k))
                    w = slice(k * P, (k + 1) * P)
                    r = slice(k * n, (k + 1) * n)
                    o = bank[s][:, 0:n]
                    mm(o, w_hi[:, s, w], rhs_hi[:, r], start=k == 0, stop=False)
                    mm(o, w_hi[:, s, w], rhs_lo[:, r], start=False, stop=False)
                    ins = mm(o, w_lo[:, s, w], rhs_hi[:, r], start=False, stop=k == kn - 1)
                if ks[-1] == kn - 1:
                    ins.then_inc(tiles, 1)

            def stat(q):
                pe.wait_ge(sq_sum, 8 * q)
                for t in range(NQ):
                    ins = mm(bank[7][:, t:t + 1], sumsq[:, t * P:(t + 1) * P], one, start=True, stop=True)
                if q == 8:
                    for t in range(NQ):
                        ins = mm(bank[7][:, NQ + t:NQ + t + 1], j_sum[:, t * P:(t + 1) * P], one, start=True, stop=True)
                ins.then_inc(stat_mm, 1)

            def spread(q):
                pe.wait_ge(stat_diag, q + 1)
                mm(bank[7][:, :], ones, diag, start=True, stop=True).then_inc(stat_bc, 1)

            def first_two(b4, q, j, **kw):
                last = (u_ready, 8 * q + 8)
                if j == 0:
                    pe.wait_ge(u_ready, 8 * q + 6)
                chunk(b4, j, u_hi, u_lo, last=last if j == 0 else None)
                if j == (1 if q == 8 else 0) and q:
                    stat(q)
                if j == 1 and q and q != 8:
                    spread(q)

            def result_transpose(k):
                pe.wait_ge(z_rounded, k + 1)
                if k >= 2:
                    pe.wait_ge(x_set, 16 + k - 1)
                for t in range(NQ):
                    ins = nc.tensor.transpose(bank[4 + k % 2][:, t * P:(t + 1) * P], z_in[:, k * S + t * P:k * S + (t + 1) * P], ident)
                ins.then_inc(x_tr, 1)

            def ffn(b4, q, f, end=False):
                for g, (f0, fn) in enumerate(F_GROUPS):
                    if g == 0:
                        if not q:
                            for k in range(KT):
                                pe.wait_ge(u_ready, k + 1)
                                chunk(b4, 0, u_hi, u_lo, ks=range(k, k + 1))
                        for j in range(0 if q else 1, 4):
                            first_two(b4, q, j)
                            if not q and j == 1:
                                pe.wait_ge(par_in_set, 16 * 15)
                                for t in range(3):
                                    ins = nc.tensor.transpose(bank[6][:, t * P:(t + 1) * P], par_in[:, t * P:(t + 1) * P], ident)
                                ins.then_inc(par_tr, 1)
                            if not q and j == 2:
                                spread(0)
                    with pe.Fori(1 if g == 0 else 0, fn // 2) as i:
                        for j in range(4):
                            chunk(b4 + i, j, u_hi, u_lo)
                    b4 = b4 + fn // 2
                    pe.wait_ge(f_ready, F_TILES * f + f0 + fn - 2)
                    if end and g == len(F_GROUPS) - 1:
                        for k in range(KT):
                            chunk(b4, k, h_hi, h_lo, kn=fn, last=(f_ready, F_TILES * f + (f0 + fn)) if k == 0 else None)
                            if k >= 2:
                                result_transpose(k - 2)
                        result_transpose(6)
                        result_transpose(7)
                        continue
                    with pe.Fori(0, 2) as i:
                        for j in range(4):
                            chunk(b4 + i, j, h_hi, h_lo, kn=fn,
                                  last=(f_ready, F_TILES * f + (f0 + fn)) if j == 0 else None)
                    b4 = b4 + 2

            def plain(b4, chunks, hi, lo, n=S, last=None):
                if last is not None:
                    pe.wait_ge(last[0], last[1] - 2)
                    for j in range(4):
                        chunk(b4, j, hi, lo, n=n, last=last if j == 0 else None)
                with pe.Fori(0 if last is None else 1, chunks // 4) as i:
                    for j in range(4):
                        chunk(b4 + i, j, hi, lo, n=n)

            def rotate(r0, r, b4, c, src, rows=P):
                pe.wait_ge(taken, 4 * b4 + c + RING + 1)
                if r >= 2:
                    pe.wait_ge(roped, r0 + r - 1)
                mm(bank[R_BANK[r % 2]][0:rows, :], rot[0:rows, 0:rows], src[0:rows, :], start=True, stop=True).then_inc(rot_mm, 1)

            def transposes(e, src, blocks, to, width=P):
                for j in range(blocks):
                    ins = nc.tensor.transpose(bank[to][:, j * P:(j + 1) * P], src[:, j * P:(j + 1) * P], ident)
                ins.then_inc(e, 1)

            def v_transpose(v0, i, b4, c, blocks=NQ, src=None, banks=T_BANK):
                pe.wait_ge(taken, 4 * b4 + c + RING + 1)
                if i >= 2:
                    pe.wait_ge(v_set, v0 + i - 1)
                transposes(v_tr, src if src is not None else y_buf[c % 2], blocks, banks[c % 2])

            pe.wait_ge(first_in, 32)
            nc.tensor.transpose(bank[3][:, 0:2 * KT], par_in[0:2 * KT, 0:P], const[0:2 * KT, C_ID:C_ID + 2 * KT]).then_inc(par_tr, 1)
            for t in range(NQ):
                pe.wait_ge(x_landed[t], 16)
            for k in range(KT):
                if k >= 4:
                    pe.wait_ge(x_set, k - 3)
                for t in range(NQ):
                    ins = nc.tensor.transpose(bank[4 + k % 4][:, t * P:(t + 1) * P],
                                              x_in[:, t * D + k * P:t * D + (k + 1) * P], ident)
                ins.then_inc(x_tr, 1)

            for l in range(2):
                L = l * (N_L1 // 4)
                ffn(L, 4 * l, 2 * l)

                b4, q, r0 = L + O_MIX // 4, 4 * l + 1, ROPES * l
                N0 = 4 * b4
                for c in range(len(IN1)):
                    if c < 2:
                        first_two(b4, q, c)
                    else:
                        chunk(b4 + c // 4, c % 4, u_hi, u_lo)
                    p = c - 1
                    if p == 0:
                        rotate(r0, 0, b4, 0, y_buf[0], 64)
                    if p == 1:
                        pe.wait_ge(taken, N0 + 2 + RING)
                        for t in range(NQ):
                            ins = nc.tensor.transpose(bank[7][:, 4 * t:4 * t + 4], w_idx_t[0:4, t * P:(t + 1) * P],
                                                      const[0:4, C_ID:C_ID + 4])
                        ins.then_inc(wi_tr, 1)
                    if 2 <= p < 6:
                        rotate(r0, p - 1, b4, p, y_buf[p % 2], 64)
                    if C_Q <= p < C_V:
                        rotate(r0, 5 + p - C_Q, b4, p, y_buf[p % 2])
                    if p == 7:
                        pe.wait_ge(roped, r0 + 5)
                        for i in range(12):
                            t, h = 1 + i // 4, i % 4
                            if i >= 2:
                                pe.wait_ge(idx_relu, 12 * l + i - 1)
                            mm(bank[S_BANK[i % 2]][:, 0:P * (t + 1)], q_idx[h][0:64, t * P:(t + 1) * P],
                               k_idx[0:64, 0:P * (t + 1)], start=True, stop=True).then_inc(idx_mm, 1)
                    if p >= C_V:
                        v_transpose(12 * l, p - C_V, b4, p, banks=V_BANK)
                v_transpose(12 * l, 3, b4, 27, banks=V_BANK)

                s0, pv0 = SCORES1 * l, PV1 * l
                pe.wait_ge(roped, r0 + ROPES)
                pe.wait_ge(taken, N0 + 28 + RING)
                pe.wait_ge(v_set, 12 * l + 4)

                def pv_sparse(h):
                    pe.wait_ge(t_set, s0 + 4 * h + 4)
                    if h >= 4 and h % 2 == 0:
                        pe.wait_ge(o_ready, PV1 * l + h // 2 - 1)
                    o = bank[(h // 2) % 2]
                    rows = slice(64 * (h % 2), 64 * (h % 2) + 64)
                    for j in range(NQ):
                        ins = mm(o[rows, j * P:S], v_t[:, j * S + 64 * h:j * S + 64 * h + 64],
                                 pt[h % 2][:, j * S + j * P:(j + 1) * S], start=j == 0, stop=j == NQ - 1)
                    ins.then_inc(pv_mm, 1)

                for i in range(32 + LAG + 2):
                    if i < 32:
                        h, t = i // 4, i % 4
                        rows = slice(64 * (h % 2), 64 * (h % 2) + 64)
                        if i >= 3:
                            pe.wait_ge(s_min, s0 + i - 2)
                        mm(bank[S_BANK[i % 3]][:, 0:P * (t + 1)],
                           q_t[rows, (h // 2) * S + t * P:(h // 2) * S + (t + 1) * P],
                           k_t[rows, (h // 2) * S:(h // 2) * S + P * (t + 1)], start=True, stop=True).then_inc(s_mm, 1)
                    n = i - LAG
                    if 0 <= n < 32:
                        pe.wait_ge(p_norm, s0 + n + 1)
                        if n >= 2:
                            pe.wait_ge(t_set, s0 + n - 1)
                        transposes(t_mm, prob[n % 4], n % 4 + 1, T_BANK[n % 2])
                    if n >= 5 and n % 4 == 1:
                        pv_sparse(n // 4 - 1)
                    if i == 8:
                        pe.wait_ge(tap_added, ADDED * (l + 1))
                        mm(bank[2][:, :], ones, conv[0], start=True, stop=False)
                        mm(bank[2][:, :], ones, conv[1], start=False, stop=True).then_inc(ln_mean, 1)
                    if i == 11:
                        pe.wait_ge(ln_sq, 2 * l + 2)
                        for t in range(NQ):
                            for c in range(2):
                                ins = mm(bank[2][:, t:t + 1], y_buf[c][:, t * P:(t + 1) * P], one, start=c == 0, stop=c == 1)
                        ins.then_inc(ln_mm, 1)
                    if i == 15:
                        pe.wait_ge(ln_d, l + 1)
                        mm(bank[2][:, :], ones, rope_t, start=True, stop=True).then_inc(ln_bc, 1)

                pe.wait_ge(y_ready, 4 * l + 4)
                plain(L + O_OUT // 4, 8, h_hi, h_lo, last=(o_ready, PV1 * l + 4))

                b4, q = L + O_WQ // 4, 4 * l + 2
                for c in range(8):
                    if c < 2:
                        first_two(b4, q, c)
                    else:
                        chunk(b4 + c // 4, c % 4, u_hi, u_lo)
                    if 2 <= c < 6:
                        r = c - 2
                        pe.wait_ge(mem_n, l + 1)
                        if r >= 2:
                            pe.wait_ge(gm_ready, 8 * l + 2 * (r - 2) + 2)
                        for k in range(2):
                            for t in range(2):
                                ins = nc.tensor.transpose(bank[S_BANK[r % 2]][:, (2 * k + t) * P:(2 * k + t + 1) * P],
                                                          mem_in[:, t * D + (2 * r + k) * P:t * D + (2 * r + k + 1) * P], ident)
                        ins.then_inc(mem_tr, 1)
                pe.wait_ge(gm_ready, 8 * l + 8)
                plain(L + O_KV // 4, 8, h_hi, h_lo, n=MEM)
                b4 = L + O_KV // 4 + 2
                for c in range(8):
                    chunk(b4 + c // 4, c % 4, h_hi, h_lo, n=MEM)
                    if c >= 1:
                        v_transpose(12 * l, 4 + c - 1, b4, c - 1, 2, vx_t[(c - 1) % 2])
                v_transpose(12 * l, 4 + 7, b4, 7, 2, vx_t[1])

                s0, pv0 = SCORES1 * l + 32, PV1 * l + 8
                pe.wait_ge(taken, 4 * b4 + 8 + RING)
                pe.wait_ge(v_set, 12 * l + 12)
                for i in range(16 + LAG + 2):
                    if i < 16:
                        h, t = i // 4, i % 4
                        if i >= 3:
                            pe.wait_ge(p_exp, s0 + i - 2)
                        for c in range(2):
                            ins = mm(bank[S_BANK[i % 3]][:, 0:MEM], qx[:, (2 * h + c) * S + t * P:(2 * h + c) * S + (t + 1) * P],
                                     km[:, (2 * h + c) * MEM:(2 * h + c + 1) * MEM], start=c == 0, stop=c == 1)
                        ins.then_inc(s_mm, 1)
                    n = i - LAG
                    if 0 <= n < 16:
                        pe.wait_ge(p_norm, s0 + n + 1)
                        if n >= 2:
                            pe.wait_ge(t_set, s0 + n - 1)
                        transposes(t_mm, px[n % 4], 2, T_BANK[n % 2])
                    if n >= 5 and n % 4 == 1:
                        h = n // 4 - 1
                        pe.wait_ge(t_set, s0 + 4 * h + 4)
                        for d in range(2):
                            if 2 * h + d >= 3:
                                pe.wait_ge(o_ready, PV1 * l + 4 + 2 * h + d - 2)
                            for j in range(2):
                                ins = mm(bank[(2 * h + d + 1) % 3][:, :], vm[:, j * D + (2 * h + d) * P:j * D + (2 * h + d + 1) * P],
                                         ptx[h % 2][:, j * S:(j + 1) * S], start=j == 0, stop=j == 1)
                        ins.then_inc(pv_mm, 1)
                plain(L + O_WO // 4, 8, h_hi, h_lo, last=(o_ready, PV1 * l + 4 + 8))
                ffn(L + O_FFN2 // 4, 4 * l + 3, 2 * l + 1)

            for l in range(2):
                L = 2 * (N_L1 // 4) + l * (N_L2 // 4)
                q = 8 + 2 * l
                v0, e0 = 24 + 8 * l, 8 * l

                def r_scores(h, j):
                    i = 4 * h + j
                    rows = slice(64 * (h % 2), 64 * (h % 2) + 64)
                    if i >= 2:
                        pe.wait_ge(r_dec, 16 * l + i - 1)
                    mm(bank[S_BANK[i % 2]][:, 0:S - j * P], rk_t[rows, (h // 2) * S + j * P:(h // 2) * S + (j + 1) * P],
                       rq_t[rows, (h // 2) * S + j * P:(h // 2 + 1) * S], start=True, stop=True).then_inc(r_mm, 1)

                def r_values(h, j):
                    pe.wait_ge(r_dec, 16 * l + 4 * h + j + 1)
                    if j == 0 and h >= 1:
                        pe.wait_ge(z_sq, e0 + h)
                    ins = mm(bank[6][:, j * P:S], rv_t[:, j * S + h * P:j * S + (h + 1) * P],
                             sd[:, j * S:(j + 1) * S - j * P], start=j == 0, stop=j == NQ - 1)
                    if j == NQ - 1:
                        ins.then_inc(rpv_mm, 1)

                def head_stat(h, first, to):
                    pe.wait_ge(z_sq, e0 + first + h + 1)
                    if first and h:
                        pe.wait_ge(z_norm, e0 + first + h)
                    for t in range(NQ):
                        ins = mm(bank[to][:, 4 * h + t:4 * h + t + 1], zsq[h % 2][:, t * P:(t + 1) * P], one,
                                 start=True, stop=True)
                    ins.then_inc(z_mm, 1)

                def head_spread(h, first, banks):
                    pe.wait_ge(h_d, e0 + first + h + 1)
                    if h >= 2 and not first:
                        pe.wait_ge(z_norm, e0 + first + h - 1)
                    mm(bank[banks[h % 2]][:, :], ones, head_d, start=True, stop=True).then_inc(h_bc, 1)

                for c in range(24):
                    if c < 2:
                        first_two(L, q, c)
                    else:
                        chunk(L + c // 4, c % 4, u_hi, u_lo)
                    p = c - 1
                    if l == 0 and c == 2:
                        spread(q)
                    if l == 0 and c == 3:
                        pe.wait_ge(j_diag_set, 1)
                        pe.wait_ge(rstd_set, q + 1)
                        mm(bank[7][:, :], ones, j_diag, start=True, stop=True).then_inc(j_bc, 1)
                    if l == 0 and p == R_V:
                        pe.wait_ge(j_set, 1)
                    if R_V <= p < R_G:
                        v_transpose(v0, p - R_V, L, p)
                    h, half = divmod(c - R_G - 1, 2)
                    if c == R_G:
                        r_scores(0, 0)
                        r_scores(0, 1)
                    if 0 <= h < 4 and half == 0:
                        if h == 0:
                            pe.wait_ge(v_set, v0 + 4)
                        r_values(h, 0)
                        r_values(h, 1)
                        r_scores(h, 2)
                        r_scores(h, 3)
                    if 0 <= h < 4 and half == 1:
                        r_values(h, 2)
                        r_values(h, 3)
                        if h < 3:
                            r_scores(h + 1, 0)
                            r_scores(h + 1, 1)
                    if 1 <= h <= 4 and half == 0:
                        head_stat(h - 1, 0, 7)
                    if NORM0 < c <= NORM0 + 4:
                        head_spread(c - NORM0 - 1, 0, S_BANK)
                    if D_V <= p:
                        v_transpose(v0, 4 + p - D_V, L, p)
                v_transpose(v0, 7, L, 23)

                s0 = 2 * SCORES1 + 16 * l
                pe.wait_ge(taken, 4 * L + 24 + RING)
                pe.wait_ge(v_set, v0 + 8)
                pe.wait_ge(z_norm, e0 + 4)
                for i in range(16 + LAG + 2):
                    if i < 16:
                        h, t = i // 4, i % 4
                        if i >= 2:
                            pe.wait_ge(s_min, s0 + i - 1)
                        for j in range(2):
                            rows = slice(64 * j, 64 * j + 64)
                            ins = mm(bank[D_BANK[i % 2][j]][:, 0:P * (t + 1)], dq_t[rows, h * S + t * P:h * S + (t + 1) * P],
                                     dk_t[rows, h * S:h * S + P * (t + 1)], start=True, stop=True)
                        ins.then_inc(s_mm, 1)
                    n = i - LAG
                    if 0 <= n < 16:
                        pe.wait_ge(p_norm, s0 + n + 1)
                        if n >= 2:
                            pe.wait_ge(t_set, s0 + n - 1)
                        transposes(t_mm, dp[n % 4][0], n % 4 + 1, T_BANK[n % 2])
                    if n >= 5 and n % 4 == 1:
                        h = n // 4 - 1
                        pe.wait_ge(t_set, s0 + 4 * h + 4)
                        if h >= 1:
                            pe.wait_ge(z_sq, e0 + 4 + h)
                        for j in range(NQ):
                            ins = mm(bank[2][:, j * P:S], dv_t[:, j * S + h * P:j * S + (h + 1) * P],
                                     d_pt[h % 2][:, j * S + j * P:(j + 1) * S], start=j == 0, stop=j == NQ - 1)
                        ins.then_inc(pv_mm, 1)
                    if n >= 7 and n % 4 == 3:
                        head_stat(n // 4 - 1, 4, 3)
                    if n >= 9 and n % 4 == 1:
                        head_spread(n // 4 - 2, 4, (3, 3))
                first = (o_ready, 2 * PV1 + 8 * l + 8)
                most, last = range(KT - 1), range(KT - 1, KT)
                b4 = L + O2_OUT // 4
                head_stat(3, 4, 3)
                pe.wait_ge(o_ready, 2 * PV1 + 8 * l + 6)
                chunk(b4, 0, h_hi, h_lo, ks=most, last=first)
                head_spread(3, 4, (3, 3))
                chunk(b4, 1, h_hi, h_lo, ks=most)
                chunk(b4, 2, h_hi, h_lo, ks=most)
                chunk(b4, 0, h_hi, h_lo, ks=last, last=first)
                chunk(b4, 1, h_hi, h_lo, ks=last)
                chunk(b4, 2, h_hi, h_lo, ks=last)
                pe.wait_ge(z_norm, e0 + 8)
                chunk(b4, 3, h_hi, h_lo)
                plain(b4 + 1, 4, h_hi, h_lo)
                ffn(L + O2_FFN // 4, 9 + 2 * l, 4 + l, end=l == 1)

            stat(12)

        @block.scalar
        def _(act):
            a = nc.scalar.activation
            chain = Chain(chain_a)

            def round_weights(b4, j, ahead=RING):
                act.wait_ge(raw_in[j], (b4 + (1 + ahead // 4)) * 16)
                if ahead:
                    act.wait_ge(tiles, 4 * b4 + j + 1)
                a(w_hi[:, j, :], raw[:, j, :], ACT.Copy).then_inc(rounded, 1)

            def finish(q, k, gain):
                a(tile(u_hi, k), tile(x, k), ACT.Copy, scale=col(gain)).then_inc(u_rounded, 1)

            def keep_rstd(q):
                act.wait_ge(stat_bc, q + 1)
                a(rstd[:, :], bank[7][:, :], ACT.Copy).then_inc(rstd_set, 1)

            def step(n4, j, more=True):
                if more:
                    round_weights(n4, j)

            def ffn(b4, q, f, gain, more=True, joint=False):
                for g, (f0, fn) in enumerate(F_GROUPS):
                    def pair(b4, f_at, h_at, jj):
                        step(b4, 2 * jj)
                        act.wait_ge(taken, 4 * b4 + 2 * jj + RING + 1)
                        a(tanh_t, gate_t, ACT.Tanh, scale=0.5).then_inc(f_tanh, 1)
                        step(b4, 2 * jj + 1)
                        act.wait_ge(f_prod, F_TILES * f + f_at + 1)
                        a(tile(h_hi, h_at), gate_t, ACT.Copy).then_inc(f_rounded, 1)

                    if g == 0:
                        step(b4, 0)
                        step(b4, 1)
                        if q:
                            keep_rstd(q)
                        act.wait_ge(taken, 4 * b4 + RING + 1)
                        a(tanh_t, gate_t, ACT.Tanh, scale=0.5).then_inc(f_tanh, 1)
                        act.wait_ge(f_prod, F_TILES * f + 1)
                        a(tile(h_hi, 0), gate_t, ACT.Copy).then_inc(f_rounded, 1)
                        pair(b4, 1, 1, 1)
                    with act.Fori(1 if g == 0 else 0, fn // 2) as i:
                        for jj in range(2):
                            pair(b4 + i, i * 2 + (f0 + jj), i * 2 + jj, jj)
                    b4 = b4 + fn // 2
                    end = g == len(F_GROUPS) - 1

                    def down(b4, k, j, more):
                        step(b4, j, more)
                        if end:
                            act.wait_ge(taken, 4 * b4 + j + RING + 1)
                            finish(q + 1, k, gain + k)
                        if end and joint:
                            a(tile(j_sq, k), tile(x, k), ACT.Square, scale=col(G_FINAL + k)).then_inc(j_squared, 1)
                    if end and not more:
                        for k in range(KT):
                            step(b4, k, k < 4)
                            act.wait_ge(taken, 4 * b4 + k + RING + 1)
                            a(tile(z_in, k), tile(x, k), ACT.Copy, scale=col(gain + k)).then_inc(z_rounded, 1)
                        continue
                    with act.Fori(0, 2) as i:
                        for j in range(4):
                            down(b4 + i, i * 4 + j, j, True)
                    b4 = b4 + 2

            def plain_finish(b4, q, gain):
                with act.Fori(0, 2) as i:
                    for j in range(4):
                        step(b4 + i, j)
                        act.wait_ge(taken, 4 * (b4 + i) + j + RING + 1)
                        finish(q, i * 4 + j, i * 4 + (gain + j))

            def v_store(i, c, dst, blocks=NQ, banks=T_BANK):
                act.wait_ge(v_tr, i + 1)
                a(dst, bank[banks[c % 2]][:, 0:blocks * P].rearrange("p (j n) -> p j n", n=P), ACT.Copy)\
                    .then_inc(v_set, 1)

            for k in range(KT):
                act.wait_ge(x_tr, k + 1)
                a(tile(x, k), bank[4 + k % 4][:, :], ACT.Copy).then_inc(x_set, 1)
                if k == 0:
                    act.wait_ge(par_set, 1)
                act.wait_ge(x_set, k + 1)
                finish(0, k, G_FFN1 + k)
                if k % 2:
                    round_weights(0, k // 2, 0)
            for t in range(NQ):
                act.wait_ge(x_landed[t], 16)
                a(x_sq[:, t * D:(t + 1) * D], x_in[:, t * D:(t + 1) * D], ACT.Square, accum_out=var[:, t:t + 1]).then_inc(x_squared, 1)
            act.wait_ge(tab_set, 1)
            act.wait_ge(pool_set, 3)
            a(sin_t[:, :], cos_t[:, :], ACT.Sin, scale=0.5)
            a(cos_half, cos_t[:, :], ACT.Sin, scale=0.5, bias=half_pi).then_inc(tab_sin, 1)
            act.wait_ge(par_set, 2)
            a(lam_s, lam_s, ACT.Exp).then_inc(tab_sin, 1)
            keep_rstd(0)
            act.wait_ge(par_set, 3)

            for l in range(2):
                L = l * (N_L1 // 4)
                ffn(L, 4 * l, 2 * l, G_MIX + 8 * l)

                b4, q, r0 = L + O_MIX // 4, 4 * l + 1, ROPES * l
                N0 = 4 * b4
                for c in range(28):
                    step(b4 + c // 4, c % 4)
                    if c == 1:
                        keep_rstd(q)
                    p = c - 1
                    if p == 7:
                        for i in range(12):
                            act.wait_ge(idx_mm, 12 * l + i + 1)
                            if i >= 2:
                                act.wait_ge(idx_add, 12 * l + i - 1)
                            n = P * (i // 4 + 2)
                            a(relu_t[i % 2][:, 0:n], bank[S_BANK[i % 2]][:, 0:n], ACT.Relu).then_inc(idx_relu, 1)
                    if c in (C_AG, C_AG + 1):
                        act.wait_ge(taken, N0 + c + RING + 1)
                        a(y_buf[c % 2], y_buf[c % 2], ACT.Tanh, scale=0.5).then_inc(a_tanh, 1)
                    for n in taps_at(c):
                        i, j = n % 2, n // 2
                        if n < 2:
                            act.wait_ge(a_glu, 4 * l + i + 1)
                        if n >= 6:
                            act.wait_ge(tap_added, ADDED * l + n - 5)
                        w, src = col(G_DW + 2 * (TAPS * l + j) + i), a_pad[i][:, j:j + S]
                        if j == 0:
                            ins = a(conv[i], src, ACT.Identity, scale=w, bias=col(G_DWB + 2 * l + i))
                        else:
                            ins = a(tap_t[n % 4], src, ACT.Copy, scale=w)
                        ins.then_inc(tap_made, 1)
                    if c in (C_BH + 3, C_BH + 5):
                        i = (c - C_BH - 3) // 2
                        act.wait_ge(y_made, 2 * l + i + 1)
                        a(tile(h_hi, 2 + i), yb_t, ACT.Copy).then_inc(y_rounded, 1)
                    if p >= C_V:
                        i = p - C_V
                        v_store(12 * l + i, p, v_t.rearrange("p (j n) -> p j n", j=NQ)[:, :, i * P:(i + 1) * P], banks=V_BANK)
                v_store(12 * l + 3, 27, v_t.rearrange("p (j n) -> p j n", j=NQ)[:, :, 3 * P:4 * P], banks=V_BANK)

                s0 = SCORES1 * l
                for i in range(32 + LAG + 3):
                    n = i - LAG
                    if 0 <= n < 32:
                        h, t = n // 4, n % 4
                        act.wait_ge(t_mm, s0 + n + 1)
                        if h >= 2 and t == 0:
                            act.wait_ge(pv_mm, PV1 * l + h - 1)
                        a(pt[h % 2].rearrange("p (j n) -> p j n", j=NQ)[:, 0:t + 1, t * P:(t + 1) * P],
                          bank[T_BANK[n % 2]][:, 0:(t + 1) * P].rearrange("p (j n) -> p j n", n=P), ACT.Copy)\
                            .then_inc(t_set, 1)
                    if i < 32:
                        t = i % 4
                        act.wait_ge(s_min, s0 + i + 1)
                        if i >= 4:
                            act.wait_ge(t_mm, s0 + i - 3)
                        a(prob[i % 4][:, 0:P * (t + 1)], sp[i % 4][:, 0:P * (t + 1)], ACT.Exp, bias=neg_max[i % 4],
                          scale=-1.0, accum_out=row_sum[i % 4]).then_inc(p_exp, 1)
                    if n >= 3 and (n - 3) % 8 == 7:
                        g = (n - 3) // 8
                        act.wait_ge(pv_mm, PV1 * l + 2 * g + 2)
                        a(tile(h_hi, 4 + g), bank[g % 2][:, :], ACT.Copy).then_inc(o_rounded, 1)
                    if i in (17, 18):
                        c = i - 17
                        act.wait_ge(ln_y, 2 * l + 2)
                        a(conv[c], conv[c], ACT.Identity, scale=col(G_LNG + 2 * l + c), bias=col(G_LNB + 2 * l + c))\
                            .then_inc(ln_z, 1)
                        act.wait_ge(ln_z, 2 * l + c + 1)
                        a(y_buf[c], conv[c], ACT.Tanh, scale=0.5).then_inc(ln_t, 1)
                    if i in (20, 21):
                        c = i - 20
                        act.wait_ge(a_glu, 4 * l + 2 + c + 1)
                        a(tile(h_hi, c), conv[c], ACT.Copy, scale=0.5).then_inc(y_rounded, 1)

                plain_finish(L + O_OUT // 4, 4 * l + 2, G_XA + 8 * l)

                b4, q = L + O_WQ // 4, 4 * l + 2
                for c in range(8):
                    step(b4 + c // 4, c % 4)
                    if c == 0:
                        act.wait_ge(mem_landed, 16 * (l + 1))
                        for t in range(2):
                            a(ptx[t], mem_in[:, t * D:(t + 1) * D], ACT.Square, accum_out=mem_var[:, t:t + 1])\
                                .then_inc(mem_sq, 1)
                    if c == 1:
                        keep_rstd(q)
                    if 3 <= c < 7:
                        r = c - 3
                        act.wait_ge(mem_tr, 4 * l + r + 1)
                        for k in range(2 * r, 2 * r + 2):
                            a(h_hi[:, k * MEM:(k + 1) * MEM], bank[S_BANK[r % 2]][:, (k % 2) * MEM:(k % 2 + 1) * MEM],
                              ACT.Copy, scale=col(G_MEM + 8 * l + k)).then_inc(gm_rounded, 1)
                with act.Fori(0, 2) as i:
                    for j in range(4):
                        step(L + O_KV // 4 + i, j)
                b4 = L + O_KV // 4 + 2
                for c in range(8):
                    step(b4 + c // 4, c % 4)
                    if c >= 1:
                        i = c - 1
                        v_store(12 * l + 4 + i, i, vm.rearrange("p (j n) -> p j n", j=2)[:, :, i * P:(i + 1) * P], 2)
                v_store(12 * l + 11, 7, vm.rearrange("p (j n) -> p j n", j=2)[:, :, 7 * P:8 * P], 2)

                s0 = SCORES1 * l + 32
                for i in range(16 + LAG + 3):
                    n = i - LAG
                    if 0 <= n < 16:
                        h, t = n // 4, n % 4
                        act.wait_ge(t_mm, s0 + n + 1)
                        if h >= 2 and t == 0:
                            act.wait_ge(pv_mm, PV1 * l + 8 + h - 1)
                        a(ptx[h % 2].rearrange("p (j n) -> p j n", j=2)[:, :, t * P:(t + 1) * P],
                          bank[T_BANK[n % 2]][:, 0:2 * P].rearrange("p (j n) -> p j n", n=P), ACT.Copy).then_inc(t_set, 1)
                    if i < 16:
                        act.wait_ge(s_min, s0 + i + 1)
                        if i >= 4:
                            act.wait_ge(t_mm, s0 + i - 3)
                        a(px[i % 4], bank[S_BANK[i % 3]][:, 0:MEM], ACT.Exp, bias=neg_max[i % 4], scale=-1.0,
                          accum_out=row_sum[i % 4]).then_inc(p_exp, 1)
                    if n >= 3 and (n - 3) % 4 == 3:
                        h = (n - 3) // 4
                        act.wait_ge(pv_mm, PV1 * l + 8 + h + 1)
                        for d in range(2):
                            a(tile(h_hi, 2 * h + d), bank[(2 * h + d + 1) % 3][:, :], ACT.Copy).then_inc(o_rounded, 1)
                plain_finish(L + O_WO // 4, 4 * l + 3, G_FFN2 + 8 * l)
                ffn(L + O_FFN2 // 4, 4 * l + 3, 2 * l + 1, G_JOINT if l else G_FFN1 + 8, joint=l == 1)

            for l in range(2):
                L = 2 * (N_L1 // 4) + l * (N_L2 // 4)
                q, v0, e0 = 8 + 2 * l, 24 + 8 * l, 8 * l

                def decay(h):
                    if h >= 2:
                        act.wait_ge(r_dec, 16 * l + 4 * (h - 2) + 4)
                    a(table[h % 2], const[:, C_DEC:C_DEC + S], ACT.Exp, scale=LOG_GAMMA[h]).then_inc(dec_set, 1)

                def head_square(h, first, done, to):
                    act.wait_ge(done, (4 * l if done is rpv_mm else 2 * PV1 + 4 * l) + h + 1)
                    if h >= 2:
                        act.wait_ge(z_mm, e0 + first + h - 1)
                    a(tile(z_t, h), bank[to][:, :], ACT.Copy)
                    a(zsq[h % 2], bank[to][:, :], ACT.Square).then_inc(z_sq, 1)

                def head_round(h, first):
                    act.wait_ge(z_norm, e0 + first + h + 1)
                    a(tile(h_hi, first + h), tile(z_t, h), ACT.Copy).then_inc(o_rounded, 1)

                for c in range(24):
                    h, half = divmod(c - R_G - 1, 2)
                    if 1 <= h <= 4 and half == 0:
                        head_square(h - 1, 0, rpv_mm, 6)
                    step(L + c // 4, c % 4)
                    if c == 1:
                        keep_rstd(q)
                    if l == 0 and c == 3:
                        act.wait_ge(j_bc, 1)
                        a(j_scale, bank[7][:, :], ACT.Copy).then_inc(j_set, 1)
                    if c == 2:
                        decay(0)
                        decay(1)
                    p = c - 1
                    if R_V <= p < R_G:
                        i = p - R_V
                        v_store(v0 + i, p, rv_t.rearrange("p (j n) -> p j n", j=NQ)[:, :, i * P:(i + 1) * P])
                    if R_G <= c < D_Q:
                        act.wait_ge(taken, 4 * L + c + RING + 1)
                        a(y_buf[c % 2], tile(gate_s, c - R_G), ACT.Tanh, scale=0.5).then_inc(g_tanh, 1)
                    if 1 <= h < 3 and half == 0:
                        decay(h + 1)
                    if NORM0 + 2 <= c < NORM0 + 6:
                        head_round(c - NORM0 - 2, 0)
                    if D_V <= p:
                        i = p - D_V
                        v_store(v0 + 4 + i, p, dv_t.rearrange("p (j n) -> p j n", j=NQ)[:, :, i * P:(i + 1) * P])
                v_store(v0 + 7, 23, dv_t.rearrange("p (j n) -> p j n", j=NQ)[:, :, 3 * P:4 * P])

                s0 = 2 * SCORES1 + 16 * l
                for i in range(16 + LAG + 3):
                    n = i - LAG
                    if 0 <= n < 16:
                        h, t = n // 4, n % 4
                        act.wait_ge(t_mm, s0 + n + 1)
                        if h >= 2 and t == 0:
                            act.wait_ge(pv_mm, 2 * PV1 + 4 * l + h - 1)
                        a(d_pt[h % 2].rearrange("p (j n) -> p j n", j=NQ)[:, 0:t + 1, t * P:(t + 1) * P],
                          bank[T_BANK[n % 2]][:, 0:(t + 1) * P].rearrange("p (j n) -> p j n", n=P), ACT.Copy)\
                            .then_inc(t_set, 1)
                    if i < 16:
                        t, b = i % 4, i % 4
                        act.wait_ge(s_min, s0 + i + 1)
                        if i >= 4:
                            act.wait_ge(t_mm, s0 + i - 3)
                        for j in range(2):
                            ins = a(dp[b][j][:, 0:P * (t + 1)], dsp[b][j][:, 0:P * (t + 1)], ACT.Exp, bias=neg_max[2 * b + j],
                                    scale=-1.0, accum_out=row_sum[2 * b + j])
                        ins.then_inc(p_exp, 1)
                    if n >= 6 and n % 4 == 2:
                        head_square(n // 4 - 1, 4, pv_mm, 2)
                    if n >= 10 and n % 4 == 2:
                        head_round(n // 4 - 2, 4)
                head_round(3, 4)
                plain_finish(L + O2_OUT // 4, 9 + 2 * l, G_FFNN2 + 8 * l)
                ffn(L + O2_FFN // 4, 9 + 2 * l, 4 + l, G_ATTN2 + 8 * (l + 1), more=l == 0)
            act.wait_ge(stat_inv, 13)
            act.wait_ge(x_set, 24)
            for t in range(2):
                yt = y_out[:, t * D:(t + 1) * D]
                a(yt, yt, ACT.Copy, scale=inv[:, t:t + 1]).then_inc(y_scaled[t], 1)

        @block.vector
        def _(v):
            tt, ts, stt = nc.vector.tensor_tensor, nc.vector.tensor_scalar, nc.vector.scalar_tensor_tensor
            chain = Chain(chain_v)

            def rest_of_weights(b4, j, ahead=RING):
                v.wait_ge(rounded, 4 * b4 + j + ahead + 1)
                tt(w_lo[:, j, :], raw[:, j, :], f32(w_hi[:, j, :]), ALU.subtract).then_inc(split, 1)

            def rest(dst_hi, dst_lo, src, scale, e):
                stt(dst_lo, src, scale, f32(dst_hi), ALU.mult, ALU.subtract).then_inc(e, 1)

            def scaled(dst, b4, c, factor=1.0, rows=P):
                v.wait_ge(tiles, 4 * b4 + c + 1)
                stt(dst[0:rows, :], bank[c % 4][0:rows, :], factor, rstd[0:rows, :], ALU.mult, ALU.mult).then_inc(taken, 1)

            def make_diag(values, to, e):
                for t in range(NQ):
                    ins = ts(to[:, t * P:(t + 1) * P], ident, values[:, t:t + 1], None, ALU.mult)
                ins.then_inc(e, 1)

            def norm_scale(q):
                v.wait_ge(stat_mm, q)
                ins = ts(var, bank[7][:, 0:NQ], 1.0 / D, EPS, ALU.mult, ALU.add)
                if q == 8:
                    chain.done(v, ins)
                    chain.done(v, nc.vector.reciprocal(j_var, var))
                    chain.done(v, stt(j_var, bank[7][:, NQ:2 * NQ], 1.0 / D, j_var, ALU.mult, ALU.mult))
                    ins = ts(j_var, j_var, EPS, None, ALU.add)
                ins.then_inc(stat_var, 1)
                v.wait_ge(stat_inv, q + 1)
                if q == 8:
                    chain.done(v, tt(j_inv, j_inv, inv, ALU.mult))
                make_diag(j_inv if q == 8 else inv, diag, stat_diag)
                if q == 8:
                    make_diag(inv, j_diag, j_diag_set)

            def finish(q, k, gain):
                v.wait_ge(u_rounded, k + 8 * q + 1)
                rest(tile(u_hi, k), tile(u_lo, k), tile(x, k), col(gain), u_ready)

            def residual(b4, j, k, factor):
                v.wait_ge(tiles, 4 * b4 + j + 1)
                stt(tile(x, k), bank[j][:, :], factor, tile(x, k), ALU.mult, ALU.add).then_inc(taken, 1)

            def result(k):
                v.wait_ge(x_tr, 8 + k + 1)
                nc.vector.tensor_copy(y_out.rearrange("p (t d) -> p t d", t=NQ)[:, :, k * P:(k + 1) * P],
                                      bank[4 + k % 2][:, :].rearrange("p (t n) -> p t n", n=P)).then_inc(x_set, 1)

            def ffn(b4, q, f, gain, factor, more=True):
                for g, (f0, fn) in enumerate(F_GROUPS):
                    def gate(b4, j, f_at):
                        if f_at is not None:
                            v.wait_ge(f_ready, F_TILES * f + (f_at - 1) + 1)
                        v.wait_ge(tiles, 4 * b4 + j + 1)
                        tt(gate_t, bank[j][:, :], rstd[:, :], ALU.mult).then_inc(taken, 1)

                    def up(b4, j, f_at, h_at):
                        v.wait_ge(tiles, 4 * b4 + j + 1)
                        tt(up_t, bank[j][:, :], rstd[:, :], ALU.mult).then_inc(taken, 1)
                        v.wait_ge(f_tanh, F_TILES * f + f_at + 1)
                        chain.done(v, stt(gate_t, tanh_t, 1.0, gate_t, ALU.add, ALU.mult))
                        tt(gate_t, gate_t, up_t, ALU.mult).then_inc(f_prod, 1)
                        rest_of_weights(b4, j)
                        v.wait_ge(f_rounded, F_TILES * f + f_at + 1)
                        rest(tile(h_hi, h_at), tile(h_lo, h_at), gate_t, 1.0, f_ready)

                    if g == 0:
                        rest_of_weights(b4, 0)
                        if q:
                            norm_scale(q)
                        v.wait_ge(rstd_set, q + 1)
                        gate(b4, 0, None)
                        up(b4, 1, 0, 0)
                        rest_of_weights(b4, 2)
                        gate(b4, 2, 1)
                        up(b4, 3, 1, 1)
                    with chain.loop(v, 1 if g == 0 else 0, fn // 2, 2) as i:
                        for jj in range(2):
                            rest_of_weights(b4 + i, 2 * jj)
                            gate(b4 + i, 2 * jj, i * 2 + (f0 + jj))
                            up(b4 + i, 2 * jj + 1, i * 2 + (f0 + jj), i * 2 + jj)
                    b4 = b4 + fn // 2
                    end = g == len(F_GROUPS) - 1
                    if end and not more:
                        for k in range(KT):
                            residual(b4 + k // 4, k % 4, k, factor)
                            if k < 4:
                                rest_of_weights(b4, k)
                            if k >= 3:
                                result(k - 3)
                        for k in range(5, KT):
                            result(k)
                        continue
                    with v.Fori(0, 2) as i:
                        for j in range(4):
                            residual(b4 + i, j, i * 4 + j, factor)
                            rest_of_weights(b4 + i, j)
                            if end:
                                finish(q + 1, i * 4 + j, i * 4 + (gain + j))
                    b4 = b4 + 2

            def plain_finish(b4, q, gain):
                with v.Fori(0, 2) as i:
                    for j in range(4):
                        residual(b4 + i, j, i * 4 + j, 1.0)
                        rest_of_weights(b4 + i, j)
                        finish(q, i * 4 + j, i * 4 + (gain + j))

            def normalise(i, p, s_at):
                v.wait_ge(p_exp, s_at + 1)
                chain.done(v, nc.vector.reciprocal(row_inv[i % 4], row_sum[i % 4]))
                ts(p, p, row_inv[i % 4], None, ALU.mult).then_inc(p_norm, 1)

            v.sem_inc(split, RING)
            v.sem_inc(taken, RING)
            v.wait_ge(par_tr, 1)
            nc.vector.tensor_copy(par[:, 0:2 * KT], bank[3][:, 0:2 * KT]).then_inc(par_set, 1)
            v.wait_ge(par_set, 1)
            for k in range(KT):
                finish(0, k, G_FFN1 + k)
                if k % 2:
                    rest_of_weights(0, k // 2, 0)
            v.wait_ge(x_squared, NQ)
            ts(var, var, 1.0 / D, EPS, ALU.mult, ALU.add).then_inc(stat_var, 1)
            v.wait_ge(stat_inv, 1)
            make_diag(inv, diag, stat_diag)
            v.wait_ge(setup_in, 16 * 6)
            chain.done(v, nc.vector.tensor_copy(ang, pos_i))
            chain.done(v, ts(ang, ang, const[:, C_INV:C_INV + 1], None, ALU.mult))
            chain.done(v, ts(turns, ang, 1.0 / (2 * math.pi), ROUND, ALU.mult, ALU.add))
            chain.done(v, ts(turns, turns, ROUND, None, ALU.subtract))
            chain.done(v, stt(ang, turns, -TWO_PI[0], ang, ALU.mult, ALU.add))
            chain.done(v, stt(ang, turns, -TWO_PI[1], ang, ALU.mult, ALU.add))
            stt(cos_t[:, :], turns, -TWO_PI[2], ang, ALU.mult, ALU.add).then_inc(tab_set, 1)
            v.wait_ge(tab_sin, 1)
            chain.done(v, stt(cos_t[:, :], sin_t[:, :], -2.0, sin_t[:, :], ALU.mult, ALU.mult))
            chain.done(v, ts(cos_t[:, :], cos_t[:, :], 1.0, None, ALU.add))
            stt(sin_t[:, :], sin_t[:, :], 2.0, cos_half, ALU.mult, ALU.mult).then_inc(tab_set, 1)
            for i in range(2):
                pr = lam_in[:, 2 * i * P:(2 * i + 1) * P]
                chain.done(v, tt(pr, pr, lam_in[:, (2 * i + 1) * P:(2 * i + 2) * P], ALU.mult))
                ins = nc.vector.tensor_reduce(lam_s[:, 2 * i:2 * i + 2], pr.rearrange("p (l d) -> p l d", l=2), AX_X, ALU.add)
                if i == 0:
                    chain.done(v, ins)
            ins.then_inc(par_set, 1)
            v.wait_ge(tab_sin, 2)
            chain.done(v, tt(neg_lam, lam_s[:, 2:4], lam_s[:, 0:2], ALU.subtract))
            for l in range(2):
                chain.done(v, ts(neg_lam[:, l:l + 1], neg_lam[:, l:l + 1], -LAM_INIT[l], None, ALU.add))
            v.wait_ge(par_tr, 2)
            chain.done(v, nc.vector.tensor_copy(par[:, 2 * KT:G_N], bank[6][:, 2 * KT:G_N]))
            ts(par[:, G_DW:G_DWB], par[:, G_DW:G_DWB], 0.5, None, ALU.mult)
            for l in range(2):
                ts(par[:, G_DIF + l:G_DIF + l + 1], par[:, G_DIF + l:G_DIF + l + 1], 1.0 - LAM_INIT[l], None, ALU.mult)
            tt(par[:, G_JOINT:G_JOINT + KT], par[:, G_FINAL:G_FINAL + KT], par[:, G_ATTN2:G_ATTN2 + KT], ALU.mult)\
                .then_inc(par_set, 1)
            v.wait_ge(par_set, 3)

            for l in range(2):
                L = l * (N_L1 // 4)
                ffn(L, 4 * l, 2 * l, G_MIX + 8 * l, 0.25)

                b4, q, r0 = L + O_MIX // 4, 4 * l + 1, ROPES * l
                N0 = 4 * b4

                def combine(r, p, dst, rows=P, between=None):
                    v.wait_ge(rot_mm, r0 + r + 1)
                    chain.done(v, tt(rope_t[0:rows, :], bank[R_BANK[r % 2]][0:rows, :], sin_t[0:rows, :], ALU.mult))
                    if between:
                        between()
                    v.wait_ge(cos_mul, r0 + r + 1)
                    tt(dst[0:rows, :], rope_t[0:rows, :], y_buf[p % 2][0:rows, :], ALU.add).then_inc(roped, 1)
                    v.wait_ge(roped, r0 + r + 1)

                def top_rounds(first, last):
                    for n in range(first, min(last, 3 * ROUNDS)):
                        w = work[1 + n // ROUNDS]
                        chain.done(v, nc.vector.max(max8, w))
                        chain.done(v, nc.vector.match_replace(w, max8, w, TAKEN))

                def take(c):
                    if c == 0:
                        scaled(y_buf[0], b4, c, rows=64)
                    elif c == 1:
                        scaled(w_idx_t, b4, c, 1.0 / 16, rows=4)
                    elif c < 6:
                        scaled(y_buf[c % 2], b4, c, rows=64)
                    elif c < C_AG:
                        if c == C_AV:
                            v.wait_ge(pads, l + 1)
                        scaled(a_pad[c % 2][:, PAD:], b4, c)
                    elif c < C_BG:
                        scaled(y_buf[c % 2], b4, c)
                    elif c < C_CG:
                        scaled(b_gate[c % 2], b4, c)
                    elif c < C_BH:
                        if c == C_CG:
                            for i in range(2):
                                chain.done(v, nc.vector.memset(c_pad[i][:, 0:SC_PAD], 0.0))
                        scaled(c_pad[c % 2][:, SC_PAD:], b4, c)
                    elif c < C_Q:
                        scaled(y_buf[c % 2], b4, c)
                        v.wait_ge(taken, N0 + c + RING + 1)
                        cp = c_pad[c % 2][:, SC_PAD:]
                        chain.done(v, tt(cp, cp, y_buf[c % 2], ALU.mult))
                    elif c < C_K:
                        scaled(y_buf[c % 2], b4, c, -0.125)
                    else:
                        if c >= C_V + 2:
                            v.wait_ge(v_tr, 12 * l + c - 2 - C_V + 1)
                        scaled(y_buf[c % 2], b4, c)

                def rounds():
                    top_rounds(rounds_before(p), rounds_before(p + 1))

                for c in range(28):
                    if c == 0:
                        rest_of_weights(b4, 0)
                        norm_scale(q)
                        continue
                    if c == 1:
                        v.wait_ge(rstd_set, q + 1)
                        take(0)
                    take(c)
                    rest_of_weights(b4 + c // 4, c % 4)
                    p = c - 1
                    if p == 0:
                        combine(0, 0, k_idx, 64)
                    if p == 1:
                        v.wait_ge(wi_tr, l + 1)
                        nc.vector.tensor_copy(w_idx, bank[7][:, 0:16]).then_inc(wi_set, 1)
                    if 2 <= p < 6:
                        combine(p - 1, p, q_idx[p - 2], 64)
                    if p == 7:
                        v.wait_ge(wi_set, l + 1)
                        for i in range(12):
                            t, h = 1 + i // 4, i % 4
                            v.wait_ge(idx_relu, 12 * l + i + 1)
                            if h:
                                v.wait_ge(idx_add, 12 * l + i)
                            n = P * (t + 1)
                            base = work[t] if h else const[:, C_NEG + S - n:C_NEG + S]
                            stt(work[t], relu_t[i % 2][:, 0:n], w_idx[:, 4 * t + h:4 * t + h + 1], base, ALU.mult, ALU.add)\
                                .then_inc(idx_add, 1)
                        v.wait_ge(idx_add, 12 * l + 12)
                    if p in (C_AG, C_AG + 1):
                        i = p - C_AG
                        v.wait_ge(a_tanh, 2 * l + i + 1)
                        ap = a_pad[i][:, PAD:]
                        stt(ap, y_buf[p % 2], 1.0, ap, ALU.add, ALU.mult).then_inc(a_glu, 1)
                        v.wait_ge(a_glu, 4 * l + i + 1)
                    if p in (C_BH + 1, C_BH + 3):
                        i = (p - C_BH - 1) // 2
                        if i:
                            v.wait_ge(y_ready, 4 * l + 1)
                        g = G_SC + 2 * SC_TAPS * l + i
                        chain.done(v, ts(yb_t, c_pad[i][:, 0:S], col(g), None, ALU.mult))
                        for j in (1, 2):
                            chain.done(v, stt(yb_t, c_pad[i][:, j:j + S], col(g + 2 * j), yb_t, ALU.mult, ALU.add))
                        tt(yb_t, yb_t, b_gate[i], ALU.mult).then_inc(y_made, 1)
                    if p in (C_BH + 2, C_BH + 4):
                        i = (p - C_BH - 2) // 2
                        v.wait_ge(y_rounded, 4 * l + i + 1)
                        rest(tile(h_hi, 2 + i), tile(h_lo, 2 + i), yb_t, 1.0, y_ready)
                    if C_Q <= p < C_K:
                        combine(5 + p - C_Q, p, tile(q_t, p - C_Q), between=rounds)
                    if C_K <= p < C_V:
                        combine(5 + p - C_Q, p, tile(k_t, p - C_K), between=rounds)
                    if p >= 8 and not C_Q <= p < C_V:
                        rounds()
                for t in range(1, NQ):
                    ins = ts(work[t], work[t], TAKEN / 2, BIG, ALU.is_gt, ALU.mult)
                ins.then_inc(masked, 1)
                v.wait_ge(masked, l + 1)

                s0 = SCORES1 * l
                for i in range(32 + LAG + 3):
                    if i < 32:
                        t = i % 4
                        n = P * (t + 1)
                        v.wait_ge(s_mm, s0 + i + 1)
                        mask = work[t] if t else const[:, C_BIG:C_BIG + P]
                        nc.vector.tensor_tensor_reduce(sp[i % 4][:, 0:n], bank[S_BANK[i % 3]][:, 0:n], mask, 1.0, BIG,
                                                       ALU.add, ALU.min, neg_max[i % 4]).then_inc(s_min, 1)
                    if 1 <= i < 33:
                        normalise(i - 1, prob[(i - 1) % 4][:, 0:P * ((i - 1) % 4 + 1)], s0 + i - 1)
                    n = i - LAG - 3
                    if n >= 0 and n % 8 == 7:
                        g = n // 8
                        v.wait_ge(o_rounded, PV1 * l + g + 1)
                        rest(tile(h_hi, 4 + g), tile(h_lo, 4 + g), bank[g % 2][:, :], 1.0, o_ready)
                    if i == 9:
                        v.wait_ge(ln_mean, l + 1)
                        for c in range(2):
                            stt(conv[c], bank[2][:, :], -1.0 / 256, conv[c], ALU.mult, ALU.add).then_inc(ln_cent, 1)
                    if i == 12:
                        v.wait_ge(ln_mm, l + 1)
                        ts(ln_var, bank[2][:, 0:NQ], 1.0 / 256, LN_EPS, ALU.mult, ALU.add).then_inc(ln_v, 1)
                    if i == 14:
                        v.wait_ge(ln_i, l + 1)
                        make_diag(ln_inv, rope_t, ln_d)
                    if i == 16:
                        v.wait_ge(ln_bc, l + 1)
                        for c in range(2):
                            tt(conv[c], bank[2][:, :], conv[c], ALU.mult).then_inc(ln_y, 1)
                    if i in (19, 20):
                        c = i - 19
                        v.wait_ge(ln_t, 2 * l + c + 1)
                        stt(conv[c], y_buf[c], 1.0, conv[c], ALU.add, ALU.mult).then_inc(a_glu, 1)
                    if i in (22, 23):
                        c = i - 22
                        v.wait_ge(y_rounded, 4 * l + 2 + c + 1)
                        rest(tile(h_hi, c), tile(h_lo, c), conv[c], 0.5, y_ready)

                plain_finish(L + O_OUT // 4, 4 * l + 2, G_XA + 8 * l)

                b4, q = L + O_WQ // 4, 4 * l + 2
                for c in range(8):
                    rest_of_weights(b4 + c // 4, c % 4)
                    if c == 0:
                        norm_scale(q)
                        continue
                    if c == 1:
                        v.wait_ge(rstd_set, q + 1)
                        scaled(tile(qx, 0), b4, 0, -1.0 / 16)
                    scaled(tile(qx, c), b4, c, -1.0 / 16)
                    if c == 1:
                        v.wait_ge(mem_i, l + 1)
                        for t in range(2):
                            mt = mem_in[:, t * D:(t + 1) * D]
                            ins = ts(mt, mt, mem_inv[:, t:t + 1], None, ALU.mult)
                        ins.then_inc(mem_n, 1)
                    if 3 <= c < 7:
                        r = c - 3
                        for k in range(2 * r, 2 * r + 2):
                            v.wait_ge(gm_rounded, 8 * l + 2 * r + 2)
                            ks = slice(k * MEM, (k + 1) * MEM)
                            rest(h_hi[:, ks], h_lo[:, ks], bank[S_BANK[r % 2]][:, (k % 2) * MEM:(k % 2 + 1) * MEM],
                                 col(G_MEM + 8 * l + k), gm_ready)
                with v.Fori(0, 2) as i:
                    for j in range(4):
                        rest_of_weights(L + O_KV // 4 + i, j)
                        v.wait_ge(tiles, 4 * (L + O_KV // 4 + i) + j + 1)
                        nc.vector.tensor_copy(km[:, bass.ds((i * 4 + j) * MEM, MEM)], bank[j][:, 0:MEM]).then_inc(taken, 1)
                b4 = L + O_KV // 4 + 2
                for c in range(8):
                    rest_of_weights(b4 + c // 4, c % 4)
                    v.wait_ge(tiles, 4 * b4 + c + 1)
                    if c >= 2:
                        v.wait_ge(v_tr, 12 * l + 4 + c - 1)
                    nc.vector.tensor_copy(vx_t[c % 2], bank[c % 4][:, 0:MEM]).then_inc(taken, 1)

                s0 = SCORES1 * l + 32
                for i in range(16 + LAG + 3):
                    if i < 16:
                        v.wait_ge(s_mm, s0 + i + 1)
                        nc.vector.tensor_reduce(neg_max[i % 4], bank[S_BANK[i % 3]][:, 0:MEM], AX_X, ALU.min).then_inc(s_min, 1)
                    if 1 <= i < 17:
                        normalise(i - 1, px[(i - 1) % 4], s0 + i - 1)
                    n = i - LAG - 3
                    if n >= 0 and n % 4 == 3:
                        h = n // 4
                        for d in range(2):
                            k = 2 * h + d
                            v.wait_ge(o_rounded, PV1 * l + 4 + k + 1)
                            rest(tile(h_hi, k), tile(h_lo, k), bank[(2 * h + d + 1) % 3][:, :], 1.0, o_ready)
                plain_finish(L + O_WO // 4, 4 * l + 3, G_FFN2 + 8 * l)
                ffn(L + O_FFN2 // 4, 4 * l + 3, 2 * l + 1, G_JOINT if l else G_FFN1 + 8, 0.25)

            for l in range(2):
                L = 2 * (N_L1 // 4) + l * (N_L2 // 4)
                q, v0, e0 = 8 + 2 * l, 24 + 8 * l, 8 * l

                def head_var(heads, h0, h1, to):
                    v.wait_ge(z_mm, e0 + heads)
                    ts(h_var[:, 4 * h0:4 * h1], bank[to][:, 4 * h0:4 * h1], 1.0 / P, EPS, ALU.mult, ALU.add).then_inc(h_v, 1)

                def head_diag(h, first):
                    v.wait_ge(h_i, 5 * l + (2 + h if first else 1))
                    make_diag(h_inv[:, 4 * h:4 * h + 4], head_d, h_d)

                def head_norm(h, first, gain, src):
                    v.wait_ge(h_bc, e0 + first + h + 1)
                    z = tile(z_t, h)
                    ins = stt(z, z, col(gain + l), src, ALU.mult, ALU.mult)
                    if first == 0:
                        chain.done(v, ins)
                        ins = stt(z, z, 0.5, tile(gate_s, h), ALU.mult, ALU.mult)
                    ins.then_inc(z_norm, 1)

                def head_rest(h, first):
                    v.wait_ge(o_rounded, 2 * PV1 + e0 + first + h + 1)
                    rest(tile(h_hi, first + h), tile(h_lo, first + h), tile(z_t, h), 1.0, o_ready)

                def take2(c):
                    if c < R_K:
                        scaled(tile(rq_t, c), L, c)
                    elif c < R_V:
                        scaled(tile(rk_t, c - R_K), L, c, 0.125)
                    elif c < R_G:
                        if c >= R_V + 2:
                            v.wait_ge(v_tr, v0 + c - 2 - R_V + 1)
                        scaled(y_buf[c % 2], L, c)
                    elif c < D_Q:
                        scaled(tile(gate_s, c - R_G), L, c)
                    elif c < D_K:
                        scaled(tile(dq_t, c - D_Q), L, c, -0.125)
                    elif c < D_V:
                        scaled(tile(dk_t, c - D_K), L, c)
                    else:
                        if c >= D_V + 2:
                            v.wait_ge(v_tr, v0 + 4 + c - 2 - D_V + 1)
                        scaled(y_buf[c % 2], L, c)

                for c in range(24):
                    if NORM0 + 2 <= c < NORM0 + 6:
                        head_norm(c - NORM0 - 2, 0, G_RET, bank[S_BANK[(c - NORM0 - 2) % 2]][:, :])
                    if NORM0 + 1 <= c < NORM0 + 5:
                        head_diag(c - NORM0 - 1, 0)
                    h, half = divmod(c - R_G - 1, 2)
                    if 0 <= h < 4:
                        if half == 0:
                            v.wait_ge(dec_set, 4 * l + h + 1)
                            if h:
                                v.wait_ge(rpv_mm, 4 * l + h)
                        for j in (2 * half, 2 * half + 1):
                            i = 4 * h + j
                            v.wait_ge(r_mm, 16 * l + i + 1)
                            tt(sd[:, j * S:(j + 1) * S - j * P], bank[S_BANK[i % 2]][:, 0:S - j * P],
                               table[h % 2][:, 0:S - j * P], ALU.mult).then_inc(r_dec, 1)
                    if R_G < c <= D_Q:
                        v.wait_ge(g_tanh, 4 * l + c - R_G)
                        gs = tile(gate_s, c - 1 - R_G)
                        chain.done(v, stt(gs, y_buf[(c - 1) % 2], 1.0, gs, ALU.add, ALU.mult))
                    rest_of_weights(L + c // 4, c % 4)
                    if c == 0:
                        norm_scale(q)
                        continue
                    if c == 1:
                        v.wait_ge(rstd_set, q + 1)
                        take2(0)
                    take2(c)
                    if l == 0 and 4 <= c < 12:
                        k = c - 4
                        if k == 0:
                            v.wait_ge(j_set, 1)
                        stt(tile(x, k), tile(x, k), col(G_FINAL + k), j_scale, ALU.mult, ALU.mult).then_inc(x_set, 1)
                    if c == NORM0:
                        head_var(4, 0, 4, 7)
                    if NORM0 + 3 <= c < NORM0 + 7:
                        head_rest(c - NORM0 - 3, 0)

                s0 = 2 * SCORES1 + 16 * l
                for i in range(16 + LAG + 2):
                    if i < 16:
                        h, t, b = i // 4, i % 4, i % 4
                        if t == 0 and i:
                            v.wait_ge(s_min, s0 + i)
                        if t == 0:
                            chain.done(v, stt(table[h % 2], const[:, C_DIST:C_DIST + S], SLOPE[h], const[:, C_NEG:C_NEG + S],
                                              ALU.mult, ALU.subtract))
                        n = P * (t + 1)
                        v.wait_ge(s_mm, s0 + i + 1)
                        for j in range(2):
                            ins = nc.vector.tensor_tensor_reduce(
                                dsp[b][j][:, 0:n], bank[D_BANK[i % 2][j]][:, 0:n], table[h % 2][:, S - n:S], 1.0, 2 * BIG,
                                ALU.add, ALU.min, neg_max[2 * b + j])
                        ins.then_inc(s_min, 1)
                    if 1 <= i < 17:
                        b, n = (i - 1) % 4, P * ((i - 1) % 4 + 1)
                        p0, p1 = dp[b][0][:, 0:n], dp[b][1][:, 0:n]
                        r0_, r1_ = row_inv[2 * b], row_inv[2 * b + 1]
                        v.wait_ge(p_exp, s0 + i)
                        chain.done(v, nc.vector.reciprocal(small[:, 16 + 2 * b:18 + 2 * b], small[:, 8 + 2 * b:10 + 2 * b]))
                        chain.done(v, ts(r1_, r1_, neg_lam[:, l:l + 1], None, ALU.mult))
                        chain.done(v, ts(p1, p1, r1_, None, ALU.mult))
                        stt(p0, p0, r0_, p1, ALU.mult, ALU.add).then_inc(p_norm, 1)
                    n = i - LAG
                    if n >= 7 and n % 4 == 3:
                        head_var(4 + n // 4, n // 4 - 1, n // 4, 3)
                        head_diag(n // 4 - 1, 4)
                    if n >= 9 and n % 4 == 1:
                        head_norm(n // 4 - 2, 4, G_DIF, bank[3][:, :])
                    if n >= 11 and n % 4 == 3:
                        head_rest(n // 4 - 2, 4)
                head_var(8, 3, 4, 3)
                head_diag(3, 4)
                head_rest(2, 4)
                head_norm(3, 4, G_DIF, bank[3][:, :])
                head_rest(3, 4)
                plain_finish(L + O2_OUT // 4, 9 + 2 * l, G_FFNN2 + 8 * l)
                ffn(L + O2_FFN // 4, 9 + 2 * l, 4 + l, G_ATTN2 + 8 * (l + 1), 0.5, more=l == 0)

            v.wait_ge(stat_mm, 12)
            ts(var, bank[7][:, 0:NQ], 1.0 / D, EPS, ALU.mult, ALU.add).then_inc(stat_var, 1)
            v.wait_ge(stat_inv, 13)
            v.wait_ge(x_set, 24)
            for t in range(2, NQ):
                yt = y_out[:, t * D:(t + 1) * D]
                ts(yt, yt, inv[:, t:t + 1], None, ALU.mult).then_inc(y_scaled[t], 1)

        @block.gpsimd
        def _(pool):
            tt, ts = nc.gpsimd.tensor_tensor, nc.gpsimd.tensor_scalar
            chain = Chain(chain_p)

            def add_square(k):
                chain.done(pool, tt(square, tile(x, k), tile(x, k), ALU.mult))
                tt(sumsq, sumsq, square, ALU.add).then_inc(sq_sum, 1)

            def clear_sum():
                chain.done(pool, nc.gpsimd.memset(sumsq, 0.0))

            def squares(b4, q):
                pool.wait_ge(taken, 4 * b4 + RING + 1)
                clear_sum()
                if q == 8:
                    chain.done(pool, nc.gpsimd.memset(j_sum, 0.0))
                with chain.loop(pool, 0, 2, 8 if q == 8 else 4) as i:
                    for j in range(4):
                        if q == 8:
                            pool.wait_ge(j_squared, i * 4 + (j + 1))
                            chain.done(pool, tt(j_sum, j_sum, tile(j_sq, i * 4 + j), ALU.add))
                        pool.wait_ge(taken, 4 * (b4 + i) + j + RING + 1)
                        if j:
                            pool.wait_ge(sq_sum, 8 * (q - 1) + 4 * i + (j - 1) + 1)
                        add_square(i * 4 + j)
                    pool.wait_ge(sq_sum, 8 * (q - 1) + 4 * i + 4)

            def norm_inv(q):
                pool.wait_ge(stat_var, q + 1)
                if q == 8:
                    chain.done(pool, tt(j_inv, j_var, minus_half[:, 0:NQ], ALU.pow))
                tt(inv, var, minus_half[:, 0:NQ], ALU.pow).then_inc(stat_inv, 1)

            nc.gpsimd.memset(par_in[:, 2 * P:3 * P], 0.0).then_inc(pool_set, 1)
            nc.gpsimd.memset(minus_half, -0.5).then_inc(pool_set, 1)
            nc.gpsimd.memset(half_pi, math.pi / 2).then_inc(pool_set, 1)
            pool.wait_ge(pool_set, 3)
            norm_inv(0)

            for l in range(2):
                L = l * (N_L1 // 4)
                last_down = L + (N_FFN - 8) // 4
                squares(last_down, 4 * l + 1)

                b4, r0 = L + O_MIX // 4, ROPES * l
                norm_inv(4 * l + 1)
                for i in range(2):
                    ins = nc.gpsimd.memset(a_pad[i][:, 0:PAD], 0.0)
                ins.then_inc(pads, 1)

                def times_cos(r, p, rows=P):
                    pool.wait_ge(rot_mm, r0 + r + 1)
                    y = y_buf[p % 2][0:rows, :]
                    tt(y, y, cos_t[0:rows, :], ALU.mult).then_inc(cos_mul, 1)

                times_cos(0, 0, 64)
                for p in range(2, 6):
                    times_cos(p - 1, p, 64)
                for c in range(6, 28):
                    p = c - 1
                    if C_Q <= p < C_V:
                        times_cos(5 + p - C_Q, p)
                    for n in taps_at(c):
                        if n < 2:
                            continue
                        pool.wait_ge(tap_made, MADE * l + n + 1)
                        if n >= 4:
                            pool.wait_ge(tap_added, ADDED * l + n - 3)
                        tt(conv[n % 2], conv[n % 2], tap_t[n % 4], ALU.add).then_inc(tap_added, 1)
                for c in range(2):
                    pool.wait_ge(ln_cent, 2 * l + c + 1)
                    tt(y_buf[c], conv[c], conv[c], ALU.mult).then_inc(ln_sq, 1)
                pool.wait_ge(ln_v, l + 1)
                tt(ln_inv, ln_var, minus_half[:, 0:NQ], ALU.pow).then_inc(ln_i, 1)

                squares(L + O_OUT // 4, 4 * l + 2)
                norm_inv(4 * l + 2)
                pool.wait_ge(mem_sq, 2 * l + 2)
                chain.done(pool, ts(mem_var, mem_var, 1.0 / D, EPS, ALU.mult, ALU.add))
                tt(mem_inv, mem_var, minus_half[:, 0:2], ALU.pow).then_inc(mem_i, 1)
                squares(L + O_WO // 4, 4 * l + 3)
                norm_inv(4 * l + 3)
                squares(L + (O_FFN2 + N_FFN - 8) // 4, 4 * l + 4)
                norm_inv(4 * l + 4)

            for l in range(2):
                L = 2 * (N_L1 // 4) + l * (N_L2 // 4)
                if l:
                    norm_inv(8 + 2 * l)
                pool.wait_ge(h_v, 5 * l + 1)
                tt(h_inv, h_var, minus_half, ALU.pow).then_inc(h_i, 1)
                for h in range(4):
                    pool.wait_ge(h_v, 5 * l + 2 + h)
                    c = slice(4 * h, 4 * h + 4)
                    tt(h_inv[:, c], h_var[:, c], minus_half[:, c], ALU.pow).then_inc(h_i, 1)
                squares(L + O2_OUT // 4, 9 + 2 * l)
                norm_inv(9 + 2 * l)
                squares(L + (O2_FFN + N_FFN - 8) // 4, 10 + 2 * l)
            norm_inv(12)


INPUTS = [
    "x", "mem", "positions", "ffn1_norm", "ffn1_w_gate", "ffn1_w_up", "ffn1_w_down", "mix_norm", "w_in", "conf_dw",
    "conf_dw_b", "conf_ln_g", "conf_ln_b", "sc_dw", "w_out", "xa_norm", "mem_norm", "xa_wq", "xa_wkv", "xa_wo",
    "ffn2_norm", "ffn2_w_gate", "ffn2_w_up", "ffn2_w_down", "final_norm", "attn_norm_2", "w_in_2", "ret_norm_2",
    "lambda_q1_2", "lambda_k1_2", "lambda_q2_2", "lambda_k2_2", "diff_norm_2", "w_out_2", "ffn_norm_2",
    "w_gate_2", "w_up_2", "w_down_2", "final_norm_2",
]


def kernel(**inputs):
    import concourse.bacc as bacc
    from concourse.bass_utils import run_bass_kernel_spmd as run

    nc = bacc.Bacc("TRN2", target_bir_lowering=False, num_devices=1)
    arrays = {f"in_{name}": np.ascontiguousarray(inputs[name]) for name in INPUTS}
    arrays["in_consts"] = constants()
    aps = {name[3:]: nc.dram_tensor(name, a.shape, mybir.dt.from_np(a.dtype), kind="ExternalInput").ap()
           for name, a in arrays.items()}
    out = nc.dram_tensor("out", (1, S, D), F32, kind="ExternalOutput").ap()
    two_blocks(nc, aps, out)
    r = run(nc, [arrays], core_ids=[0])
    return r.results[0]["out"]
```
